# Optimizing a Trainium2 kernel written in Bass

```python
import jax, jax.numpy as jnp
from jax import lax
import numpy as np

D_MODEL = 1024
BATCH = 1
SEQ = 512
DEPTH = 2

HGRN_HEADS = 4
HGRN_DIM = 128
HGRN_WIDTH = HGRN_HEADS * HGRN_DIM
CHUNK = 64
ATTN_HEADS = 8
KV_HEADS = 2
HEAD_DIM = 64
ATTN_WIDTH = ATTN_HEADS * HEAD_DIM
KV_WIDTH = KV_HEADS * HEAD_DIM
GROUP = ATTN_HEADS // KV_HEADS
WINDOW = 128
BLOCK = 128
ROPE_THETA = 500000.0
ROPE_DIM = HEAD_DIM // 4
MIX_WIDTH = HGRN_WIDTH + ATTN_WIDTH
IN_SIZES = (HGRN_WIDTH, HGRN_WIDTH, HGRN_WIDTH, HGRN_WIDTH,
            ATTN_WIDTH, KV_WIDTH, KV_WIDTH)
IN_WIDTH = sum(IN_SIZES)
IN_SPLITS = tuple(int(s) for s in np.cumsum(IN_SIZES)[:-1])
D_FF = 2816
N_MOD = 9
EPS = 1e-6

kernel_name = "hymba_hgrn2_swa_sink_macaron_adaln"

def rmsnorm(x, w):
    xf = x.astype(jnp.float32)
    y = xf * lax.rsqrt(jnp.mean(xf * xf, axis=-1, keepdims=True) + EPS)
    return (y * w.astype(jnp.float32)).astype(x.dtype)

def swiglu(h, w_gate, w_up, w_down):
    return (jax.nn.silu(h @ w_gate) * (h @ w_up)) @ w_down

def partial_rope(t, pos):
    inv_freq = ROPE_THETA ** (-jnp.arange(0, ROPE_DIM, 2, dtype=jnp.float32) / ROPE_DIM)
    ang = pos.astype(jnp.float32)[..., None] * inv_freq
    cos = jnp.cos(ang)[:, :, None, :].astype(t.dtype)
    sin = jnp.sin(ang)[:, :, None, :].astype(t.dtype)
    t1 = t[..., : ROPE_DIM // 2]
    t2 = t[..., ROPE_DIM // 2: ROPE_DIM]
    return jnp.concatenate([t1 * cos - t2 * sin, t2 * cos + t1 * sin, t[..., ROPE_DIM:]], axis=-1)

def hgrn2_mixer(q, f_logit, i, g, lb, norm_w):
    B, T, _ = q.shape
    n = T // CHUNK
    dt = q.dtype
    lb = lb.astype(jnp.float32)
    fl = f_logit.astype(jnp.float32)
    log_f = jnp.logaddexp(jnp.log(lb), jnp.log1p(-lb) + jax.nn.log_sigmoid(fl))
    k = (1.0 - lb) * jax.nn.sigmoid(-fl)

    def to_chunks(t):
        return t.astype(jnp.float32).reshape(B, n, CHUNK, HGRN_HEADS, HGRN_DIM).transpose(1, 0, 3, 2, 4)

    qc = to_chunks(q) * (HGRN_DIM ** -0.5)
    kc, vc, gc = to_chunks(k), to_chunks(i), to_chunks(log_f)
    tril = jnp.tril(jnp.ones((CHUNK, CHUNK), dtype=bool))[:, :, None]

    def step(S, inp):
        qx, kx, vx, gx = inp
        b = jnp.cumsum(gx, axis=-2)
        o_inter = jnp.einsum('bhtd,bhde->bhte', qx * jnp.exp(b), S)
        diff = b[:, :, :, None, :] - b[:, :, None, :, :]
        decay = jnp.exp(jnp.where(tril, diff, -jnp.inf))
        att = jnp.einsum('bhtd,bhtsd,bhsd->bhts', qx, decay, kx)
        o_intra = jnp.einsum('bhts,bhse->bhte', att, vx)
        b_last = b[:, :, -1:, :]
        S_new = jnp.exp(b_last[:, :, 0, :])[..., None] * S + jnp.einsum(
            'bhsd,bhse->bhde', kx * jnp.exp(b_last - b), vx)
        return S_new, o_inter + o_intra

    S0 = jnp.zeros((B, HGRN_HEADS, HGRN_DIM, HGRN_DIM), jnp.float32)
    _, o = lax.scan(step, S0, (qc, kc, vc, gc))
    o = o.transpose(1, 0, 3, 2, 4).reshape(B, T, HGRN_HEADS, HGRN_DIM)
    o = rmsnorm(o, norm_w) * jax.nn.silu(g.astype(jnp.float32).reshape(B, T, HGRN_HEADS, HGRN_DIM))
    return o.reshape(B, T, HGRN_WIDTH).astype(dt)

def swa_sink_mixer(q, k, v, pos, q_norm_w, k_norm_w, sinks):
    B, T, _ = q.shape
    nb = T // BLOCK
    dt = q.dtype
    q = partial_rope(rmsnorm(q.reshape(B, T, ATTN_HEADS, HEAD_DIM), q_norm_w), pos)
    k = partial_rope(rmsnorm(k.reshape(B, T, KV_HEADS, HEAD_DIM), k_norm_w), pos)
    v = v.reshape(B, T, KV_HEADS, HEAD_DIM)
    qb = q.reshape(B, nb, BLOCK, KV_HEADS, GROUP, HEAD_DIM)

    def band(t):
        tb = t.reshape(B, nb, BLOCK, KV_HEADS, HEAD_DIM)
        prev = jnp.concatenate([jnp.zeros_like(tb[:, :1]), tb[:, :-1]], axis=1)
        return jnp.concatenate([prev, tb], axis=2)

    kb, vb = band(k), band(v)
    s = jnp.einsum('bnqkgd,bnskd->bkgnqs', qb, kb).astype(jnp.float32) * (HEAD_DIM ** -0.5)
    qi = jnp.arange(BLOCK)[:, None]
    kj = jnp.arange(2 * BLOCK)[None, :] - BLOCK
    delta = qi - kj
    blk = jnp.arange(nb)[:, None, None]
    valid = ((delta >= 0) & (delta < WINDOW))[None] & (blk * BLOCK + kj[None] >= 0)
    s = jnp.where(valid, s, -jnp.inf)
    sink = sinks.astype(jnp.float32).reshape(KV_HEADS, GROUP)[None, :, :, None, None, None]
    m = jnp.maximum(jnp.max(s, axis=-1, keepdims=True), sink)
    p = jnp.exp(s - m)
    p = p / (jnp.sum(p, axis=-1, keepdims=True) + jnp.exp(sink - m))
    o = jnp.einsum('bkgnqs,bnskd->bnqkgd', p, vb.astype(jnp.float32))
    return o.reshape(B, T, ATTN_WIDTH).astype(dt)

def setup_inputs(seed: int = 0) -> dict:
    key = jax.random.key(seed)
    ks = jax.random.split(key, 24)
    nrm = lambda k, shape, s: jax.random.normal(k, shape, jnp.float32) * s
    gain = lambda k, shape: 1.0 + nrm(k, shape, 0.05)
    x = nrm(ks[0], (BATCH, SEQ, D_MODEL), 1.0)
    c = nrm(ks[1], (BATCH, D_MODEL), 1.0)
    positions = (jnp.arange(SEQ, dtype=jnp.int32)[None, :]
                 + jax.random.randint(ks[2], (BATCH, 1), 0, 1024, dtype=jnp.int32))
    return {
        "x": x,
        "c": c,
        "positions": positions,
        "ada_w": nrm(ks[3], (DEPTH, D_MODEL, N_MOD * D_MODEL), 0.5 * D_MODEL ** -0.5),
        "ada_b": nrm(ks[4], (DEPTH, N_MOD * D_MODEL), 0.02),
        "norm_ffn1": gain(ks[5], (DEPTH, D_MODEL)),
        "ffn1_w_gate": nrm(ks[6], (DEPTH, D_MODEL, D_FF), D_MODEL ** -0.5),
        "ffn1_w_up": nrm(ks[7], (DEPTH, D_MODEL, D_FF), D_MODEL ** -0.5),
        "ffn1_w_down": nrm(ks[8], (DEPTH, D_FF, D_MODEL), D_FF ** -0.5),
        "norm_mix": gain(ks[9], (DEPTH, D_MODEL)),
        "w_in": nrm(ks[10], (DEPTH, D_MODEL, IN_WIDTH), D_MODEL ** -0.5),
        "lb_logits": nrm(ks[11], (DEPTH, HGRN_WIDTH), 1.0),
        "hgrn_norm": gain(ks[12], (DEPTH, HGRN_DIM)),
        "q_norm": gain(ks[13], (DEPTH, HEAD_DIM)),
        "k_norm": gain(ks[14], (DEPTH, HEAD_DIM)),
        "sinks": nrm(ks[15], (DEPTH, ATTN_HEADS), 1.0),
        "w_out": nrm(ks[16], (DEPTH, MIX_WIDTH, D_MODEL), MIX_WIDTH ** -0.5),
        "norm_ffn2": gain(ks[17], (DEPTH, D_MODEL)),
        "ffn2_w_gate": nrm(ks[18], (DEPTH, D_MODEL, D_FF), D_MODEL ** -0.5),
        "ffn2_w_up": nrm(ks[19], (DEPTH, D_MODEL, D_FF), D_MODEL ** -0.5),
        "ffn2_w_down": nrm(ks[20], (DEPTH, D_FF, D_MODEL), D_FF ** -0.5),
    }

def reference(x, c, positions, ada_w, ada_b, norm_ffn1, ffn1_w_gate, ffn1_w_up, ffn1_w_down,
              norm_mix, w_in, lb_logits, hgrn_norm, q_norm, k_norm, sinks, w_out,
              norm_ffn2, ffn2_w_gate, ffn2_w_up, ffn2_w_down):
    B = x.shape[0]
    lb_cum = jnp.cumsum(jax.nn.softmax(lb_logits.astype(jnp.float32), axis=0), axis=0)
    lower_bounds = lb_cum - lb_cum[0:1]
    c_act = jax.nn.silu(c)
    for l in range(DEPTH):
        mod = (c_act @ ada_w[l] + ada_b[l]).reshape(B, N_MOD, 1, D_MODEL)
        sh1, sc1, g1, shm, scm, gm, sh2, sc2, g2 = [mod[:, j] for j in range(N_MOD)]
        h = rmsnorm(x, norm_ffn1[l]) * (1.0 + sc1) + sh1
        x = x + 0.5 * g1 * swiglu(h, ffn1_w_gate[l], ffn1_w_up[l], ffn1_w_down[l])
        h = rmsnorm(x, norm_mix[l]) * (1.0 + scm) + shm
        proj = h @ w_in[l]
        hq, hf, hi, hg, aq, ak, av = jnp.split(proj, IN_SPLITS, axis=-1)
        o_hgrn = hgrn2_mixer(hq, hf, hi, hg, lower_bounds[l], hgrn_norm[l])
        o_attn = swa_sink_mixer(aq, ak, av, positions, q_norm[l], k_norm[l], sinks[l])
        x = x + gm * (jnp.concatenate([o_hgrn, o_attn], axis=-1) @ w_out[l])
        h = rmsnorm(x, norm_ffn2[l]) * (1.0 + sc2) + sh2
        x = x + 0.5 * g2 * swiglu(h, ffn2_w_gate[l], ffn2_w_up[l], ffn2_w_down[l])
    return x


_drawn_inputs = setup_inputs


def setup_inputs(seed=0):
    import zlib

    import numpy as np

    out = dict(_drawn_inputs(seed))
    spreads = {}
    factors = {'norm_ffn1': 4.685,
     'hgrn_norm': 5.781,
     'q_norm': 8.0,
     'k_norm': 8.0,
     'sinks': 200.0,
     'norm_ffn2': 5.28}
    for name, (base, spread) in spreads.items():
        noise = np.random.default_rng([zlib.crc32(name.encode()), seed]).standard_normal(out[name].shape)
        drawn = base * np.exp(spread * noise) if base else spread * noise
        out[name] = __import__('jax').numpy.asarray(drawn.astype(out[name].dtype))
    for name, factor in factors.items():
        out[name] = (out[name] * factor).astype(out[name].dtype)
    return out
```

```python
from contextlib import ExitStack

import numpy as np

import concourse.bass as bass
from concourse import mybir

ALU = mybir.AluOpType
ACT = mybir.ActivationFunctionType
F32 = mybir.dt.float32
F32R = mybir.dt.float32r
I32 = mybir.dt.int32
AX_X = mybir.AxisListType.X

P = 128
DEPTH = 2
D = 1024
T = 512
KD = D // P
NT = T // P
F = 2816
FT = F // P
HH, HD = 4, 128
AH, KVH, AD = 8, 2, 64
QK = AH + KVH
ROPE_HALF = AD // 8
ROPE_THETA = 500000.0
N_MOD = 9
EPS = 1e-6
IN_TILES = 22
LEVELS = 7
NEG = -1e30
TWO_PI = float(2 * np.pi)
TWO_PI_PARTS = (6.28125, 4058 / 2.0 ** 21, 3.0199159795074593e-07)
PI_BELOW = 3.1415925
MAGIC = 1.5 * 2.0 ** 23

GU = 2 * FT
DN = 2 * KD
HALF = FT // 2
P_GU1, P_DN1 = 0, GU
P_IN = P_DN1 + DN
P_OUT = P_IN + IN_TILES
P_GU2 = P_OUT + KD
P_DN2 = P_GU2 + GU
PANELS = P_DN2 + DN
WIDE = HALF * P

C_ADAB, C_NORM = 0, N_MOD * KD
C_LB = C_NORM + 3 * KD
C_HNORM = C_LB + HH
C_C = C_HNORM + 1
N_COLS = C_C + KD

ADA_RING = 4
ADA_EARLY = 2
ADA_ITERATIONS = (10, 4, 4)
ADA_FIRST = (0, 10, 14)
ADA_UNITS = 18
assert ADA_UNITS == 2 * N_MOD and ADA_UNITS - ADA_FIRST[2] == 2 * ADA_EARLY
ADA_SHARE = ((0, 3), (3, 6), (6, 8), (8, 8))

IN_ORDER = [4, 5, 6, 7, 0, 1, 2, 3, 8, 9, 10, 11, 12, 13, 14, 15, 16, 17, 18, 19, 20, 21]
K_F, K_Q, K_V, K_G, K_AQ, K_AK, K_AV = "f", "q", "v", "g", "aq", "ak", "av"
KINDS = [K_Q] * 4 + [K_F] * 4 + [K_V] * 4 + [K_G] * 4 + [K_AQ] * 4 + [K_AK, K_AV]
TURNED = (K_V, K_AQ, K_AK, K_AV)
TURN_OF = {}
for _i, _c in enumerate(IN_ORDER):
    if KINDS[_c] in TURNED:
        TURN_OF[_i] = len(TURN_OF)
TURNS = len(TURN_OF)

MIX_STEPS = []
for _i in range(8):
    MIX_STEPS.append(("tile", _i))
MIX_STEPS += [("tile", 8), ("diag", 0)]
for _v in range(LEVELS):
    MIX_STEPS += [("tile", 9 + _v)]
    if 8 + _v in TURN_OF:
        MIX_STEPS += [("turn", 8 + _v)]
    MIX_STEPS += [("level", _v)]
MIX_STEPS += [("tile", 16), ("keys", 0), ("tile", 17), ("turn", 16), ("states", 0), ("tile", 18), ("turn", 17),
              ("hout", 0), ("tile", 19), ("turn", 18), ("hout", 1), ("hms", 0), ("tile", 20), ("turn", 19), ("hout", 2),
              ("hms", 1), ("tile", 21), ("turn", 20), ("hout", 3), ("hms", 2), ("turn", 21), ("hms", 3), ("hroot", 0)]
MIX_STEPS += [("hnorm", _h) for _h in range(HH)] + [("aprep", 0)]
for _n in range(NT):
    MIX_STEPS += [("score", _n), ("prob", _n)]

K_IDENT, K_AMASK, K_INVF, K_ONE, K_PER_D, K_PER_H, K_EPS = 0, 128, 384, 392, 393, 394, 395
K_COLS = 396


def constants():
    c = np.zeros((P, K_COLS), np.float32)
    c[:, K_IDENT:K_IDENT + P] = np.eye(P)
    q, k = np.arange(P)[:, None], np.arange(2 * P)[None, :] - P
    c[:, K_AMASK:K_AMASK + 2 * P] = np.where((q - k >= 0) & (q - k < P), 0.0, NEG)
    rope = np.arange(0, 2 * ROPE_HALF, 2, dtype=np.float32) / np.float32(2 * ROPE_HALF)
    c[:, K_INVF:K_INVF + ROPE_HALF] = np.float32(ROPE_THETA) ** (-rope)
    c[:, K_ONE], c[:, K_PER_D], c[:, K_PER_H], c[:, K_EPS] = 1.0, 1.0 / D, 1.0 / HD, EPS
    s, t = np.arange(P)[:, None], np.arange(P)[None, :]
    masks = [(((s ^ t) >> v) == 1) & (t > s) for v in range(LEVELS)]
    return c, np.concatenate(masks, axis=1).astype(np.int32)


def trunk_kernel(nc, a, out):
    ctx = ExitStack()
    with ctx:
        place = [16512]

        def sb(name, shape, dt=F32, at=None):
            n = int(np.prod(shape[1:])) * 4
            off = place[0] if at is None else at
            if at is None:
                place[0] += (n + 31) // 32 * 32
            return nc.alloc_sbuf_tensor_at(name, shape, dt, offset=off)

        UNIT = T * 4
        x = sb("x", [P, KD, T])
        h_hi = sb("h_hi", [P, KD, T], F32R)
        h_lo = sb("h_lo", [P, KD, T], F32R)
        raw = sb("raw", [P, 2, WIDE])
        w_hi = sb("w_hi", [P, 2, WIDE], F32R)
        w_lo = sb("w_lo", [P, 2, WIDE], F32R)
        ada_at = place[0]
        ada_raw = sb("ada_raw", [P, ADA_RING, T])
        ada_acc = sb("ada_acc", [P, T])
        ada_rest = sb("ada_rest", [P, T])
        region = place[0]
        place[0] += 2 * FT * UNIT
        hid_hi = sb("hid_hi", [P, FT, T], F32R, at=region)
        hid_lo = sb("hid_lo", [P, FT, T], F32R, at=region + FT * UNIT)
        tmp_at = place[0]
        sil = sb("sil", [P, 2, T])
        hidf = sb("hidf", [P, 2, T])
        sq = sb("sq", [P, 2, T])
        root = sb("root", [P, NT])
        inv = sb("inv", [P, NT])
        o_root = sb("o_root", [P, HH * NT])
        o_inv = sb("o_inv", [P, HH * NT])
        ssum = sb("ssum", [P, T])
        const = sb("const", [P, K_COLS])
        lmask = sb("lmask", [P, LEVELS, P], I32)
        qkw = sb("qkw", [P, QK, AD])
        cols = sb("cols", [P, DEPTH, N_COLS])
        lower = sb("lower", [P, DEPTH, HH])
        one_minus_lower = sb("one_minus_lower", [P, DEPTH, HH])
        mod = sb("mod", [P, N_MOD * KD])
        scale_col = sb("scale_col", [P, KD])
        gate_col = sb("gate_col", [P, KD])
        cact = sb("cact", [P, KD])
        sin_t = sb("sin_t", [P, NT, ROPE_HALF])
        cos_t = sb("cos_t", [P, NT, ROPE_HALF])
        sinks = sb("sinks", [P, DEPTH, AH])
        a_ss = sb("a_ss", [P, NT, QK])
        a_max = sb("a_max", [P, 2, AH])
        a_negmax = sb("a_negmax", [P, 2, AH])
        a_sink = sb("a_sink", [P, 2, AH])
        a_den = sb("a_den", [P, 2, AH])
        assert place[0] <= 229344, place[0]

        def unit(name, shape, first):
            return sb(name, shape, F32, at=region + first * UNIT)

        x_rows = unit("x_rows", [P, NT, D], 0)
        col_rows = unit("col_rows", [P, DEPTH, P], 8)
        rope_tmp = unit("rope_tmp", [P, 4, NT, ROPE_HALF], 9)
        pos_i = sb("pos_i", [P, NT], I32, at=region + 10 * UNIT)
        pos_f = unit("pos_f", [P, NT], 11)
        lb_tmp = sb("lb_tmp", [P, 4 + DEPTH, HH], F32, at=region + 11 * UNIT + 64)
        ada_first = unit("ada_first", [P, KD, 2 * D], 12)
        ada_sum = sb("ada_sum", [P, 2 * D], F32, at=ada_at)
        q_t = unit("q_t", [P, HH, T], 0)
        f_t = unit("f_t", [P, HH, T], 4)
        k_t = unit("k_t", [P, HH, T], 8)
        v_n = unit("v_n", [P, HH, NT, P], 12)
        g_t = unit("g_t", [P, HH, T], 16)
        aqk = unit("aqk", [P, NT, QK, AD], 20)
        a_v = unit("a_v", [P, NT, KVH, AD], 25)
        suf = unit("suf", [P, HH, T], 26)
        kq = unit("kq", [P, 2, HH, T], 30)
        att = unit("att", [P, HH, T], 38)
        evac = unit("evac", [P, 2, T], 42)
        state = unit("state", [P, HH, NT, P], 0)
        key_n = unit("key_n", [P, HH, NT, P], 26)
        o_n = unit("o_n", [P, HH, T], 4)
        o_mix = unit("o_mix", [P, 2, T], 8)
        pt = unit("pt", [P, 2, 4, P], 10)
        aq_t = sb("aq_t", [P, 4, T], F32, at=ada_at)
        ak_t = sb("ak_t", [P, T], F32, at=ada_at + 4 * UNIT)
        score = sb("score", [P, AH, 2 * P], F32, at=tmp_at)
        a_sq = sb("a_sq", [P, QK, AD], F32, at=region + 30 * UNIT)
        a_rot = sb("a_rot", [P, 4, NT * QK * ROPE_HALF], F32, at=region + 32 * UNIT)

        bank = [ctx.enter_context(nc.psum_tensor(f"bank{i}", [P, T], F32)) for i in range(8)]

        ident = const[:, K_IDENT:K_IDENT + P]
        per_d, per_h = const[:, K_PER_D:K_PER_D + 1], const[:, K_PER_H:K_PER_H + 1]
        eps = const[:, K_EPS:K_EPS + 1]
        amask = const[:, K_AMASK:K_AMASK + 2 * P]
        one = const[:, K_ONE:K_ONE + 1]

        def sem(name):
            return ctx.enter_context(nc.semaphore(name))

        setup_in = sem("setup_in")
        setup_pe = sem("setup_pe")
        setup_cols = sem("setup_cols")
        setup_step = sem("setup_step")
        setup_act = sem("setup_act")
        angles = sem("angles")
        raw_in = [sem("raw_in0"), sem("raw_in1")]
        hi_ready = sem("hi_ready")
        lo_ready = sem("lo_ready")
        panel_used = sem("panel_used")
        x_in = sem("x_in")
        lmask_in = sem("lmask_in")
        first_in = [sem(f"first_in{k}") for k in range(KD)]
        first_step = sem("first_step")
        ada_in = [sem(f"ada_in{i}") for i in range(ADA_RING)]
        ada_step = sem("ada_step")
        ada_cols = sem("ada_cols")
        mod_ready = sem("mod_ready")
        silu_done = sem("silu_done")
        hid_done = sem("hid_done")
        hid_hi_done = sem("hid_hi_done")
        hid_lo_done = sem("hid_lo_done")
        setup_x = sem("setup_x")
        x_done = sem("x_done")
        sq_done = sem("sq_done")
        sum_done = sem("sum_done")
        sum_zero = sem("sum_zero")
        ms_done = sem("ms_done")
        root_done = sem("root_done")
        inv_done = sem("inv_done")
        rstd_done = sem("rstd_done")
        xn_done = sem("xn_done")
        hf_done = sem("hf_done")
        h_hi_done = sem("h_hi_done")
        h_lo_done = sem("h_lo_done")
        gate_col_done = sem("gate_col_done")
        in_read = sem("in_read")
        turn_done = sem("turn_done")
        turn_read = sem("turn_read")
        gates_ready = sem("gates_ready")
        att_done = sem("att_done")
        att_read = sem("att_read")
        kq_ready = sem("kq_ready")
        key_done = sem("key_done")
        key_read = sem("key_read")
        upd_done = sem("upd_done")
        state_done = sem("state_done")
        o_done = sem("o_done")
        osq_done = sem("osq_done")
        oms_done = sem("oms_done")
        oroot_done = sem("oroot_done")
        oinv_done = sem("oinv_done")
        orstd_done = sem("orstd_done")
        aroot_done = sem("aroot_done")
        omix_done = sem("omix_done")
        mix_hi = sem("mix_hi")
        mix_lo = sem("mix_lo")
        asq_done = sem("asq_done")
        asq_read = sem("asq_read")
        rot_done = sem("rot_done")
        at_done = sem("at_done")
        at_read = sem("at_read")
        score_done = sem("score_done")
        score_read = sem("score_read")
        max_done = sem("max_done")
        exp_done = sem("exp_done")
        prob_done = sem("prob_done")
        pt_done = sem("pt_done")
        pt_read = sem("pt_read")
        pv_done = sem("pv_done")
        amix_hi = sem("amix_hi")
        amix_lo = sem("amix_lo")
        passed = sem("passed")
        step = sem("step")
        row_in = sem("row_in")
        out_pe = sem("out_pe")
        out_sb = sem("out_sb")
        stored = sem("stored")

        STARTS = [(lo_ready, 2), (panel_used, 2), (ada_step, ADA_RING), (silu_done, 2), (hid_done, 2), (x_done, 2),
                  (sum_done, 2), (h_lo_done, 2), (in_read, 2), (turn_done, 2), (turn_read, 2), (att_read, 2),
                  (asq_read, 1), (score_read, 2), (rot_done, 1)]

        def X(l, stage, d):
            return KD + l * 3 * KD + stage * KD + d

        def A(l, u):
            return l * ADA_UNITS + ADA_FIRST[u[0]] + u[1]

        def A_COL(u):
            return (ADA_EARLY * KD, ADA_EARLY * KD + ADA_ITERATIONS[0] * KD // 2, 0)[u[0]] + u[1] * (KD // 2)

        def A_LAYER(l, u):
            return DEPTH - 1 if u[0] == 2 else l

        def M(l, v):
            return l * ADA_UNITS + 1 + (0 if v < ADA_EARLY else 2 * (v + 1 - ADA_EARLY))

        N_SETUP = 1 + DEPTH * 7 + 2
        UNITS = HH * (LEVELS + 1)
        STEPS = 47

        w_gu = {P_GU1: (a["ffn1_w_gate"], a["ffn1_w_up"]), P_GU2: (a["ffn2_w_gate"], a["ffn2_w_up"])}
        w_dn = {P_DN1: a["ffn1_w_down"], P_DN2: a["ffn2_w_down"]}

        block = ctx.enter_context(nc.Block())

        @block.sync
        def _(sp):
            def load_in(dst, src):
                sp.dma_start(dst, src).then_inc(setup_in, 16)

            for l in range(DEPTH):
                load_in(col_rows[C_C:C_C + KD, l, :], a["c"][0].rearrange("(r p) -> r p", p=P))
                for at, src, n in ((C_ADAB, a["ada_b"], N_MOD * KD), (C_NORM, a["norm_ffn1"], KD),
                                   (C_NORM + KD, a["norm_mix"], KD), (C_NORM + 2 * KD, a["norm_ffn2"], KD),
                                   (C_LB, a["lb_logits"], HH), (C_HNORM, a["hgrn_norm"], 1)):
                    load_in(col_rows[at:at + n, l, :], src[l].rearrange("(r p) -> r p", p=P))
            load_in(const[:], a["const"])
            sp.dma_start(pos_i[:], a["positions"][0].rearrange("(n p) -> p n", p=P), allow_slow_non_contiguous=True)\
              .then_inc(setup_in, 16)
            load_in(sinks[:].rearrange("p l h -> p (l h)"),
                    a["sinks"].rearrange("(o l) h -> o (l h)", o=1).to_broadcast([P, DEPTH * AH]))
            sp.dma_start(x_rows[:], a["x"][0].rearrange("(n p) d -> p n d", p=P)).then_inc(x_in, 16)
            for k in range(KD):
                sp.dma_start(ada_first[:, k, :], a["ada_w"][0, k * P:(k + 1) * P, 0:2 * D]).then_inc(first_in[k], 16)
            sp.dma_start(lmask[:], a["lmask"].rearrange("p (v t) -> p v t", v=LEVELS)).then_inc(lmask_in, 16)

            def load_panel(l, n, kind, i, slot):
                sp.wait_ge(lo_ready, l * PANELS + n + 1)
                if kind in w_gu:
                    src = w_gu[kind][slot % 2][bass.ds(l, 1), :, bass.ds(i * P, P)]
                    k = KD
                elif kind in w_dn:
                    d, half = i
                    src = w_dn[kind][bass.ds(l, 1), half * HALF * P:(half + 1) * HALF * P, bass.ds(d * P, P)]
                    k = HALF
                else:
                    src = (a["w_in"] if kind == P_IN else a["w_out"])[bass.ds(l, 1), :, bass.ds(i * P, P)]
                    k = KD
                dst = raw[:, slot % 2, 0:k * P].rearrange("p (k c) -> p k c", c=P)
                sp.dma_start(dst, src.rearrange("a (k p) c -> p (a k) c", p=P)).then_inc(raw_in[slot % 2], 16)

            def load_ada(l, u, s):
                sp.wait_ge(ada_step, A(l, u) * KD + s + 1)
                src = a["ada_w"][bass.ds(A_LAYER(l, u), 1), s * P:(s + 1) * P, bass.ds(A_COL(u) * P, T)]
                sp.dma_start(ada_raw[:, s % ADA_RING, :], src.rearrange("a p c -> p (a c)"))\
                  .then_inc(ada_in[s % ADA_RING], 16)

            def gate_up_loads(l, ffn, i, ada=None, last=False):
                base = (P_GU1, P_GU2)[ffn]
                for q in range(4):
                    if last and q >= 2:
                        load_panel(l, base + GU + q - 2, base + GU, (0, q % 2), q)
                    else:
                        load_panel(l, base + 4 * i + q + 2, base, 2 * i + (q + 2) // 2, q)
                    if ada is not None:
                        for s in range(*ADA_SHARE[q]):
                            load_ada(l, ada, s)

            def down_loads(l, ffn, i, last=False):
                base = (P_DN1, P_DN2)[ffn]
                for q in range(4):
                    if last and q >= 2:
                        if ffn == 0:
                            load_panel(l, P_IN + q - 2, P_IN, IN_ORDER[q - 2], q)
                    else:
                        load_panel(l, base + 4 * i + q + 2, base, (2 * i + (q + 2) // 2, q % 2), q)
                    if ffn == 0:
                        for s in range(*ADA_SHARE[q]):
                            load_ada(l, (1, i), s)

            def ffn_loads(l, ffn):
                phase = 2 * ffn
                n_ada = ADA_ITERATIONS[phase]
                with sp.Fori(0, n_ada) as i:
                    gate_up_loads(l, ffn, i, (phase, i))
                if n_ada < FT // 2 - 1:
                    with sp.Fori(n_ada, FT // 2 - 1) as i:
                        gate_up_loads(l, ffn, i)
                gate_up_loads(l, ffn, FT // 2 - 1, last=True)
                with sp.Fori(0, KD // 2 - 1) as i:
                    down_loads(l, ffn, i)
                down_loads(l, ffn, KD // 2 - 1, last=True)

            with sp.Fori(0, DEPTH) as l:
                sp.wait_ge(rot_done, l + 1)
                sp.dma_start(qkw[:, 0:AH, :], a["q_norm"][bass.ds(l, 1)].unsqueeze(1).to_broadcast([P, AH, AD]))\
                  .then_inc(row_in, 16)
                sp.dma_start(qkw[:, AH:QK, :], a["k_norm"][bass.ds(l, 1)].unsqueeze(1).to_broadcast([P, KVH, AD]))\
                  .then_inc(row_in, 16)
                for q in range(2):
                    load_panel(l, P_GU1 + q, P_GU1, 0, q)
                ffn_loads(l, 0)
                for i in range(2, IN_TILES):
                    load_panel(l, P_IN + i, P_IN, IN_ORDER[i], i)
                with sp.Fori(0, KD // 2) as i:
                    for q in range(2):
                        load_panel(l, P_OUT + 2 * i + q, P_OUT, 2 * i + q, q)
                for q in range(2):
                    load_panel(l, P_GU2 + q, P_GU2, 0, q)
                sp.wait_ge(score_read, (l + 1) * 4 * NT + 2)
                sp.sem_inc(passed, 1)
                ffn_loads(l, 1)

            sp.wait_ge(out_sb, KD)
            sp.dma_start(out[0].rearrange("(n p) d -> p n d", p=P), x_rows[:]).then_inc(stored, 16)
            sp.wait_ge(stored, 16)

        @block.scalar
        def _(act):
            def split_hi(l, n, k, slot):
                act.wait_ge(raw_in[slot % 2], l * (PANELS // 2 * 16) + (n // 2 + 1) * 16 if isinstance(n, int)
                            else l * (PANELS // 2 * 16) + n * 8 + (16 - 8 * (slot % 2)))
                act.wait_ge(panel_used, l * PANELS + n + 1)
                nc.scalar.activation(w_hi[:, slot % 2, 0:k * P], raw[:, slot % 2, 0:k * P], ACT.Copy)\
                    .then_inc(hi_ready, 1)

            def square_tile(l, stage, d, slot):
                act.wait_ge(x_done, X(l, stage, d) + 3)
                act.wait_ge(sum_done, X(l, stage, d) + 1)
                nc.scalar.activation(sq[:, slot % 2, :], x[:, bass.ds(d, 1), :].rearrange("p a t -> p (a t)"), ACT.Square)\
                    .then_inc(sq_done, 1)

            act.wait_ge(setup_cols, DEPTH)
            nc.scalar.activation(cact[:], cols[:, 0, C_C:C_C + KD], ACT.Silu).then_inc(setup_act, 1)
            act.wait_ge(angles, 1)
            nc.scalar.activation(lb_tmp[:, 4:4 + DEPTH], lb_tmp[:, 4:4 + DEPTH], ACT.Exp).then_inc(setup_act, 1)
            act.wait_ge(angles, 2)
            nc.scalar.activation(sin_t[:], rope_tmp[:, 0], ACT.Sin).then_inc(setup_act, 1)
            nc.scalar.activation(cos_t[:], rope_tmp[:, 0], ACT.Sin, scale=0.5).then_inc(setup_act, 1)
            for d in range(KD):
                square_tile(0, -1, d, d)

            def norm(l, n):
                vec = (0, 3, 6)[n]
                act.wait_ge(ms_done, l * 3 + n + 1)
                nc.scalar.activation(root[:], bank[6][:, 0:NT], ACT.Sqrt, bias=eps).then_inc(root_done, 1)
                act.wait_ge(inv_done, l * 3 + n + 1)
                for k in range(KD):
                    at = l * (3 * KD) + n * KD + k
                    act.wait_ge(xn_done, at + 1)
                    act.wait_ge(h_lo_done, at + 1)
                    nc.scalar.activation(hidf[:, k % 2, :], sil[:, k % 2, :], ACT.Identity,
                                         bias=mod[:, vec * KD + k:vec * KD + k + 1], scale=scale_col[:, k:k + 1]).then_inc(hf_done, 1)
                    act.wait_ge(hf_done, at + 1)
                    nc.scalar.activation(h_hi[:, k, :], hidf[:, k % 2, :], ACT.Copy).then_inc(h_hi_done, 1)

            def silu_tile(l, ffn, f, slot):
                at = l * (2 * FT) + ffn * FT + f
                act.wait_ge(panel_used, l * PANELS + (P_GU1, P_GU2)[ffn] + 2 * f + 3)
                act.wait_ge(hid_done, at + 1)
                nc.scalar.activation(sil[:, slot, :], bank[2 * slot][:], ACT.Silu).then_inc(silu_done, 1)

            def hidden_hi(l, ffn, f, slot):
                act.wait_ge(hid_done, l * (2 * FT) + ffn * FT + f + 3)
                nc.scalar.activation(hid_hi[:, bass.ds(f, 1), :].rearrange("p a t -> p (a t)"), hidf[:, slot, :], ACT.Copy)\
                    .then_inc(hid_hi_done, 1)

            def gate_up(l, ffn, i, last=False):
                base = (P_GU1, P_GU2)[ffn]
                for q in range(4):
                    split_hi(l, base + 4 * i + q + 2, HALF if last and q >= 2 else KD, q)
                    if q % 2 == 0:
                        silu_tile(l, ffn, 2 * i + q // 2, q // 2)
                    else:
                        hidden_hi(l, ffn, 2 * i + q // 2, q // 2)

            def down(l, ffn, i, after):
                base = (P_DN1, P_DN2)[ffn]
                for q in range(4):
                    if q < 2 or after:
                        split_hi(l, base + 4 * i + q + 2, HALF if q < 2 else after, q)
                    if q % 2:
                        square_tile(l, 2 * ffn, 2 * i + q // 2, q // 2)

            def ffn_phase(l, ffn):
                norm(l, 2 * ffn)
                with act.Fori(0, FT // 2 - 1) as i:
                    gate_up(l, ffn, i)
                gate_up(l, ffn, FT // 2 - 1, last=True)
                with act.Fori(0, KD // 2 - 1) as i:
                    down(l, ffn, i, HALF)
                down(l, ffn, KD // 2 - 1, (KD, 0)[ffn])

            def mixers(l):
                def tile_(i):
                    kind, c = KINDS[IN_ORDER[i]], IN_ORDER[i] % 4
                    split_hi(l, P_IN + i + 2, KD, i)
                    act.wait_ge(panel_used, l * PANELS + P_IN + i + 3)
                    src = bank[i % 2][:]
                    if kind == K_F:
                        nc.scalar.activation(f_t[:, c, :], src, ACT.Sigmoid)
                        nc.scalar.activation(k_t[:, c, :], src, ACT.Sigmoid, scale=-1.0).then_inc(in_read, 1)
                    elif kind == K_Q:
                        nc.scalar.activation(q_t[:, c, :], src, ACT.Copy, scale=HD ** -0.5).then_inc(in_read, 1)
                    elif kind == K_G:
                        nc.scalar.activation(g_t[:, c, :], src, ACT.Silu).then_inc(in_read, 1)
                    else:
                        act.wait_ge(turn_done, l * TURNS + TURN_OF[i] + 1)
                        nc.scalar.activation(evac[:, TURN_OF[i] % 2, :], src, ACT.Copy).then_inc(in_read, 1)

                def keys(_):
                    for h in range(HH):
                        act.wait_ge(key_done, l * HH + h + 1)
                        nc.scalar.activation(key_n[:, h, 0:NT - 1, :],
                                             bank[6 + h % 2][:, 0:(NT - 1) * P].rearrange("p (c d) -> p c d", d=P),
                                             ACT.Copy).then_inc(key_read, 1)

                def hout(h):
                    act.wait_ge(o_done, l * HH + h + 1)
                    if h >= 2:
                        act.wait_ge(oms_done, l * HH + h - 1)
                    nc.scalar.activation(o_n[:, h, :], bank[2 + h % 2][:], ACT.Copy)
                    nc.scalar.activation(sq[:, h % 2, :], bank[2 + h % 2][:], ACT.Square).then_inc(osq_done, 1)

                def hroot(_):
                    act.wait_ge(oms_done, (l + 1) * HH)
                    nc.scalar.activation(o_root[:], bank[7][:, 0:HH * NT], ACT.Sqrt, bias=eps).then_inc(oroot_done, 1)

                def hnorm(h):
                    act.wait_ge(omix_done, l * HH + h + 1)
                    act.wait_ge(panel_used, l * PANELS + P_OUT + 2)
                    nc.scalar.activation(h_hi[:, h, :], o_mix[:, h % 2, :], ACT.Copy).then_inc(mix_hi, 1)

                def aprep(_):
                    act.wait_ge(turn_read, (l + 1) * TURNS + 2)
                    for n in range(NT):
                        act.wait_ge(asq_read, l * NT + n + 1)
                        nc.scalar.activation(a_sq[:], aqk[:, n], ACT.Square).then_inc(asq_done, 1)
                    act.wait_ge(asq_read, (l + 1) * NT + 1)
                    nc.scalar.activation(a_ss[:], a_ss[:], ACT.Sqrt, bias=eps, scale=1.0 / AD).then_inc(aroot_done, 1)
                    for j in range(QK // 2):
                        act.wait_ge(at_done, l * 5 + j + 1)
                        dst, mul = (aq_t[:, j, :], AD ** -0.5) if j < 4 else (ak_t[:], 1.0)
                        nc.scalar.activation(dst, bank[4 + j % 2][:], ACT.Copy, scale=mul).then_inc(at_read, 1)

                def prob(n):
                    lo = 0 if n else P
                    act.wait_ge(max_done, l * NT + n + 1)
                    for j in range(AH):
                        nc.scalar.activation(score[:, j, lo:], score[:, j, lo:], ACT.Exp,
                                             bias=a_negmax[:, n % 2, j:j + 1], accum_out=a_den[:, n % 2, j:j + 1])
                    nc.scalar.activation(a_sink[:, n % 2, :], a_sink[:, n % 2, :], ACT.Exp).then_inc(exp_done, 1)
                    for j in range(4):
                        act.wait_ge(pt_done, l * 4 * NT + n * 4 + j + 1)
                        src = bank[2 + j % 2][:].rearrange("p (a q) -> p a q", q=P)
                        dst = pt[:, j % 2]
                        if n == 0:
                            src, dst = src[:, 1::2], dst[:, 1::2]
                        nc.scalar.activation(dst, src, ACT.Copy).then_inc(pt_read, 1)
                    act.wait_ge(pv_done, l * NT + n + 1)
                    nc.scalar.activation(h_hi[:, 4:8, n * P:(n + 1) * P], bank[6][:].rearrange("p (c q) -> p c q", q=P),
                                         ACT.Copy).then_inc(amix_hi, 1)

                do = dict(tile=tile_, keys=keys, hout=hout, hroot=hroot, hnorm=hnorm, aprep=aprep, prob=prob)
                for what, n in MIX_STEPS:
                    if what in do:
                        do[what](n)

            with act.Fori(0, DEPTH) as l:
                for n in range(2):
                    split_hi(l, n, KD, n)
                ffn_phase(l, 0)
                norm(l, 1)
                mixers(l)
                with act.Fori(0, KD // 2) as i:
                    for q in range(2):
                        split_hi(l, P_OUT + 2 * i + q + 2, KD, q)
                        square_tile(l, 1, 2 * i + q, q)
                ffn_phase(l, 1)

            for d in range(KD):
                act.wait_ge(out_pe, d + 1)
                nc.scalar.activation(x_rows[:, :, d * P:(d + 1) * P], bank[d][:].rearrange("p (n c) -> p n c", c=P),
                                     ACT.Copy).then_inc(out_sb, 1)

        @block.tensor
        def _(pe):
            def product(dst, wslot, k, act_hi, act_lo, k0=0, first=True, last=True, ready=None):
                for kt in range(k):
                    hi = w_hi[:, wslot, kt * P:(kt + 1) * P]
                    lo = w_lo[:, wslot, kt * P:(kt + 1) * P]
                    if ready is not None:
                        ready(kt)
                    nc.tensor.matmul(dst, hi, act_hi[:, k0 + kt, :], start=first and kt == 0, stop=False)
                    nc.tensor.matmul(dst, hi, act_lo[:, k0 + kt, :], start=False, stop=False)
                    mm = nc.tensor.matmul(dst, lo, act_hi[:, k0 + kt, :], start=False, stop=last and kt == k - 1)
                mm.then_inc(panel_used, 1)
                return mm

            pe.wait_ge(setup_in, N_SETUP * 16)
            for l in range(DEPTH):
                nc.tensor.transpose(bank[l][:, 0:N_COLS], col_rows[0:N_COLS, l, :], ident[0:N_COLS, 0:N_COLS])\
                    .then_inc(setup_pe, 1)
            pe.wait_ge(x_in, 16)
            for d in range(KD):
                pe.wait_ge(x_done, d + 1)
                for n in range(NT):
                    mm = nc.tensor.transpose(bank[4 + d % 2][:, n * P:(n + 1) * P], x_rows[:, n, d * P:(d + 1) * P], ident)
                mm.then_inc(setup_x, 1)

            pe.wait_ge(first_step, KD)
            for m in range(2 * KD):
                mm = nc.tensor.matmul(bank[7][:, m:m + 1], ada_sum[:, m * P:(m + 1) * P], one, start=True, stop=True)
            mm.then_inc(ada_cols, 1)

            def ada_columns(l, u):
                pe.wait_ge(ada_step, A(l, u) * KD + KD + ADA_RING)
                for m in range(KD // 2):
                    mm = nc.tensor.matmul(bank[7][:, m:m + 1], ada_acc[:, m * P:(m + 1) * P], one, start=True, stop=True)
                mm.then_inc(ada_cols, 1)

            def norm(l, n):
                pe.wait_ge(sum_done, X(l, n - 1, 0) + KD + 2)
                for c in range(NT):
                    mm = nc.tensor.matmul(bank[6][:, c:c + 1], ssum[:, c * P:(c + 1) * P], per_d, start=True, stop=True)
                mm.then_inc(ms_done, 1)
                pe.wait_ge(inv_done, l * 3 + n + 1)
                for c in range(NT):
                    mm = nc.tensor.matmul(bank[6][:, c * P:(c + 1) * P], inv[:, c:c + 1].to_broadcast([P, P]), ident,
                                          start=True, stop=True)
                mm.then_inc(rstd_done, 1)

            def gate_up(l, ffn, i, ada=None):
                base = (P_GU1, P_GU2)[ffn]
                for q in range(4):
                    f = 2 * i + q // 2
                    pe.wait_ge(lo_ready, l * PANELS + base + 4 * i + q + 3)
                    pe.wait_ge(hid_done if q % 2 else silu_done, l * (2 * FT) + ffn * FT + f + 1)
                    ready = (lambda kt: pe.wait_ge(h_lo_done, l * (3 * KD) + 2 * ffn * KD + kt + 3)) if q == 0 else None
                    product(bank[q][:], q % 2, KD, h_hi, h_lo, ready=ready)
                if ada is not None:
                    ada_columns(l, ada)

            def down(l, ffn, i, first):
                base = (P_DN1, P_DN2)[ffn]
                for q in range(4):
                    d = 2 * i + q // 2
                    pe.wait_ge(lo_ready, l * PANELS + base + 4 * i + q + 3)
                    if q % 2 == 0:
                        pe.wait_ge(x_done, X(l, 2 * ffn, d) + 1)
                    ready = None
                    if first and q < 2:
                        def ready(kt, q=q):
                            pe.wait_ge(hid_lo_done, l * (2 * FT) + ffn * FT + q * HALF + kt + 1)
                    product(bank[4 + q // 2][:], q % 2, HALF, hid_hi, hid_lo, k0=(q % 2) * HALF, first=q % 2 == 0,
                            last=q % 2 == 1, ready=ready)
                if ffn == 0:
                    ada_columns(l, (1, i))

            def ffn_phase(l, ffn):
                norm(l, 2 * ffn)
                phase = 2 * ffn
                n_ada = ADA_ITERATIONS[phase]
                with pe.Fori(0, n_ada) as i:
                    gate_up(l, ffn, i, (phase, i))
                with pe.Fori(n_ada, FT // 2) as i:
                    gate_up(l, ffn, i)
                down(l, ffn, 0, True)
                with pe.Fori(1, KD // 2) as i:
                    down(l, ffn, i, False)

            def mixers(l):
                def tile_(i):
                    pe.wait_ge(lo_ready, l * PANELS + P_IN + i + 3)
                    pe.wait_ge(in_read, l * IN_TILES + i + 1)
                    ready = (lambda kt: pe.wait_ge(h_lo_done, l * (3 * KD) + KD + kt + 3)) if i == 0 else None
                    product(bank[i % 2][:], i % 2, KD, h_hi, h_lo, ready=ready)

                def turn(i):
                    e = TURN_OF[i]
                    pe.wait_ge(in_read, l * IN_TILES + i + 3)
                    pe.wait_ge(turn_read, l * TURNS + e + 1)
                    for n in range(NT):
                        mm = nc.tensor.transpose(bank[4 + e % 2][:, n * P:(n + 1) * P], evac[:, e % 2, n * P:(n + 1) * P], ident)
                    mm.then_inc(turn_done, 1)

                def units(first, left, right):
                    for h in range(HH):
                        u = first + h
                        pe.wait_ge(att_read, l * UNITS + u + 1)
                        for c in range(NT):
                            cut = slice(c * P, (c + 1) * P)
                            mm = nc.tensor.matmul(bank[6 + u % 2][:, cut], left(h)[:, cut], right(h)[:, cut],
                                                  start=True, stop=True)
                        mm.then_inc(att_done, 1)

                def diag(_):
                    pe.wait_ge(gates_ready, l + 1)
                    pe.wait_ge(in_read, l * IN_TILES + 8 + 2)
                    units(0, lambda h: k_t[:, h, :], lambda h: q_t[:, h, :])

                def level(v):
                    pe.wait_ge(kq_ready, l * (LEVELS + 2) + v + 1)
                    units(HH * (v + 1), lambda h: kq[:, v % 2, h, :], lambda h: kq[:, v % 2, h, :])

                def keys(_):
                    pe.wait_ge(kq_ready, l * (LEVELS + 2) + LEVELS + 2)
                    pe.wait_ge(att_read, (l + 1) * UNITS + 2)
                    for h in range(HH):
                        if h >= 2:
                            pe.wait_ge(key_read, l * HH + h - 1)
                        for c in range(NT - 1):
                            mm = nc.tensor.transpose(bank[6 + h % 2][:, c * P:(c + 1) * P],
                                                     kq[:, 0, h, c * P:(c + 1) * P], ident)
                        mm.then_inc(key_done, 1)

                def states(_):
                    pe.wait_ge(turn_read, l * TURNS + HH + 2)
                    for h in range(HH):
                        pe.wait_ge(key_read, l * HH + max(h, 2 + h % 2) + 1)
                        if h >= 2:
                            pe.wait_ge(state_done, l * HH + h - 1)
                        for c in range(NT - 1):
                            mm = nc.tensor.matmul(bank[6 + h % 2][:, c * P:(c + 1) * P], key_n[:, h, c, :],
                                                  v_n[:, h, c, :], start=True, stop=True)
                        mm.then_inc(upd_done, 1)

                def hout(h):
                    pe.wait_ge(state_done, l * HH + HH)
                    if h >= 2:
                        pe.wait_ge(osq_done, l * HH + h - 1)
                    for c in range(NT):
                        cut = slice(c * P, (c + 1) * P)
                        mm = nc.tensor.matmul(bank[2 + h % 2][:, cut], v_n[:, h, c, :], att[:, h, cut], start=True, stop=c == 0)
                        if c:
                            mm = nc.tensor.matmul(bank[2 + h % 2][:, cut], state[:, h, c - 1, :], kq[:, 1, h, cut],
                                                  start=False, stop=True)
                    mm.then_inc(o_done, 1)

                def hms(h):
                    pe.wait_ge(osq_done, l * HH + h + 1)
                    for c in range(NT):
                        mm = nc.tensor.matmul(bank[7][:, h * NT + c:h * NT + c + 1], sq[:, h % 2, c * P:(c + 1) * P], per_h,
                                              start=True, stop=True)
                    mm.then_inc(oms_done, 1)

                def hnorm(h):
                    pe.wait_ge(oinv_done, l + 1)
                    if h >= 2:
                        pe.wait_ge(omix_done, l * HH + h - 1)
                    for c in range(NT):
                        mm = nc.tensor.matmul(bank[6 + h % 2][:, c * P:(c + 1) * P],
                                              o_inv[:, h * NT + c:h * NT + c + 1].to_broadcast([P, P]), ident,
                                              start=True, stop=True)
                    mm.then_inc(orstd_done, 1)

                def aprep(_):
                    pe.wait_ge(rot_done, l + 2)
                    for j in range(QK // 2):
                        if j >= 2:
                            pe.wait_ge(at_read, l * 5 + j - 1)
                        for n in range(NT):
                            mm = nc.tensor.transpose(bank[4 + j % 2][:, n * P:(n + 1) * P],
                                                     aqk[:, n, 2 * j:2 * j + 2, :].rearrange("p a d -> p (a d)"), ident)
                        mm.then_inc(at_done, 1)

                def score_(n):
                    if n == 0:
                        pe.wait_ge(at_read, l * 5 + 5)
                    lo = 0 if n else P
                    for u in range(4):
                        pair, g = u // 2, u % 2
                        pe.wait_ge(score_read, l * 4 * NT + n * 4 + u + 1)
                        for e in range(2):
                            mm = nc.tensor.matmul(bank[4 + g][:, e * 2 * P + lo:(e + 1) * 2 * P],
                                                  aq_t[AD * g:AD * (g + 1), 2 * pair + e, n * P:(n + 1) * P],
                                                  ak_t[AD * g:AD * (g + 1), (n - 1) * P + lo:(n + 1) * P],
                                                  start=True, stop=True)
                        mm.then_inc(score_done, 1)

                def prob(n):
                    pe.wait_ge(prob_done, l * NT + n + 1)
                    if n:
                        pe.wait_ge(amix_lo, l * NT + n)

                    def weigh(j):
                        pe.wait_ge(pt_read, l * 4 * NT + n * 4 + j + 1)
                        for e in range(2):
                            head = 2 * j + e
                            for b in range(0 if n else 1, 2):
                                mm = nc.tensor.matmul(
                                    bank[6][AD * (head % 2):AD * (head % 2 + 1), (head // 2) * P:(head // 2 + 1) * P],
                                    a_v[:, n - 1 + b, head // 4, :], pt[:, j % 2, 2 * e + b, :],
                                    start=b == 0 or n == 0, stop=b == 1, skip_group_check=True)
                        return mm

                    for j in range(4):
                        if j >= 2:
                            weigh(j - 2)
                        for e in range(2):
                            for b in range(0 if n else 1, 2):
                                mm = nc.tensor.transpose(bank[2 + j % 2][:, (2 * e + b) * P:(2 * e + b + 1) * P],
                                                         score[:, 2 * j + e, b * P:(b + 1) * P], ident)
                        mm.then_inc(pt_done, 1)
                    weigh(2)
                    weigh(3).then_inc(pv_done, 1)

                do = dict(tile=tile_, turn=turn, diag=diag, level=level, keys=keys, states=states, hout=hout, hms=hms,
                          hnorm=hnorm, aprep=aprep, score=score_, prob=prob)
                for what, n in MIX_STEPS:
                    if what in do:
                        do[what](n)

            with pe.Fori(0, DEPTH) as l:
                ffn_phase(l, 0)
                norm(l, 1)
                mixers(l)
                with pe.Fori(0, KD // 2) as i:
                    for q in range(2):
                        pe.wait_ge(lo_ready, l * PANELS + P_OUT + 2 * i + q + 3)
                        pe.wait_ge(x_done, X(l, 1, 2 * i + q) + 1)
                        if q == 0:
                            pe.wait_ge(mix_lo, l * HH + HH)
                            pe.wait_ge(amix_lo, l * NT + NT)
                        product(bank[4 + q][:], q, KD, h_hi, h_lo)
                ffn_phase(l, 1)

            pe.wait_ge(x_done, X(DEPTH - 1, 2, KD - 1) + 3)
            for d in range(KD):
                for n in range(NT):
                    mm = nc.tensor.transpose(bank[d][:, n * P:(n + 1) * P], x[:, d, n * P:(n + 1) * P], ident)
                mm.then_inc(out_pe, 1)

        @block.vector
        def _(dve):
            tt, ts, stt = nc.vector.tensor_tensor, nc.vector.tensor_scalar, nc.vector.scalar_tensor_tensor
            for signal, start in STARTS:
                dve.sem_inc(signal, start)

            def add_squares(l, stage, d, slot):
                at = X(l, stage, d)
                dve.wait_ge(sq_done, at + 1)
                dve.wait_ge(sum_done, at + 2)
                tt(ssum[:], ssum[:], sq[:, slot, :], ALU.add).then_inc(sum_done, 1)

            done = [0]

            def link(ins):
                done[0] += 1
                ins.then_inc(setup_step, 1)
                dve.wait_ge(setup_step, done[0])

            nc.vector.memset(ssum[:], 0.0).then_inc(sum_zero, 1)
            dve.wait_ge(sum_zero, 1)
            dve.wait_ge(setup_in, N_SETUP * 16)
            for l in range(DEPTH):
                dve.wait_ge(setup_pe, l + 1)
                nc.vector.tensor_copy(cols[:, l, :], bank[l][:, 0:N_COLS]).then_inc(setup_cols, 1)
            dve.wait_ge(setup_cols, DEPTH)
            logit = lambda l: cols[:, l, C_LB:C_LB + HH]
            top, total, run = lb_tmp[:, 0], lb_tmp[:, 1], lb_tmp[:, 2]
            prob_l = lambda l: lb_tmp[:, 4 + l]
            link(nc.vector.tensor_copy(top, logit(0)))
            for l in range(1, DEPTH):
                link(tt(top, top, logit(l), ALU.max))
            for l in range(DEPTH):
                link(tt(prob_l(l), logit(l), top, ALU.subtract))
            dve.sem_inc(angles, 1)
            dve.wait_ge(setup_act, 2)
            for l in range(DEPTH):
                link(nc.vector.tensor_copy(total, prob_l(0)) if l == 0 else tt(total, total, prob_l(l), ALU.add))
            link(nc.vector.reciprocal(total, total))
            for l in range(DEPTH):
                link(tt(prob_l(l), prob_l(l), total, ALU.mult))
                link(nc.vector.tensor_copy(run, prob_l(0)) if l == 0 else tt(run, run, prob_l(l), ALU.add))
                link(tt(lower[:, l, :], run, prob_l(0), ALU.subtract))
                link(ts(one_minus_lower[:, l, :], lower[:, l, :], -1.0, 1.0, ALU.mult, ALU.add))

            ang, turns_, part = rope_tmp[:, 0], rope_tmp[:, 1], rope_tmp[:, 2]
            link(nc.vector.tensor_copy(pos_f[:], pos_i[:]))
            link(tt(ang, pos_f[:].unsqueeze(2).to_broadcast([P, NT, ROPE_HALF]),
                    const[:, K_INVF:K_INVF + ROPE_HALF].unsqueeze(1).to_broadcast([P, NT, ROPE_HALF]), ALU.mult))
            link(ts(turns_, ang, 1.0 / TWO_PI, MAGIC, ALU.mult, ALU.add))
            link(ts(turns_, turns_, MAGIC, None, ALU.subtract))
            for c in TWO_PI_PARTS:
                link(stt(ang, turns_, -c, ang, ALU.mult, ALU.add))
            ts(ang, ang, PI_BELOW, -PI_BELOW, ALU.min, ALU.max).then_inc(angles, 1)
            dve.wait_ge(setup_act, 4)
            link(tt(part, cos_t[:], cos_t[:], ALU.mult))
            link(ts(cos_t[:], part, -2.0, 1.0, ALU.mult, ALU.add))

            for d in range(KD):
                dve.wait_ge(setup_x, d + 1)
                nc.vector.tensor_copy(x[:, d, :], bank[4 + d % 2][:]).then_inc(x_done, 1)
                if d:
                    add_squares(0, -1, d - 1, (d - 1) % 2)
            add_squares(0, -1, KD - 1, (KD - 1) % 2)

            dve.wait_ge(setup_act, 1)
            for k in range(KD):
                dve.wait_ge(first_in[k], 16)
                if k == 0:
                    ins = ts(ada_sum[:], ada_first[:, k, :], cact[:, k:k + 1], None, ALU.mult)
                else:
                    dve.wait_ge(first_step, k)
                    ins = stt(ada_sum[:], ada_first[:, k, :], cact[:, k:k + 1], ada_sum[:], ALU.mult, ALU.add)
                ins.then_inc(first_step, 1)
            dve.wait_ge(ada_cols, 1)
            tt(mod[:, 0:2 * KD], bank[7][:, 0:2 * KD], cols[:, 0, 0:2 * KD], ALU.add).then_inc(mod_ready, 1)
            dve.wait_ge(lmask_in, 16)

            def ada_piece(l, u, k):
                dve.wait_ge(ada_in[k % ADA_RING], A(l, u) * (KD // ADA_RING * 16) + (k // ADA_RING + 1) * 16)
                if k == 0:
                    ins = ts(ada_acc[:], ada_raw[:, k % ADA_RING, :], cact[:, k:k + 1], None, ALU.mult)
                else:
                    dve.wait_ge(ada_step, A(l, u) * KD + k + ADA_RING)
                    ins = stt(ada_acc[:], ada_raw[:, k % ADA_RING, :], cact[:, k:k + 1], ada_acc[:], ALU.mult, ALU.add)
                ins.then_inc(ada_step, 1)

            def ada_store(l, u):
                dve.wait_ge(ada_cols, A(l, u) + 2)
                tt(mod[:, bass.ds(A_COL(u), KD // 2)], bank[7][:, 0:KD // 2],
                   cols[:, bass.ds(A_LAYER(l, u), 1), bass.ds(A_COL(u), KD // 2)].rearrange("p a k -> p (a k)"), ALU.add)\
                    .then_inc(mod_ready, 1)

            def split_lo(l, n, k, slot):
                dve.wait_ge(hi_ready, l * PANELS + n + 1)
                tt(w_lo[:, slot % 2, 0:k * P], raw[:, slot % 2, 0:k * P], w_hi[:, slot % 2, 0:k * P], ALU.subtract)\
                    .then_inc(lo_ready, 1)

            def norm(l, n):
                dve.wait_ge(mod_ready, M(l, 3 * n + 1))
                dve.wait_ge(root_done, l * 3 + n + 1)
                stt(scale_col[:], mod[:, (3 * n + 1) * KD:(3 * n + 2) * KD], 1.0,
                    cols[:, bass.ds(l, 1), C_NORM + n * KD:C_NORM + (n + 1) * KD].rearrange("p a k -> p (a k)"),
                    ALU.add, ALU.mult)
                nc.vector.reciprocal(inv[:], root[:]).then_inc(inv_done, 1)
                nc.vector.memset(ssum[:], 0.0).then_inc(sum_zero, 1)
                dve.wait_ge(rstd_done, l * 3 + n + 1)

                def low(k):
                    dve.wait_ge(h_hi_done, l * (3 * KD) + n * KD + k + 1)
                    tt(h_lo[:, k, :], hidf[:, k % 2, :], h_hi[:, k, :], ALU.subtract).then_inc(h_lo_done, 1)

                for k in range(KD):
                    tt(sil[:, k % 2, :], bank[6][:], x[:, k, :], ALU.mult).then_inc(xn_done, 1)
                    if k:
                        low(k - 1)
                low(KD - 1)

            def gate_column(l, stage):
                dve.wait_ge(mod_ready, M(l, 3 * stage + 2))
                ts(gate_col[:], mod[:, (3 * stage + 2) * KD:(3 * stage + 3) * KD], 1.0 if stage == 1 else 0.5, None, ALU.mult)\
                    .then_inc(gate_col_done, 1)
                dve.wait_ge(gate_col_done, l * 3 + stage + 1)
                dve.sem_inc(passed, 1)

            def update_x(l, stage, d, slot, panels):
                dve.wait_ge(panel_used, panels + 2)
                xd = x[:, bass.ds(d, 1), :].rearrange("p a t -> p (a t)")
                stt(xd, bank[4 + slot][:], gate_col[:, bass.ds(d, 1)], xd, ALU.mult, ALU.add).then_inc(x_done, 1)

            def hidden(l, ffn, f, slot):
                dve.wait_ge(panel_used, l * PANELS + (P_GU1, P_GU2)[ffn] + 2 * f + 4)
                dve.wait_ge(silu_done, l * (2 * FT) + ffn * FT + f + 3)
                tt(hidf[:, slot, :], bank[2 * slot + 1][:], sil[:, slot, :], ALU.mult).then_inc(hid_done, 1)

            def hidden_lo(l, ffn, f, slot):
                dve.wait_ge(hid_hi_done, l * (2 * FT) + ffn * FT + f + 1)
                at = (slice(None), bass.ds(f, 1), slice(None))
                tt(hid_lo[at].rearrange("p a t -> p (a t)"), hidf[:, slot, :], hid_hi[at].rearrange("p a t -> p (a t)"),
                   ALU.subtract).then_inc(hid_lo_done, 1)

            def gate_up(l, ffn, i, last=False, ada=None):
                base = (P_GU1, P_GU2)[ffn]
                for q in range(4):
                    f, slot = 2 * i + q // 2, q // 2
                    if q % 2:
                        hidden(l, ffn, f, slot)
                    split_lo(l, base + 4 * i + q + 2, HALF if last and q >= 2 else KD, q)
                    if q % 2:
                        hidden_lo(l, ffn, f, slot)
                    if ada is not None:
                        for s in range(*ADA_SHARE[q]):
                            ada_piece(l, ada, s)
                if ada is not None:
                    ada_store(l, ada)

            def down(l, ffn, i, after):
                base = (P_DN1, P_DN2)[ffn]
                for q in range(4):
                    d = 2 * i + q // 2
                    if q % 2:
                        update_x(l, 2 * ffn, d, q // 2, l * PANELS + base + 4 * i + q + 1)
                    if q < 2 or after:
                        split_lo(l, base + 4 * i + q + 2, HALF if q < 2 else after, q)
                    if q % 2:
                        add_squares(l, 2 * ffn, d, q // 2)
                    if ffn == 0:
                        for s in range(*ADA_SHARE[q]):
                            ada_piece(l, (1, i), s)
                if ffn == 0:
                    ada_store(l, (1, i))

            def ffn_phase(l, ffn):
                norm(l, 2 * ffn)
                phase = 2 * ffn
                n_ada = ADA_ITERATIONS[phase]
                with dve.Fori(0, n_ada) as i:
                    gate_up(l, ffn, i, ada=(phase, i))
                if n_ada < FT // 2 - 1:
                    with dve.Fori(n_ada, FT // 2 - 1) as i:
                        gate_up(l, ffn, i)
                gate_up(l, ffn, FT // 2 - 1, last=True)
                gate_column(l, 2 * ffn)
                with dve.Fori(0, KD // 2 - 1) as i:
                    down(l, ffn, i, HALF)
                down(l, ffn, KD // 2 - 1, (KD, 0)[ffn])

            def mixers(l):
                count = [0]

                def own(ins):
                    count[0] += 1
                    ins.then_inc(step, 1)
                    dve.wait_ge(step, l * STEPS + count[0])

                def chunks(ap):
                    return ap.rearrange("p (c t) -> p c t", t=P)

                def tile_(i):
                    kind, c = KINDS[IN_ORDER[i]], IN_ORDER[i] % 4
                    split_lo(l, P_IN + i + 2, KD, i)
                    if kind == K_F:
                        dve.wait_ge(in_read, l * IN_TILES + i + 3)
                        ts(f_t[:, c, :], f_t[:, c, :], one_minus_lower[:, bass.ds(l, 1), c], lower[:, bass.ds(l, 1), c],
                           ALU.mult, ALU.add)
                        ins = ts(k_t[:, c, :], k_t[:, c, :], one_minus_lower[:, bass.ds(l, 1), c], None, ALU.mult)
                        if c == HH - 1:
                            ins.then_inc(gates_ready, 1)

                def turn(i):
                    kind, c, e = KINDS[IN_ORDER[i]], IN_ORDER[i] % 4, TURN_OF[i]
                    dve.wait_ge(turn_done, l * TURNS + e + 3)
                    src = chunks(bank[4 + e % 2][:])
                    if kind == K_V:
                        dst = v_n[:, c]
                    elif kind == K_AV:
                        dst = a_v[:].rearrange("p n g d -> p n (g d)")
                    elif kind == K_AK:
                        dst = aqk[:, :, AH:QK, :].rearrange("p n g d -> p n (g d)")
                    else:
                        at = 2 * (2 * c % 4) + 2 * c // 4
                        dst, src = aqk[:, :, at:at + 3:2, :], src.rearrange("p n (e d) -> p n e d", d=AD)
                    nc.vector.tensor_copy(dst, src).then_inc(turn_read, 1)

                def diag(_):
                    dve.wait_ge(gates_ready, l + 1)
                    own(nc.vector.memset(suf[:], 1.0))
                    build(0)
                    for h in range(HH):
                        dve.wait_ge(att_done, l * UNITS + h + 1)
                        tt(chunks(att[:, h, :]), chunks(bank[6 + h % 2][:]), ident.unsqueeze(1).to_broadcast([P, NT, P]),
                           ALU.mult).then_inc(att_read, 1)

                def halves(ap, v):
                    return ap.rearrange("p h (b w s) -> p (h b) w s", w=2, s=1 << v)

                def build(v):
                    kq_v, q_v, k_v, p_v, s_v = (halves(z, v) for z in (kq[:, v % 2], q_t[:], k_t[:], f_t[:], suf[:]))
                    b = 1 << v
                    shape = [P, HH * T // (2 * b), b]
                    tt(kq_v[:, :, 0], k_v[:, :, 0], s_v[:, :, 0], ALU.mult)
                    tt(kq_v[:, :, 1], q_v[:, :, 1], p_v[:, :, 1], ALU.mult).then_inc(kq_ready, 1)
                    own(tt(s_v[:, :, 0], s_v[:, :, 0], p_v[:, :, 1, b - 1:b].to_broadcast(shape), ALU.mult))
                    own(tt(p_v[:, :, 1], p_v[:, :, 1], p_v[:, :, 0, b - 1:b].to_broadcast(shape), ALU.mult))

                def level(v):
                    if v + 1 < LEVELS:
                        if v:
                            dve.wait_ge(att_done, l * UNITS + HH * (v + 1))
                        build(v + 1)
                    for h in range(HH):
                        u = HH * (v + 1) + h
                        dve.wait_ge(att_done, l * UNITS + u + 1)
                        dve.wait_ge(att_read, l * UNITS + u - HH + 3)
                        dve.sem_inc(passed, 1)
                        nc.vector.copy_predicated(chunks(att[:, h, :]), lmask[:, v].unsqueeze(1).to_broadcast([P, NT, P]),
                                                  chunks(bank[6 + u % 2][:])).then_inc(att_read, 1)

                def keys(_):
                    tt(kq[:, 1], q_t[:], f_t[:], ALU.mult).then_inc(kq_ready, 1)
                    tt(kq[:, 0], k_t[:], suf[:], ALU.mult).then_inc(kq_ready, 1)

                def states(_):
                    for h in range(HH):
                        dve.wait_ge(upd_done, l * HH + h + 1)
                        own(nc.vector.tensor_copy(state[:, h, 0, :], bank[6 + h % 2][:, 0:P]))
                        own(stt(state[:, h, 1, :], state[:, h, 0, :], f_t[:, h, 2 * P - 1:2 * P],
                                bank[6 + h % 2][:, P:2 * P], ALU.mult, ALU.add))
                        stt(state[:, h, 2, :], state[:, h, 1, :], f_t[:, h, 3 * P - 1:3 * P],
                            bank[6 + h % 2][:, 2 * P:3 * P], ALU.mult, ALU.add).then_inc(state_done, 1)

                def hroot(_):
                    dve.wait_ge(oroot_done, l + 1)
                    nc.vector.reciprocal(o_inv[:], o_root[:]).then_inc(oinv_done, 1)

                def hlow(h):
                    dve.wait_ge(mix_hi, l * HH + h + 1)
                    tt(h_lo[:, h, :], o_mix[:, h % 2, :], h_hi[:, h, :], ALU.subtract).then_inc(mix_lo, 1)

                def hnorm(h):
                    dve.wait_ge(orstd_done, l * HH + h + 1)
                    own(tt(o_n[:, h, :], bank[6 + h % 2][:], o_n[:, h, :], ALU.mult))
                    stt(o_mix[:, h % 2, :], o_n[:, h, :], cols[:, bass.ds(l, 1), C_HNORM],
                        g_t[:, h, :], ALU.mult, ALU.mult).then_inc(omix_done, 1)
                    if h:
                        hlow(h - 1)
                    if h == HH - 1:
                        hlow(h)

                def aprep(_):
                    for n in range(NT):
                        dve.wait_ge(asq_done, l * NT + n + 1)
                        nc.vector.tensor_reduce(a_ss[:, n, :], a_sq[:], AX_X, ALU.add).then_inc(asq_read, 1)
                    dve.wait_ge(aroot_done, l + 1)
                    own(nc.vector.reciprocal(a_ss[:], a_ss[:]))
                    dve.wait_ge(turn_read, (l + 1) * TURNS + 2)
                    flat = aqk[:].rearrange("p n h d -> p (n h) d")
                    own(tt(flat, flat, a_ss[:].rearrange("p n h -> p (n h)").unsqueeze(2).to_broadcast([P, NT * QK, AD]),
                           ALU.mult))
                    dve.wait_ge(row_in, (l + 1) * 32)
                    flat = aqk[:].rearrange("p n h d -> p n (h d)")
                    own(tt(flat, flat, qkw[:].rearrange("p h d -> p (h d)").unsqueeze(1).to_broadcast([P, NT, QK * AD]),
                           ALU.mult))
                    one_, two = aqk[:, :, :, 0:ROPE_HALF], aqk[:, :, :, ROPE_HALF:2 * ROPE_HALF]
                    shape = [P, NT, QK, ROPE_HALF]
                    cos_b, sin_b = (z[:].unsqueeze(2).to_broadcast(shape) for z in (cos_t, sin_t))
                    r = [a_rot[:, j].rearrange("p (n h d) -> p n h d", n=NT, h=QK) for j in range(4)]
                    tt(r[0], one_, cos_b, ALU.mult)
                    tt(r[1], two, sin_b, ALU.mult)
                    tt(r[2], two, cos_b, ALU.mult)
                    own(tt(r[3], one_, sin_b, ALU.mult))
                    tt(one_, r[0], r[1], ALU.subtract)
                    tt(two, r[2], r[3], ALU.add).then_inc(rot_done, 1)

                def score_(n):
                    lo = 0 if n else P
                    w = 2 * P - lo
                    if n:
                        dve.wait_ge(pt_done, l * 4 * NT + 4 * n)
                    for u in range(4):
                        pair, g = u // 2, u % 2
                        dve.wait_ge(score_done, l * 4 * NT + n * 4 + u + 1)
                        tt(score[:, 4 * g + 2 * pair:4 * g + 2 * pair + 2, lo:],
                           bank[4 + g][:].rearrange("p (e k) -> p e k", e=2)[:, :, lo:],
                           amask[:, lo:].unsqueeze(1).to_broadcast([P, 2, w]), ALU.add).then_inc(score_read, 1)
                    dve.wait_ge(score_read, l * 4 * NT + n * 4 + 6)
                    sink = sinks[:, bass.ds(l, 1), :].rearrange("p a h -> p (a h)")
                    own(nc.vector.tensor_reduce(a_max[:, n % 2, :], score[:, :, lo:], AX_X, ALU.max))
                    own(tt(a_max[:, n % 2, :], a_max[:, n % 2, :], sink, ALU.max))
                    tt(a_sink[:, n % 2, :], sink, a_max[:, n % 2, :], ALU.subtract)
                    ts(a_negmax[:, n % 2, :], a_max[:, n % 2, :], -1.0, None, ALU.mult).then_inc(max_done, 1)

                def prob(n):
                    lo = 0 if n else P
                    dve.wait_ge(exp_done, l * NT + n + 1)
                    own(tt(a_den[:, n % 2, :], a_den[:, n % 2, :], a_sink[:, n % 2, :], ALU.add))
                    own(nc.vector.reciprocal(a_den[:, n % 2, :], a_den[:, n % 2, :]))
                    tt(score[:, :, lo:], score[:, :, lo:],
                       a_den[:, n % 2, :].unsqueeze(2).to_broadcast([P, AH, 2 * P - lo]), ALU.mult).then_inc(prob_done, 1)
                    dve.wait_ge(amix_hi, l * NT + n + 1)
                    cut = slice(n * P, (n + 1) * P)
                    tt(h_lo[:, 4:8, cut], chunks(bank[6][:]), h_hi[:, 4:8, cut], ALU.subtract).then_inc(amix_lo, 1)

                do = dict(tile=tile_, turn=turn, diag=diag, level=level, keys=keys, states=states, hroot=hroot, hnorm=hnorm,
                          aprep=aprep, score=score_, prob=prob)
                for what, n in MIX_STEPS:
                    if what in do:
                        do[what](n)
                assert count[0] == STEPS, count[0]

            with dve.Fori(0, DEPTH) as l:
                for n in range(2):
                    split_lo(l, n, KD, n)
                ffn_phase(l, 0)
                norm(l, 1)
                mixers(l)
                gate_column(l, 1)
                with dve.Fori(0, KD // 2) as i:
                    for q in range(2):
                        update_x(l, 1, 2 * i + q, q, l * PANELS + P_OUT + 2 * i + q + 1)
                        split_lo(l, P_OUT + 2 * i + q + 2, KD, q)
                        add_squares(l, 1, 2 * i + q, q)
                ffn_phase(l, 1)


INPUTS = ["x", "c", "positions", "ada_w", "ada_b", "norm_ffn1", "ffn1_w_gate", "ffn1_w_up", "ffn1_w_down", "norm_mix",
          "w_in", "lb_logits", "hgrn_norm", "q_norm", "k_norm", "sinks", "w_out", "norm_ffn2", "ffn2_w_gate",
          "ffn2_w_up", "ffn2_w_down"]


def kernel(**inputs):
    import concourse.bacc as bacc
    from concourse.bass_utils import run_bass_kernel_spmd

    nc = bacc.Bacc("TRN2", target_bir_lowering=False, num_devices=1)
    arrays = {name: np.ascontiguousarray(inputs[name]) for name in INPUTS}
    arrays["const"], arrays["lmask"] = constants()
    aps = {name: nc.dram_tensor(name, v.shape, mybir.dt.from_np(v.dtype), kind="ExternalInput").ap()
           for name, v in arrays.items()}
    out = nc.dram_tensor("out", (1, T, D), F32, kind="ExternalOutput").ap()
    trunk_kernel(nc, aps, out)
    return run_bass_kernel_spmd(nc, [arrays], core_ids=[0]).results[0]["out"]
```

```python
from contextlib import ExitStack

import numpy as np

import concourse.bass as bass
from concourse import mybir

ALU = mybir.AluOpType
ACT = mybir.ActivationFunctionType
F32 = mybir.dt.float32
F32R = mybir.dt.float32r
I32 = mybir.dt.int32
AX_X = mybir.AxisListType.X

P = 128
DEPTH = 2
D = 1024
T = 512
KD = D // P
NT = T // P
F = 2816
FT = F // P
HH, HD = 4, 128
AH, KVH, AD = 8, 2, 64
QK = AH + KVH
ROPE_HALF = AD // 8
ROPE_THETA = 500000.0
N_MOD = 9
EPS = 1e-6
IN_TILES = 22
LEVELS = 7
NEG = -1e30
TWO_PI = float(2 * np.pi)
TWO_PI_PARTS = (6.28125, 4058 / 2.0 ** 21, 3.0199159795074593e-07)
PI_BELOW = 3.1415925
MAGIC = 1.5 * 2.0 ** 23

GU = 2 * FT
DN = 2 * KD
HALF = FT // 2
P_GU1, P_DN1 = 0, GU
P_IN = P_DN1 + DN
P_OUT = P_IN + IN_TILES
P_GU2 = P_OUT + KD
P_DN2 = P_GU2 + GU
PANELS = P_DN2 + DN
WIDE = HALF * P

C_ADAB, C_NORM = 0, N_MOD * KD
C_LB = C_NORM + 3 * KD
C_HNORM = C_LB + HH
C_C = C_HNORM + 1
N_COLS = C_C + KD

ADA_RING = 4
ADA_EARLY = 2
ADA_ITERATIONS = (10, 4, 4)
ADA_FIRST = (0, 10, 14)
ADA_UNITS = 18
assert ADA_UNITS == 2 * N_MOD and ADA_UNITS - ADA_FIRST[2] == 2 * ADA_EARLY
ADA_SHARE = ((0, 3), (3, 6), (6, 8), (8, 8))

IN_ORDER = [4, 5, 6, 7, 0, 1, 2, 3, 16, 17, 18, 19, 20, 21, 8, 9, 10, 11, 12, 13, 14, 15]
K_F, K_Q, K_V, K_G, K_AQ, K_AK, K_AV = "f", "q", "v", "g", "aq", "ak", "av"
KINDS = [K_Q] * 4 + [K_F] * 4 + [K_V] * 4 + [K_G] * 4 + [K_AQ] * 4 + [K_AK, K_AV]
TURNED = (K_V, K_AQ, K_AK, K_AV)
TURN_OF = {}
for _i, _c in enumerate(IN_ORDER):
    if KINDS[_c] in TURNED:
        TURN_OF[_i] = len(TURN_OF)
TURNS = len(TURN_OF)

A_UNITS = 4 * NT


def attention_at(u):
    steps = []
    if 0 <= u - 1 < A_UNITS:
        steps += [("prob", u - 1)]
    if 0 <= u - 2 < A_UNITS:
        steps += [("weigh", u - 2)]
    if u < A_UNITS:
        steps += [("score", u)]
        if u % 4 == 3:
            steps += [("sink", u // 4)]
    if u >= 2 and (u - 2) % 4 == 3:
        steps += [("anorm", (u - 2) // 4)]
    return steps


MIX_STEPS = []
for _i in range(8):
    MIX_STEPS += [("prod", (_i, 0)), ("prod", (_i, 1)), ("split", _i), ("read", _i)]
    if _i == 4:
        MIX_STEPS += [("ones", 0)]
MIX_STEPS += [("prod", (8, 0)), ("diag", 0), ("build", 0), ("prod", (8, 1)), ("diag", 1), ("extend", 0)]
for _v in range(LEVELS):
    _i = 9 + _v
    MIX_STEPS += [("read", _i - 1), ("level", (_v, 0)), ("split", _i - 1), ("prod", (_i, 0))]
    MIX_STEPS += [("build", _v + 1)] if _v + 1 < LEVELS else [("key_side", 0)]
    MIX_STEPS += [("turn", _i - 1), ("level", (_v, 1))]
    if _v + 1 < LEVELS:
        MIX_STEPS += [("extend", _v + 1)]
    if _i == 13:
        MIX_STEPS += [("asq", 0)]
    if _i == 14:
        MIX_STEPS += [("asq", 1), ("asq", 2), ("asq", 3), ("aroot", 0)]
    if _i == 15:
        MIX_STEPS += [("normalise", 0)]
    MIX_STEPS += [("prod", (_i, 1))]
MIX_STEPS += [("read", 15), ("split", 15), ("key", 0), ("key", 1), ("prod", (16, 0)), ("turn", 15),
              ("weights", 0), ("rotate", 0), ("key", 2), ("key", 3), ("prod", (16, 1))]
MIX_STEPS += [("read", 16), ("split", 16), ("query_side", 0)] + [("flip", _j) for _j in range(QK // 2)]
MIX_STEPS += [("prod", (17, 0)), ("turn", 16), ("update", 0), ("update", 1)] + attention_at(0)
MIX_STEPS += [("prod", (17, 1)), ("update", 2)]
_u = 1
for _i in range(18, IN_TILES):
    MIX_STEPS += [("read", _i - 1), ("split", _i - 1)]
    if _i == 18:
        MIX_STEPS += [("turn", 17), ("update", 3)]
    if _i < 20:
        MIX_STEPS += [("hout", 2 * (_i - 18))]
    MIX_STEPS += attention_at(_u) + [("prod", (_i, 0))]
    if _i < 20:
        MIX_STEPS += [("hout", 2 * (_i - 18) + 1)]
    MIX_STEPS += attention_at(_u + 1)
    if _i == IN_TILES - 1:
        MIX_STEPS += [("hms", 0), ("gates", 0)]
    MIX_STEPS += [("prod", (_i, 1))] + attention_at(_u + 2)
    _u += 3
MIX_STEPS += [("read", IN_TILES - 1), ("split", IN_TILES - 1)]
for _h in range(HH):
    MIX_STEPS += attention_at(_u) + [("hnorm", _h)]
    _u += 1
while _u < A_UNITS + 2:
    MIX_STEPS += attention_at(_u)
    _u += 1
MIX_STEPS += [("out", 0)] + [("back", _j) for _j in range(4)] + [("out", 1)]

K_IDENT, K_INVF, K_ONE, K_PER_D, K_PER_H, K_EPS = 0, 128, 136, 137, 138, 139
K_COLS = 140


def constants():
    c = np.zeros((P, K_COLS), np.float32)
    c[:, K_IDENT:K_IDENT + P] = np.eye(P)
    q, k = np.arange(P)[:, None], np.arange(2 * P)[None, :] - P
    amask = np.where((q - k >= 0) & (q - k < P), 0.0, NEG).astype(np.float32)
    rope = np.arange(0, 2 * ROPE_HALF, 2, dtype=np.float32) / np.float32(2 * ROPE_HALF)
    c[:, K_INVF:K_INVF + ROPE_HALF] = np.float32(ROPE_THETA) ** (-rope)
    c[:, K_ONE], c[:, K_PER_D], c[:, K_PER_H], c[:, K_EPS] = 1.0, 1.0 / D, 1.0 / HD, EPS
    s, t = np.arange(P)[:, None], np.arange(P)[None, :]
    masks = [(((s ^ t) >> v) == 1) & (t > s) for v in range(LEVELS)]
    return c, amask, np.concatenate(masks, axis=1).astype(np.int32)


def trunk_kernel(nc, a, out):
    ctx = ExitStack()
    with ctx:
        place = [16512]

        def sb(name, shape, dt=F32, at=None):
            n = int(np.prod(shape[1:])) * 4
            off = place[0] if at is None else at
            if at is None:
                place[0] += (n + 31) // 32 * 32
            return nc.alloc_sbuf_tensor_at(name, shape, dt, offset=off)

        UNIT = T * 4
        x = sb("x", [P, KD, T])
        h_hi = sb("h_hi", [P, KD, T], F32R)
        h_lo_at = place[0]
        h_lo = sb("h_lo", [P, KD, T], F32R)
        raw = sb("raw", [P, 2, WIDE])
        w_hi = sb("w_hi", [P, 2, WIDE], F32R)
        w_lo = sb("w_lo", [P, 2, WIDE], F32R)
        ada_at = place[0]
        ada_raw = sb("ada_raw", [P, ADA_RING, T])
        ada_acc = sb("ada_acc", [P, T])
        ada_rest = sb("ada_rest", [P, T])
        region = place[0]
        place[0] += 2 * FT * UNIT
        hid_hi = sb("hid_hi", [P, FT, T], F32R, at=region)
        hid_lo = sb("hid_lo", [P, FT, T], F32R, at=region + FT * UNIT)
        tmp_at = place[0]
        sil = sb("sil", [P, 2, T])
        hidf = sb("hidf", [P, 2, T])
        sq = sb("sq", [P, 2, T])
        root = sb("root", [P, NT])
        inv = sb("inv", [P, NT])
        o_root = sb("o_root", [P, HH * NT])
        o_inv = sb("o_inv", [P, HH * NT])
        ssum = sb("ssum", [P, T])
        const = sb("const", [P, K_COLS])
        lmask = sb("lmask", [P, LEVELS, P], I32)
        qkw = sb("qkw", [P, QK, AD])
        cols = sb("cols", [P, DEPTH, N_COLS])
        lower = sb("lower", [P, DEPTH, HH])
        one_minus_lower = sb("one_minus_lower", [P, DEPTH, HH])
        mod = sb("mod", [P, N_MOD * KD])
        scale_col = sb("scale_col", [P, KD])
        gate_col = sb("gate_col", [P, KD])
        cact = sb("cact", [P, KD])
        sin_t = sb("sin_t", [P, NT, ROPE_HALF])
        cos_t = sb("cos_t", [P, NT, ROPE_HALF])
        sinks = sb("sinks", [P, DEPTH, AH])
        minus_sinks = sb("minus_sinks", [P, DEPTH, AH])
        ident_r = sb("ident_r", [P, P], F32R)
        amask_r = sb("amask_r", [P, 2 * P], F32R)
        warm = sb("warm", [P, 1])
        a_ss = sb("a_ss", [P, NT, QK])
        a_max = sb("a_max", [P, 2, 2])
        a_negmax = sb("a_negmax", [P, 2, AH])
        a_sink = sb("a_sink", [P, 2, AH])
        a_den = sb("a_den", [P, 2, AH])
        assert place[0] <= 229344, place[0]
        y_h = sb("y_h", [P, KD, T], F32, at=h_lo_at)

        def unit(name, shape, first):
            return sb(name, shape, F32, at=region + first * UNIT)

        x_rows = unit("x_rows", [P, NT, D], 0)
        col_rows = unit("col_rows", [P, DEPTH, P], 8)
        rope_tmp = unit("rope_tmp", [P, 4, NT, ROPE_HALF], 9)
        pos_i = sb("pos_i", [P, NT], I32, at=region + 10 * UNIT)
        pos_f = unit("pos_f", [P, NT], 11)
        lb_tmp = sb("lb_tmp", [P, 4 + DEPTH, HH], F32, at=region + 11 * UNIT + 64)
        amask = sb("amask", [P, 2 * P], F32, at=region + 11 * UNIT + 512)
        ada_first = unit("ada_first", [P, KD, 2 * D], 12)
        ada_sum = sb("ada_sum", [P, 2 * D], F32, at=ada_at)
        q_t = unit("q_t", [P, HH, T], 0)
        f_t = unit("f_t", [P, HH, T], 4)
        k_t = unit("k_t", [P, HH, T], 8)
        v_n = unit("v_n", [P, HH, NT, P], 12)
        g_t = unit("g_t", [P, HH, T], 16)
        aqk = unit("aqk", [P, NT, QK, AD], 20)
        a_v = unit("a_v", [P, NT, KVH, AD], 25)
        suf = unit("suf", [P, HH, T], 26)
        kq = unit("kq", [P, 2, HH, T], 30)
        att = unit("att", [P, HH, T], 38)
        evac = unit("evac", [P, 2, T], 42)
        state = unit("state", [P, HH, NT, P], 0)
        key_n = unit("key_n", [P, HH, NT, P], 26)
        o_n = unit("o_n", [P, HH, T], 4)
        o_sq = unit("o_sq", [P, HH, T], 8)
        o_mix = sb("o_mix", [P, 2, T], F32, at=tmp_at + 4 * UNIT)
        aq_t = sb("aq_t", [P, 4, T], F32, at=ada_at)
        ak_t = sb("ak_t", [P, T], F32, at=ada_at + 4 * UNIT)
        probs = sb("probs", [P, 2, 2, 2 * P], F32, at=tmp_at)
        pt = sb("pt", [P, 2, 4, P], F32, at=tmp_at + 2 * UNIT)
        a_out = unit("a_out", [P, NT, AH * AD], 20)
        a_sq = sb("a_sq", [P, QK, AD], F32, at=tmp_at)
        a_rot = sb("a_rot", [P, 4, NT * QK * ROPE_HALF], F32, at=tmp_at + 2 * UNIT)
        y_r = unit("y_r", [P, KD, T], 0)

        bank = [ctx.enter_context(nc.psum_tensor(f"bank{i}", [P, T], F32)) for i in range(8)]

        ident = const[:, K_IDENT:K_IDENT + P]
        per_d, per_h = const[:, K_PER_D:K_PER_D + 1], const[:, K_PER_H:K_PER_H + 1]
        eps = const[:, K_EPS:K_EPS + 1]
        one = const[:, K_ONE:K_ONE + 1]

        def sem(name):
            return ctx.enter_context(nc.semaphore(name))

        setup_in = sem("setup_in")
        setup_pe = sem("setup_pe")
        setup_cols = sem("setup_cols")
        setup_step = sem("setup_step")
        setup_act = sem("setup_act")
        angles = sem("angles")
        raw_in = [sem("raw_in0"), sem("raw_in1")]
        hi_ready = sem("hi_ready")
        lo_ready = sem("lo_ready")
        panel_used = sem("panel_used")
        x_in = sem("x_in")
        lmask_in = sem("lmask_in")
        first_in = [sem(f"first_in{k}") for k in range(KD)]
        first_step = sem("first_step")
        ada_in = [sem(f"ada_in{i}") for i in range(ADA_RING)]
        ada_step = sem("ada_step")
        ada_cols = sem("ada_cols")
        mod_ready = sem("mod_ready")
        silu_done = sem("silu_done")
        hid_done = sem("hid_done")
        hid_hi_done = sem("hid_hi_done")
        hid_lo_done = sem("hid_lo_done")
        setup_x = sem("setup_x")
        x_done = sem("x_done")
        sq_done = sem("sq_done")
        sum_done = sem("sum_done")
        sum_zero = sem("sum_zero")
        ms_done = sem("ms_done")
        root_done = sem("root_done")
        inv_done = sem("inv_done")
        rstd_done = sem("rstd_done")
        xn_done = sem("xn_done")
        y_done = sem("y_done")
        h_hi_done = sem("h_hi_done")
        h_lo_done = sem("h_lo_done")
        gate_col_done = sem("gate_col_done")
        cols_done = sem("cols_done")
        in_read = sem("in_read")
        turn_done = sem("turn_done")
        turn_read = sem("turn_read")
        gates_ready = sem("gates_ready")
        att_done = sem("att_done")
        att_read = sem("att_read")
        kq_ready = sem("kq_ready")
        key_done = sem("key_done")
        key_read = sem("key_read")
        upd_done = sem("upd_done")
        state_done = sem("state_done")
        o_done = sem("o_done")
        osq_done = sem("osq_done")
        oms_done = sem("oms_done")
        oroot_done = sem("oroot_done")
        oinv_done = sem("oinv_done")
        orstd_done = sem("orstd_done")
        aroot_done = sem("aroot_done")
        omix_done = sem("omix_done")
        mix_hi = sem("mix_hi")
        mix_lo = sem("mix_lo")
        asq_done = sem("asq_done")
        rot_done = sem("rot_done")
        at_done = sem("at_done")
        at_read = sem("at_read")
        score_done = sem("score_done")
        max_done = sem("max_done")
        exp_done = sem("exp_done")
        sink_arg = sem("sink_arg")
        sink_exp = sem("sink_exp")
        pt_done = sem("pt_done")
        pt_read = sem("pt_read")
        pv_done = sem("pv_done")
        anorm_done = sem("anorm_done")
        back_done = sem("back_done")
        amix_hi = sem("amix_hi")
        amix_lo = sem("amix_lo")
        passed = sem("passed")
        step = sem("step")
        row_in = sem("row_in")
        out_pe = sem("out_pe")
        out_sb = sem("out_sb")
        stored = sem("stored")

        STARTS = [(lo_ready, 2), (panel_used, 2), (ada_step, ADA_RING), (silu_done, 2), (hid_done, 2), (x_done, 2),
                  (sum_done, 2), (h_lo_done, 2), (in_read, 2), (turn_done, 2), (turn_read, 1), (att_read, 2),
                  (rot_done, 1), (exp_done, 2), (pt_done, 2), (pt_read, 1), (pv_done, 2),
                  (anorm_done, 1)]

        def X(l, stage, d):
            return KD + l * 3 * KD + stage * KD + d

        def A(l, u):
            return l * ADA_UNITS + ADA_FIRST[u[0]] + u[1]

        def A_COL(u):
            return (ADA_EARLY * KD, ADA_EARLY * KD + ADA_ITERATIONS[0] * KD // 2, 0)[u[0]] + u[1] * (KD // 2)

        def A_LAYER(l, u):
            return DEPTH - 1 if u[0] == 2 else l

        def M(l, v):
            return l * ADA_UNITS + 1 + (0 if v < ADA_EARLY else 2 * (v + 1 - ADA_EARLY))

        def N_COLS_DONE(l, n):
            return l * 3 + n + 1

        def A_UNIT(u):
            n, pair, g = u // 4, u % 4 // 2, u % 2
            return n, 4 * g + 2 * pair, g

        N_SETUP = 2 + DEPTH * 7 + 2
        UNITS = HH * (LEVELS + 1)
        STEPS = 55

        O_BANK = (4, 6)

        w_gu = {P_GU1: (a["ffn1_w_gate"], a["ffn1_w_up"]), P_GU2: (a["ffn2_w_gate"], a["ffn2_w_up"])}
        w_dn = {P_DN1: a["ffn1_w_down"], P_DN2: a["ffn2_w_down"]}

        block = ctx.enter_context(nc.Block())

        @block.sync
        def _(sp):
            def load_in(dst, src):
                sp.dma_start(dst, src).then_inc(setup_in, 16)

            for l in range(DEPTH):
                load_in(col_rows[C_C:C_C + KD, l, :], a["c"][0].rearrange("(r p) -> r p", p=P))
                for at, src, n in ((C_ADAB, a["ada_b"], N_MOD * KD), (C_NORM, a["norm_ffn1"], KD),
                                   (C_NORM + KD, a["norm_mix"], KD), (C_NORM + 2 * KD, a["norm_ffn2"], KD),
                                   (C_LB, a["lb_logits"], HH), (C_HNORM, a["hgrn_norm"], 1)):
                    load_in(col_rows[at:at + n, l, :], src[l].rearrange("(r p) -> r p", p=P))
            load_in(const[:], a["const"])
            load_in(amask[:], a["amask"])
            sp.dma_start(pos_i[:], a["positions"][0].rearrange("(n p) -> p n", p=P), allow_slow_non_contiguous=True)\
              .then_inc(setup_in, 16)
            load_in(sinks[:].rearrange("p l h -> p (l h)"),
                    a["sinks"].rearrange("(o l) h -> o (l h)", o=1).to_broadcast([P, DEPTH * AH]))
            sp.dma_start(x_rows[:], a["x"][0].rearrange("(n p) d -> p n d", p=P)).then_inc(x_in, 16)
            for k in range(KD):
                sp.dma_start(ada_first[:, k, :], a["ada_w"][0, k * P:(k + 1) * P, 0:2 * D]).then_inc(first_in[k], 16)
            sp.dma_start(lmask[:], a["lmask"].rearrange("p (v t) -> p v t", v=LEVELS)).then_inc(lmask_in, 16)

            def load_panel(l, n, kind, i, slot):
                sp.wait_ge(lo_ready, l * PANELS + n + 1)
                if kind in w_gu:
                    src = w_gu[kind][slot % 2][bass.ds(l, 1), :, bass.ds(i * P, P)]
                    k = KD
                elif kind in w_dn:
                    d, half = i
                    src = w_dn[kind][bass.ds(l, 1), half * HALF * P:(half + 1) * HALF * P, bass.ds(d * P, P)]
                    k = HALF
                else:
                    src = (a["w_in"] if kind == P_IN else a["w_out"])[bass.ds(l, 1), :, bass.ds(i * P, P)]
                    k = KD
                dst = raw[:, slot % 2, 0:k * P].rearrange("p (k c) -> p k c", c=P)
                sp.dma_start(dst, src.rearrange("a (k p) c -> p (a k) c", p=P)).then_inc(raw_in[slot % 2], 16)

            def load_ada(l, u, s):
                sp.wait_ge(ada_step, A(l, u) * KD + s + 1)
                src = a["ada_w"][bass.ds(A_LAYER(l, u), 1), s * P:(s + 1) * P, bass.ds(A_COL(u) * P, T)]
                sp.dma_start(ada_raw[:, s % ADA_RING, :], src.rearrange("a p c -> p (a c)"))\
                  .then_inc(ada_in[s % ADA_RING], 16)

            def gate_up_loads(l, ffn, i, ada=None, last=False):
                base = (P_GU1, P_GU2)[ffn]
                for q in range(4):
                    if last and q >= 2:
                        load_panel(l, base + GU + q - 2, base + GU, (0, q % 2), q)
                    else:
                        load_panel(l, base + 4 * i + q + 2, base, 2 * i + (q + 2) // 2, q)
                    if ada is not None:
                        for s in range(*ADA_SHARE[q]):
                            load_ada(l, ada, s)

            def down_loads(l, ffn, i, last=False):
                base = (P_DN1, P_DN2)[ffn]
                for q in range(4):
                    if last and q >= 2:
                        if ffn == 0:
                            load_panel(l, P_IN + q - 2, P_IN, IN_ORDER[q - 2], q)
                    else:
                        load_panel(l, base + 4 * i + q + 2, base, (2 * i + (q + 2) // 2, q % 2), q)
                    if ffn == 0:
                        for s in range(*ADA_SHARE[q]):
                            load_ada(l, (1, i), s)

            def ffn_loads(l, ffn):
                phase = 2 * ffn
                n_ada = ADA_ITERATIONS[phase]
                with sp.Fori(0, n_ada) as i:
                    gate_up_loads(l, ffn, i, (phase, i))
                if n_ada < FT // 2 - 1:
                    with sp.Fori(n_ada, FT // 2 - 1) as i:
                        gate_up_loads(l, ffn, i)
                gate_up_loads(l, ffn, FT // 2 - 1, last=True)
                with sp.Fori(0, KD // 2 - 1) as i:
                    down_loads(l, ffn, i)
                down_loads(l, ffn, KD // 2 - 1, last=True)

            with sp.Fori(0, DEPTH) as l:
                sp.wait_ge(rot_done, l + 1)
                sp.dma_start(qkw[:, 0:AH, :], a["q_norm"][bass.ds(l, 1)].unsqueeze(1).to_broadcast([P, AH, AD]))\
                  .then_inc(row_in, 16)
                sp.dma_start(qkw[:, AH:QK, :], a["k_norm"][bass.ds(l, 1)].unsqueeze(1).to_broadcast([P, KVH, AD]))\
                  .then_inc(row_in, 16)
                for q in range(2):
                    load_panel(l, P_GU1 + q, P_GU1, 0, q)
                ffn_loads(l, 0)
                for i in range(2, IN_TILES):
                    load_panel(l, P_IN + i, P_IN, IN_ORDER[i], i)
                with sp.Fori(0, KD // 2) as i:
                    for q in range(2):
                        load_panel(l, P_OUT + 2 * i + q, P_OUT, 2 * i + q, q)
                for q in range(2):
                    load_panel(l, P_GU2 + q, P_GU2, 0, q)
                sp.wait_ge(score_done, (l + 1) * A_UNITS)
                sp.sem_inc(passed, 1)
                ffn_loads(l, 1)

            sp.wait_ge(out_sb, KD)
            sp.dma_start(out[0].rearrange("(n p) d -> p n d", p=P), x_rows[:]).then_inc(stored, 16)
            sp.wait_ge(stored, 16)

        @block.scalar
        def _(act):
            def split_hi(l, n, k, slot):
                act.wait_ge(raw_in[slot % 2], l * (PANELS // 2 * 16) + (n // 2 + 1) * 16 if isinstance(n, int)
                            else l * (PANELS // 2 * 16) + n * 8 + (16 - 8 * (slot % 2)))
                act.wait_ge(panel_used, l * PANELS + n + 1)
                nc.scalar.activation(w_hi[:, slot % 2, 0:k * P], raw[:, slot % 2, 0:k * P], ACT.Copy)\
                    .then_inc(hi_ready, 1)

            def square_tile(l, stage, d, slot):
                act.wait_ge(x_done, X(l, stage, d) + 3)
                act.wait_ge(sum_done, X(l, stage, d) + 1)
                nc.scalar.activation(sq[:, slot % 2, :], x[:, bass.ds(d, 1), :].rearrange("p a t -> p (a t)"), ACT.Square)\
                    .then_inc(sq_done, 1)

            def warm_root():
                nc.scalar.activation(warm[:], eps, ACT.Sqrt)

            act.wait_ge(setup_cols, DEPTH)
            nc.scalar.activation(cact[:], cols[:, 0, C_C:C_C + KD], ACT.Silu).then_inc(setup_act, 1)
            nc.scalar.activation(ident_r[:], ident, ACT.Copy)
            nc.scalar.activation(amask_r[:], amask[:], ACT.Copy).then_inc(setup_act, 1)
            act.wait_ge(angles, 1)
            nc.scalar.activation(lb_tmp[:, 4:4 + DEPTH], lb_tmp[:, 4:4 + DEPTH], ACT.Exp).then_inc(setup_act, 1)
            act.wait_ge(angles, 2)
            nc.scalar.activation(sin_t[:], rope_tmp[:, 0], ACT.Sin).then_inc(setup_act, 1)
            nc.scalar.activation(cos_t[:], rope_tmp[:, 0], ACT.Sin, scale=0.5).then_inc(setup_act, 1)
            for d in range(KD):
                square_tile(0, -1, d, d)

            def norm(l, n):
                vec = (0, 3, 6)[n]
                act.wait_ge(ms_done, l * 3 + n + 1)
                nc.scalar.activation(root[:], bank[6][:, 0:NT], ACT.Sqrt, bias=eps).then_inc(root_done, 1)
                for k in range(KD):
                    act.wait_ge(xn_done, l * (3 * KD) + n * KD + k + 1)
                    nc.scalar.activation(h_hi[:, k, :], sil[:, k % 2, :], ACT.Identity,
                                         bias=mod[:, vec * KD + k:vec * KD + k + 1]).then_inc(h_hi_done, 1)

            def silu_tile(l, ffn, f, slot):
                at = l * (2 * FT) + ffn * FT + f
                act.wait_ge(panel_used, l * PANELS + (P_GU1, P_GU2)[ffn] + 2 * f + 3)
                act.wait_ge(hid_done, at + 1)
                nc.scalar.activation(sil[:, slot, :], bank[2 * slot][:], ACT.Silu).then_inc(silu_done, 1)

            def hidden_hi(l, ffn, f, slot):
                act.wait_ge(hid_done, l * (2 * FT) + ffn * FT + f + 3)
                nc.scalar.activation(hid_hi[:, bass.ds(f, 1), :].rearrange("p a t -> p (a t)"), hidf[:, slot, :], ACT.Copy)\
                    .then_inc(hid_hi_done, 1)

            def gate_up(l, ffn, i, last=False):
                base = (P_GU1, P_GU2)[ffn]
                for q in range(4):
                    split_hi(l, base + 4 * i + q + 2, HALF if last and q >= 2 else KD, q)
                    if q % 2 == 0:
                        silu_tile(l, ffn, 2 * i + q // 2, q // 2)
                    else:
                        hidden_hi(l, ffn, 2 * i + q // 2, q // 2)

            def down(l, ffn, i, after):
                base = (P_DN1, P_DN2)[ffn]
                for q in range(4):
                    if q == 3 and after != HALF:
                        warm_root()
                        square_tile(l, 2 * ffn, 2 * i + 1, 1)
                    if q < 2 or after:
                        split_hi(l, base + 4 * i + q + 2, HALF if q < 2 else after, q)
                    if q == 1 or q == 3 and after == HALF:
                        square_tile(l, 2 * ffn, 2 * i + q // 2, q // 2)

            def ffn_phase(l, ffn):
                norm(l, 2 * ffn)
                with act.Fori(0, FT // 2 - 1) as i:
                    gate_up(l, ffn, i)
                gate_up(l, ffn, FT // 2 - 1, last=True)
                with act.Fori(0, KD // 2 - 1) as i:
                    down(l, ffn, i, HALF)
                down(l, ffn, KD // 2 - 1, (KD, 0)[ffn])

            def mixers(l):
                def split_(i):
                    split_hi(l, P_IN + i + 2, KD, i)

                def read(i):
                    kind, c = KINDS[IN_ORDER[i]], IN_ORDER[i] % 4
                    act.wait_ge(panel_used, l * PANELS + P_IN + i + 3)
                    src = bank[i % 2][:]
                    if kind == K_F:
                        nc.scalar.activation(f_t[:, c, :], src, ACT.Sigmoid)
                        nc.scalar.activation(k_t[:, c, :], src, ACT.Sigmoid, scale=-1.0).then_inc(in_read, 1)
                    elif kind == K_Q:
                        nc.scalar.activation(q_t[:, c, :], src, ACT.Copy, scale=HD ** -0.5).then_inc(in_read, 1)
                    elif kind == K_G:
                        nc.scalar.activation(g_t[:, c, :], src, ACT.Silu if c == HH - 1 else ACT.Copy).then_inc(in_read, 1)
                    else:
                        act.wait_ge(turn_done, l * TURNS + TURN_OF[i] + 1)
                        nc.scalar.activation(evac[:, TURN_OF[i] % 2, :], src, ACT.Copy).then_inc(in_read, 1)

                def turn(i):
                    kind, c, e = KINDS[IN_ORDER[i]], IN_ORDER[i] % 4, TURN_OF[i]
                    act.wait_ge(turn_done, l * TURNS + e + 3)
                    src = bank[5][:].rearrange("p (c t) -> p c t", t=P)
                    if kind == K_V:
                        dst = v_n[:, c]
                    elif kind == K_AV:
                        dst = a_v[:].rearrange("p n g d -> p n (g d)")
                    elif kind == K_AK:
                        dst = aqk[:, :, AH:QK, :].rearrange("p n g d -> p n (g d)")
                    else:
                        at = 2 * (2 * c % 4) + 2 * c // 4
                        dst, src = aqk[:, :, at:at + 3:2, :], src.rearrange("p n (e d) -> p n e d", d=AD)
                    nc.scalar.activation(dst, src, ACT.Copy).then_inc(turn_read, 1)

                def key(h):
                    act.wait_ge(key_done, l * HH + h + 1)
                    nc.scalar.activation(key_n[:, h, 0:NT - 1, :],
                                         bank[6 + h % 2][:, 0:(NT - 1) * P].rearrange("p (c d) -> p c d", d=P),
                                         ACT.Copy).then_inc(key_read, 1)

                def hout(h):
                    act.wait_ge(o_done, l * HH + h + 1)
                    nc.scalar.activation(o_n[:, h, :], bank[6 + h % 2][:], ACT.Copy)
                    nc.scalar.activation(o_sq[:, h, :], bank[6 + h % 2][:], ACT.Square).then_inc(osq_done, 1)

                def gates(_):
                    act.wait_ge(oms_done, l + 1)
                    nc.scalar.activation(o_root[:], bank[0][:, 0:HH * NT], ACT.Sqrt, bias=eps).then_inc(oroot_done, 1)
                    act.wait_ge(in_read, (l + 1) * IN_TILES + 1)
                    nc.scalar.activation(g_t[:, 0:HH - 1, :], g_t[:, 0:HH - 1, :], ACT.Silu)

                def hnorm(h):
                    act.wait_ge(omix_done, l * HH + h + 1)
                    act.wait_ge(panel_used, l * PANELS + P_OUT + 2)
                    nc.scalar.activation(h_hi[:, h, :], o_mix[:, h % 2, :], ACT.Copy).then_inc(mix_hi, 1)

                def asq(n):
                    act.wait_ge(turn_read, l * TURNS + 6)
                    act.wait_ge(rot_done, l + 1)
                    if n:
                        act.wait_ge(asq_done, l * NT + n)
                    for j in range(QK):
                        ins = nc.scalar.activation(a_sq[:, j, :], aqk[:, n, j, :], ACT.Square, accum_out=a_ss[:, n, j:j + 1])
                    ins.then_inc(asq_done, 1)

                def aroot(_):
                    act.wait_ge(asq_done, (l + 1) * NT)
                    nc.scalar.activation(a_ss[:], a_ss[:], ACT.Sqrt, bias=eps, scale=1.0 / AD).then_inc(aroot_done, 1)

                def flip(j):
                    act.wait_ge(at_done, l * 5 + j + 1)
                    dst, mul = (aq_t[:, j, :], AD ** -0.5) if j < 4 else (ak_t[:], 1.0)
                    nc.scalar.activation(dst, bank[2 + j % 2][:], ACT.Copy, scale=mul).then_inc(at_read, 1)

                def score_(u):
                    n, head, _ = A_UNIT(u)
                    lo = 0 if n else P
                    act.wait_ge(max_done, l * A_UNITS + u + 1)
                    act.wait_ge(pt_done, l * A_UNITS + u + 1)
                    for e in range(2):
                        ins = nc.scalar.activation(probs[:, u % 2, e, lo:], bank[2 + u % 2][:, e * 2 * P + lo:(e + 1) * 2 * P],
                                                   ACT.Exp, bias=a_negmax[:, n % 2, head + e:head + e + 1],
                                                   accum_out=a_den[:, n % 2, head + e:head + e + 1])
                    ins.then_inc(exp_done, 1)

                def sink(n):
                    act.wait_ge(sink_arg, l * NT + n + 1)
                    nc.scalar.activation(a_sink[:, n % 2, :], a_sink[:, n % 2, :], ACT.Exp).then_inc(sink_exp, 1)

                def prob(u):
                    n, _, _ = A_UNIT(u)
                    act.wait_ge(pt_done, l * A_UNITS + u + 3)
                    act.wait_ge(pv_done, l * A_UNITS + u + 1)
                    src, dst = bank[5][:].rearrange("p (a q) -> p a q", q=P), pt[:, u % 2]
                    if n == 0:
                        src, dst = src[:, 1::2], dst[:, 1::2]
                    nc.scalar.activation(dst, src, ACT.Copy).then_inc(pt_read, 1)

                def back(j):
                    act.wait_ge(back_done, l * 4 + j + 1)
                    act.wait_ge(panel_used, l * PANELS + P_OUT + 2)
                    nc.scalar.activation(h_hi[:, HH + j, :], bank[2 + j % 2][:], ACT.Copy).then_inc(amix_hi, 1)

                do = dict(split=split_, read=read, turn=turn, key=key, hout=hout, gates=gates, hnorm=hnorm, asq=asq, aroot=aroot,
                          flip=flip, score=score_, sink=sink, prob=prob, back=back)
                for what, n in MIX_STEPS:
                    if what in do:
                        do[what](n)

            with act.Fori(0, DEPTH) as l:
                for n in range(2):
                    split_hi(l, n, KD, n)
                ffn_phase(l, 0)
                norm(l, 1)
                mixers(l)
                with act.Fori(0, KD // 2 - 1) as i:
                    for q in range(2):
                        split_hi(l, P_OUT + 2 * i + q + 2, KD, q)
                        square_tile(l, 1, 2 * i + q, q)
                split_hi(l, P_OUT + KD, KD, 0)
                square_tile(l, 1, KD - 2, 0)
                warm_root()
                square_tile(l, 1, KD - 1, 1)
                split_hi(l, P_OUT + KD + 1, KD, 1)
                ffn_phase(l, 1)

            for d in range(KD):
                act.wait_ge(out_pe, d + 1)
                nc.scalar.activation(x_rows[:, :, d * P:(d + 1) * P], bank[d][:].rearrange("p (n c) -> p n c", c=P),
                                     ACT.Copy).then_inc(out_sb, 1)

        @block.tensor
        def _(pe):
            def product(dst, wslot, k, act_hi, act_lo, k0=0, first=True, last=True, ready=None, part=None):
                lo_k, hi_k = part or (0, k)
                for kt in range(lo_k, hi_k):
                    hi = w_hi[:, wslot, kt * P:(kt + 1) * P]
                    lo = w_lo[:, wslot, kt * P:(kt + 1) * P]
                    if ready is not None:
                        ready(kt)
                    nc.tensor.matmul(dst, hi, act_hi[:, k0 + kt, :], start=first and kt == 0, stop=False)
                    nc.tensor.matmul(dst, hi, act_lo[:, k0 + kt, :], start=False, stop=False)
                    mm = nc.tensor.matmul(dst, lo, act_hi[:, k0 + kt, :], start=False, stop=last and kt == k - 1)
                if hi_k == k:
                    mm.then_inc(panel_used, 1)

            def product_pair(dsts, ready):
                for kt in range(KD):
                    ready(kt)
                    for n in range(2):
                        hi = w_hi[:, n, kt * P:(kt + 1) * P]
                        lo = w_lo[:, n, kt * P:(kt + 1) * P]
                        nc.tensor.matmul(dsts[n], hi, h_hi[:, kt, :], start=kt == 0, stop=False)
                        nc.tensor.matmul(dsts[n], hi, h_lo[:, kt, :], start=False, stop=False)
                        mm = nc.tensor.matmul(dsts[n], lo, h_hi[:, kt, :], start=False, stop=kt == KD - 1)
                        if kt == KD - 1:
                            mm.then_inc(panel_used, 1)

            pe.wait_ge(setup_in, N_SETUP * 16)
            for l in range(DEPTH):
                nc.tensor.transpose(bank[l][:, 0:N_COLS], col_rows[0:N_COLS, l, :], ident[0:N_COLS, 0:N_COLS])\
                    .then_inc(setup_pe, 1)
            pe.wait_ge(x_in, 16)
            for d in range(KD):
                pe.wait_ge(x_done, d + 1)
                for n in range(NT):
                    mm = nc.tensor.transpose(bank[4 + d % 2][:, n * P:(n + 1) * P], x_rows[:, n, d * P:(d + 1) * P], ident)
                mm.then_inc(setup_x, 1)

            pe.wait_ge(first_step, KD)
            for m in range(2 * KD):
                mm = nc.tensor.matmul(bank[7][:, m:m + 1], ada_sum[:, m * P:(m + 1) * P], one, start=True, stop=True)
            mm.then_inc(ada_cols, 1)

            def ada_columns(l, u):
                pe.wait_ge(ada_step, A(l, u) * KD + KD + ADA_RING)
                for m in range(KD // 2):
                    mm = nc.tensor.matmul(bank[7][:, m:m + 1], ada_acc[:, m * P:(m + 1) * P], one, start=True, stop=True)
                mm.then_inc(ada_cols, 1)

            def norm(l, n):
                pe.wait_ge(sum_done, X(l, n - 1, 0) + KD + 2)
                for c in range(NT):
                    mm = nc.tensor.matmul(bank[6][:, c:c + 1], ssum[:, c * P:(c + 1) * P], per_d, start=True, stop=True)
                mm.then_inc(ms_done, 1)
                pe.wait_ge(inv_done, l * 3 + n + 1)
                for c in range(NT):
                    mm = nc.tensor.matmul(bank[6][:, c * P:(c + 1) * P], inv[:, c:c + 1].to_broadcast([P, P]), ident,
                                          start=True, stop=True)
                mm.then_inc(rstd_done, 1)

            def gate_up(l, ffn, i, ada=None, first=False):
                base = (P_GU1, P_GU2)[ffn]
                for q in range(4):
                    f = 2 * i + q // 2
                    pe.wait_ge(lo_ready, l * PANELS + base + 4 * i + q + 3)
                    pe.wait_ge(hid_done if q % 2 else silu_done, l * (2 * FT) + ffn * FT + f + 1)
                    if not first or q >= 2:
                        product(bank[q][:], q % 2, KD, h_hi, h_lo)
                    elif q == 1:
                        product_pair([bank[0][:], bank[1][:]],
                                     lambda kt: pe.wait_ge(h_lo_done, l * (3 * KD) + 2 * ffn * KD + kt + 3))
                if ada is not None:
                    ada_columns(l, ada)

            def down(l, ffn, i, first):
                base = (P_DN1, P_DN2)[ffn]
                for q in range(4):
                    d = 2 * i + q // 2
                    pe.wait_ge(lo_ready, l * PANELS + base + 4 * i + q + 3)
                    if q % 2 == 0:
                        pe.wait_ge(x_done, X(l, 2 * ffn, d) + 1)
                    ready = None
                    if first and q < 2:
                        def ready(kt, q=q):
                            pe.wait_ge(hid_lo_done, l * (2 * FT) + ffn * FT + q * HALF + kt + 1)
                    product(bank[4 + q // 2][:], q % 2, HALF, hid_hi, hid_lo, k0=(q % 2) * HALF, first=q % 2 == 0,
                            last=q % 2 == 1, ready=ready)
                if ffn == 0:
                    ada_columns(l, (1, i))

            def ffn_phase(l, ffn):
                norm(l, 2 * ffn)
                phase = 2 * ffn
                n_ada = ADA_ITERATIONS[phase]
                gate_up(l, ffn, 0, (phase, 0), first=True)
                with pe.Fori(1, n_ada) as i:
                    gate_up(l, ffn, i, (phase, i))
                with pe.Fori(n_ada, FT // 2) as i:
                    gate_up(l, ffn, i)
                down(l, ffn, 0, True)
                with pe.Fori(1, KD // 2) as i:
                    down(l, ffn, i, False)

            def out_product(l, i, q, ready=None, part=None):
                pe.wait_ge(lo_ready, l * PANELS + P_OUT + 2 * i + q + 3)
                pe.wait_ge(x_done, X(l, 1, 2 * i + q) + 1)
                product(bank[4 + q][:], q, KD, h_hi, h_lo, ready=ready, part=part)

            def mixers(l):
                def prod(at):
                    i, part = at
                    if i == 0:
                        return
                    if i == 1:
                        if part == 0:
                            pe.wait_ge(lo_ready, l * PANELS + P_IN + 4)
                            pe.wait_ge(in_read, l * IN_TILES + 2)
                            product_pair([bank[0][:], bank[1][:]],
                                         lambda kt: pe.wait_ge(h_lo_done, l * (3 * KD) + KD + kt + 3))
                        return
                    if part == 0:
                        pe.wait_ge(lo_ready, l * PANELS + P_IN + i + 3)
                        pe.wait_ge(in_read, l * IN_TILES + i + 1)
                    product(bank[i % 2][:], i % 2, KD, h_hi, h_lo, part=(part * KD // 2, (part + 1) * KD // 2))

                def turn(i):
                    e = TURN_OF[i]
                    pe.wait_ge(in_read, l * IN_TILES + i + 3)
                    pe.wait_ge(turn_read, l * TURNS + e + 1)
                    for n in range(NT):
                        mm = nc.tensor.transpose(bank[5][:, n * P:(n + 1) * P], evac[:, e % 2, n * P:(n + 1) * P], ident)
                    mm.then_inc(turn_done, 1)

                def units(first, half, left, right):
                    for h in (2 * half, 2 * half + 1):
                        u = first + h
                        pe.wait_ge(att_read, l * UNITS + u + 1)
                        for c in range(NT):
                            cut = slice(c * P, (c + 1) * P)
                            mm = nc.tensor.matmul(bank[6 + u % 2][:, cut], left(h)[:, cut], right(h)[:, cut],
                                                  start=True, stop=True)
                        mm.then_inc(att_done, 1)

                def diag(half):
                    pe.wait_ge(gates_ready, l + 1)
                    pe.wait_ge(in_read, l * IN_TILES + 8 + 2)
                    units(0, half, lambda h: k_t[:, h, :], lambda h: q_t[:, h, :])

                def level(at):
                    v, half = at
                    pe.wait_ge(kq_ready, l * (LEVELS + 2) + v + 1)
                    units(HH * (v + 1), half, lambda h: kq[:, v % 2, h, :], lambda h: kq[:, v % 2, h, :])

                def key(h):
                    pe.wait_ge(kq_ready, l * (LEVELS + 2) + LEVELS + 1)
                    if h < 2:
                        pe.wait_ge(att_read, (l + 1) * UNITS + 2)
                    else:
                        pe.wait_ge(key_read, l * HH + h - 1)
                    for c in range(NT - 1):
                        mm = nc.tensor.transpose(bank[6 + h % 2][:, c * P:(c + 1) * P], kq[:, 1, h, c * P:(c + 1) * P], ident)
                    mm.then_inc(key_done, 1)

                def update(h):
                    pe.wait_ge(turn_read, l * TURNS + TURN_OF[IN_ORDER.index(8 + h)] + 2)
                    pe.wait_ge(key_read, l * HH + max(h, 2 + h % 2) + 1)
                    if h >= 2:
                        pe.wait_ge(state_done, l * HH + h - 1)
                    for c in range(NT - 1):
                        mm = nc.tensor.matmul(bank[6 + h % 2][:, c * P:(c + 1) * P], key_n[:, h, c, :],
                                              v_n[:, h, c, :], start=True, stop=True)
                    mm.then_inc(upd_done, 1)

                def hout(h):
                    pe.wait_ge(kq_ready, (l + 1) * (LEVELS + 2))
                    pe.wait_ge(state_done, l * HH + max(h, 2 + h % 2) + 1)
                    if h >= 2:
                        pe.wait_ge(osq_done, l * HH + h - 1)
                    for c in range(NT):
                        cut = slice(c * P, (c + 1) * P)
                        mm = nc.tensor.matmul(bank[6 + h % 2][:, cut], v_n[:, h, c, :], att[:, h, cut], start=True, stop=c == 0)
                        if c:
                            mm = nc.tensor.matmul(bank[6 + h % 2][:, cut], state[:, h, c - 1, :], kq[:, 0, h, cut],
                                                  start=False, stop=True)
                    mm.then_inc(o_done, 1)

                def hms(_):
                    pe.wait_ge(osq_done, (l + 1) * HH)
                    pe.wait_ge(in_read, (l + 1) * IN_TILES - 1 + 2)
                    for h in range(HH):
                        for c in range(NT):
                            mm = nc.tensor.matmul(bank[0][:, h * NT + c:h * NT + c + 1], o_sq[:, h, c * P:(c + 1) * P], per_h,
                                                  start=True, stop=True)
                    mm.then_inc(oms_done, 1)

                def hnorm(h):
                    pe.wait_ge(oinv_done, l + 1)
                    pe.wait_ge(in_read, (l + 1) * IN_TILES + 2)
                    if h >= 2:
                        pe.wait_ge(omix_done, l * HH + h - 1)
                    for c in range(NT):
                        mm = nc.tensor.matmul(bank[h % 2][:, c * P:(c + 1) * P],
                                              o_inv[:, h * NT + c:h * NT + c + 1].to_broadcast([P, P]), ident,
                                              start=True, stop=True)
                    mm.then_inc(orstd_done, 1)

                def flip(j):
                    pe.wait_ge(rot_done, l + 2)
                    if j >= 2:
                        pe.wait_ge(at_read, l * 5 + j - 1)
                    for n in range(NT):
                        mm = nc.tensor.transpose(bank[2 + j % 2][:, n * P:(n + 1) * P],
                                                 aqk[:, n, 2 * j:2 * j + 2, :].rearrange("p a d -> p (a d)"), ident)
                    mm.then_inc(at_done, 1)

                def score_(u):
                    n, head, g = A_UNIT(u)
                    lo = 0 if n else P
                    if u == 0:
                        pe.wait_ge(at_read, l * 5 + 5)
                    pe.wait_ge(exp_done, l * A_UNITS + u + 1)
                    dst = bank[2 + u % 2][:].rearrange("p (e k) -> p e k", e=2)
                    for e in range(2):
                        nc.tensor.matmul(dst[:, e, lo:], aq_t[AD * g:AD * (g + 1), (head + e) % 4, n * P:(n + 1) * P],
                                         ak_t[AD * g:AD * (g + 1), (n - 1) * P + lo:(n + 1) * P],
                                         start=True, stop=False, skip_group_check=True)
                        mm = nc.tensor.matmul(dst[:, e, lo:], ident_r[:], amask_r[:, lo:], start=False, stop=True,
                                              skip_group_check=True)
                    mm.then_inc(score_done, 1)

                def prob(u):
                    n, _, _ = A_UNIT(u)
                    pe.wait_ge(exp_done, l * A_UNITS + u + 3)
                    pe.wait_ge(pt_read, l * A_UNITS + u + 1)
                    if u == 0:
                        pe.wait_ge(turn_read, (l + 1) * TURNS + 1)
                    for e in range(2):
                        for b in range(0 if n else 1, 2):
                            mm = nc.tensor.transpose(bank[5][:, (2 * e + b) * P:(2 * e + b + 1) * P],
                                                     probs[:, u % 2, e, b * P:(b + 1) * P], ident)
                    mm.then_inc(pt_done, 1)

                def weigh(u):
                    n, head, g = A_UNIT(u)
                    pe.wait_ge(pt_read, l * A_UNITS + u + 2)
                    if u == 4:
                        pe.wait_ge(osq_done, l * HH + 3)
                    elif u > 4 and u % 4 == 0:
                        pe.wait_ge(anorm_done, l * NT + n)
                    for e in range(2):
                        for b in range(0 if n else 1, 2):
                            mm = nc.tensor.matmul(bank[O_BANK[n % 2]][:, (head + e) * AD:(head + e + 1) * AD],
                                                  pt[:, u % 2, 2 * e + b, :], a_v[:, n - 1 + b, g, :],
                                                  start=b == 0 or n == 0, stop=b == 1, skip_group_check=True)
                    mm.then_inc(pv_done, 1)

                def back(j):
                    pe.wait_ge(anorm_done, (l + 1) * NT + 1)
                    if j >= 2:
                        pe.wait_ge(amix_lo, l * 4 + j - 1)
                    else:
                        pe.wait_ge(exp_done, (l + 1) * A_UNITS + 2)
                    for n in range(NT):
                        mm = nc.tensor.transpose(bank[2 + j % 2][:, n * P:(n + 1) * P], a_out[:, n, j * P:(j + 1) * P], ident)
                    mm.then_inc(back_done, 1)

                def out(part):
                    if part == 0:
                        pe.wait_ge(anorm_done, l * NT + 4)
                    out_product(l, 0, 0, lambda kt: pe.wait_ge(mix_lo, l * HH + kt + 1) if kt < HH
                                else pe.wait_ge(amix_lo, l * 4 + kt - HH + 1), (part * KD // 2, (part + 1) * KD // 2))

                do = dict(out=out, prod=prod, turn=turn, diag=diag, level=level, key=key, update=update, hout=hout, hms=hms,
                          hnorm=hnorm, flip=flip, score=score_, prob=prob, weigh=weigh, back=back)
                for what, n in MIX_STEPS:
                    if what in do:
                        do[what](n)

            with pe.Fori(0, DEPTH) as l:
                ffn_phase(l, 0)
                norm(l, 1)
                mixers(l)
                out_product(l, 0, 1)
                with pe.Fori(1, KD // 2) as i:
                    for q in range(2):
                        out_product(l, i, q)
                ffn_phase(l, 1)

            pe.wait_ge(x_done, X(DEPTH - 1, 2, KD - 1) + 3)
            for d in range(KD):
                for n in range(NT):
                    mm = nc.tensor.transpose(bank[d][:, n * P:(n + 1) * P], x[:, d, n * P:(n + 1) * P], ident)
                mm.then_inc(out_pe, 1)

        @block.vector
        def _(dve):
            tt, ts, stt = nc.vector.tensor_tensor, nc.vector.tensor_scalar, nc.vector.scalar_tensor_tensor
            for signal, start in STARTS:
                dve.sem_inc(signal, start)

            def add_squares(l, stage, d, slot):
                at = X(l, stage, d)
                dve.wait_ge(sq_done, at + 1)
                dve.wait_ge(sum_done, at + 2)
                tt(ssum[:], ssum[:], sq[:, slot, :], ALU.add).then_inc(sum_done, 1)

            def scale_column(l, n):
                dve.wait_ge(mod_ready, M(l, 3 * n + 1))
                stt(scale_col[:], mod[:, (3 * n + 1) * KD:(3 * n + 2) * KD], 1.0,
                    cols[:, bass.ds(l, 1), C_NORM + n * KD:C_NORM + (n + 1) * KD].rearrange("p a k -> p (a k)"),
                    ALU.add, ALU.mult).then_inc(cols_done, 1)
                dve.wait_ge(cols_done, N_COLS_DONE(l, n))
                dve.sem_inc(passed, 1)

            def scale_x(l, stage, d):
                dve.wait_ge(x_done, X(l, stage, d) + 3)
                y = y_r if stage == 1 else y_h
                ts(y[:, bass.ds(d, 1), :].rearrange("p a t -> p (a t)"), x[:, bass.ds(d, 1), :].rearrange("p a t -> p (a t)"),
                   scale_col[:, bass.ds(d, 1)], None, ALU.mult).then_inc(y_done, 1)

            done = [0]

            def link(ins):
                done[0] += 1
                ins.then_inc(setup_step, 1)
                dve.wait_ge(setup_step, done[0])

            nc.vector.memset(ssum[:], 0.0).then_inc(sum_zero, 1)
            dve.wait_ge(sum_zero, 1)
            dve.wait_ge(setup_in, N_SETUP * 16)
            for l in range(DEPTH):
                dve.wait_ge(setup_pe, l + 1)
                nc.vector.tensor_copy(cols[:, l, :], bank[l][:, 0:N_COLS]).then_inc(setup_cols, 1)
            dve.wait_ge(setup_cols, DEPTH)
            logit = lambda l: cols[:, l, C_LB:C_LB + HH]
            top, total, run = lb_tmp[:, 0], lb_tmp[:, 1], lb_tmp[:, 2]
            prob_l = lambda l: lb_tmp[:, 4 + l]
            link(nc.vector.tensor_copy(top, logit(0)))
            for l in range(1, DEPTH):
                link(tt(top, top, logit(l), ALU.max))
            for l in range(DEPTH):
                link(tt(prob_l(l), logit(l), top, ALU.subtract))
            dve.sem_inc(angles, 1)
            dve.wait_ge(setup_act, 3)
            for l in range(DEPTH):
                link(nc.vector.tensor_copy(total, prob_l(0)) if l == 0 else tt(total, total, prob_l(l), ALU.add))
            link(nc.vector.reciprocal(total, total))
            for l in range(DEPTH):
                link(tt(prob_l(l), prob_l(l), total, ALU.mult))
                link(nc.vector.tensor_copy(run, prob_l(0)) if l == 0 else tt(run, run, prob_l(l), ALU.add))
                link(tt(lower[:, l, :], run, prob_l(0), ALU.subtract))
                link(ts(one_minus_lower[:, l, :], lower[:, l, :], -1.0, 1.0, ALU.mult, ALU.add))

            ang, turns_, part = rope_tmp[:, 0], rope_tmp[:, 1], rope_tmp[:, 2]
            link(nc.vector.tensor_copy(pos_f[:], pos_i[:]))
            link(tt(ang, pos_f[:].unsqueeze(2).to_broadcast([P, NT, ROPE_HALF]),
                    const[:, K_INVF:K_INVF + ROPE_HALF].unsqueeze(1).to_broadcast([P, NT, ROPE_HALF]), ALU.mult))
            link(ts(turns_, ang, 1.0 / TWO_PI, MAGIC, ALU.mult, ALU.add))
            link(ts(turns_, turns_, MAGIC, None, ALU.subtract))
            for c in TWO_PI_PARTS:
                link(stt(ang, turns_, -c, ang, ALU.mult, ALU.add))
            ts(ang, ang, PI_BELOW, -PI_BELOW, ALU.min, ALU.max).then_inc(angles, 1)
            dve.wait_ge(setup_act, 5)
            link(tt(part, cos_t[:], cos_t[:], ALU.mult))
            link(ts(cos_t[:], part, -2.0, 1.0, ALU.mult, ALU.add))

            nc.vector.tensor_scalar(minus_sinks[:], sinks[:], -1.0, None, ALU.mult)
            for d in range(KD):
                dve.wait_ge(setup_x, d + 1)
                nc.vector.tensor_copy(x[:, d, :], bank[4 + d % 2][:]).then_inc(x_done, 1)
                if d:
                    add_squares(0, -1, d - 1, (d - 1) % 2)
            add_squares(0, -1, KD - 1, (KD - 1) % 2)

            dve.wait_ge(setup_act, 1)
            for k in range(KD):
                dve.wait_ge(first_in[k], 16)
                if k == 0:
                    ins = ts(ada_sum[:], ada_first[:, k, :], cact[:, k:k + 1], None, ALU.mult)
                else:
                    dve.wait_ge(first_step, k)
                    ins = stt(ada_sum[:], ada_first[:, k, :], cact[:, k:k + 1], ada_sum[:], ALU.mult, ALU.add)
                ins.then_inc(first_step, 1)
            dve.wait_ge(ada_cols, 1)
            tt(mod[:, 0:2 * KD], bank[7][:, 0:2 * KD], cols[:, 0, 0:2 * KD], ALU.add).then_inc(mod_ready, 1)
            dve.wait_ge(lmask_in, 16)
            scale_column(0, 0)
            for d in range(KD):
                scale_x(0, -1, d)

            def ada_piece(l, u, k):
                dve.wait_ge(ada_in[k % ADA_RING], A(l, u) * (KD // ADA_RING * 16) + (k // ADA_RING + 1) * 16)
                if k == 0:
                    ins = ts(ada_acc[:], ada_raw[:, k % ADA_RING, :], cact[:, k:k + 1], None, ALU.mult)
                else:
                    dve.wait_ge(ada_step, A(l, u) * KD + k + ADA_RING)
                    ins = stt(ada_acc[:], ada_raw[:, k % ADA_RING, :], cact[:, k:k + 1], ada_acc[:], ALU.mult, ALU.add)
                ins.then_inc(ada_step, 1)

            def ada_store(l, u):
                dve.wait_ge(ada_cols, A(l, u) + 2)
                tt(mod[:, bass.ds(A_COL(u), KD // 2)], bank[7][:, 0:KD // 2],
                   cols[:, bass.ds(A_LAYER(l, u), 1), bass.ds(A_COL(u), KD // 2)].rearrange("p a k -> p (a k)"), ALU.add)\
                    .then_inc(mod_ready, 1)

            def split_lo(l, n, k, slot):
                dve.wait_ge(hi_ready, l * PANELS + n + 1)
                tt(w_lo[:, slot % 2, 0:k * P], raw[:, slot % 2, 0:k * P], w_hi[:, slot % 2, 0:k * P], ALU.subtract)\
                    .then_inc(lo_ready, 1)

            def norm(l, n):
                dve.wait_ge(root_done, l * 3 + n + 1)
                nc.vector.reciprocal(inv[:], root[:]).then_inc(inv_done, 1)
                dve.wait_ge(rstd_done, l * 3 + n + 1)
                dve.wait_ge(y_done, l * (3 * KD) + (n + 1) * KD)
                y = y_r if n == 2 else y_h

                def low(k):
                    vec = 3 * n * KD + k
                    dve.wait_ge(h_hi_done, l * (3 * KD) + n * KD + k + 1)
                    stt(h_lo[:, k, :], sil[:, k % 2, :], mod[:, vec:vec + 1], h_hi[:, k, :], ALU.add, ALU.subtract)\
                        .then_inc(h_lo_done, 1)

                for k in range(KD):
                    if k >= 2:
                        low(k - 2)
                        dve.wait_ge(h_lo_done, l * (3 * KD) + n * KD + k + 1)
                    tt(sil[:, k % 2, :], bank[6][:], y[:, k, :], ALU.mult).then_inc(xn_done, 1)
                low(KD - 2)
                low(KD - 1)
                nc.vector.memset(ssum[:], 0.0).then_inc(sum_zero, 1)

            def stage_columns(l, stage):
                dve.wait_ge(mod_ready, M(l, 3 * stage + 2))
                ts(gate_col[:], mod[:, (3 * stage + 2) * KD:(3 * stage + 3) * KD], 1.0 if stage == 1 else 0.5, None, ALU.mult)\
                    .then_inc(gate_col_done, 1)
                dve.wait_ge(gate_col_done, l * 3 + stage + 1)
                dve.sem_inc(passed, 1)
                if stage < 2:
                    scale_column(l, stage + 1)
                else:
                    stt(scale_col[:], mod[:, KD:2 * KD], 1.0, cols[:, DEPTH - 1, C_NORM:C_NORM + KD], ALU.add, ALU.mult)\
                        .then_inc(cols_done, 1)
                    dve.wait_ge(cols_done, N_COLS_DONE(l, 3))
                    dve.sem_inc(passed, 1)

            def update_x(l, stage, d, slot, panels):
                dve.wait_ge(panel_used, panels + 2)
                xd = x[:, bass.ds(d, 1), :].rearrange("p a t -> p (a t)")
                stt(xd, bank[4 + slot][:], gate_col[:, bass.ds(d, 1)], xd, ALU.mult, ALU.add).then_inc(x_done, 1)

            def hidden(l, ffn, f, slot):
                dve.wait_ge(panel_used, l * PANELS + (P_GU1, P_GU2)[ffn] + 2 * f + 4)
                dve.wait_ge(silu_done, l * (2 * FT) + ffn * FT + f + 3)
                tt(hidf[:, slot, :], bank[2 * slot + 1][:], sil[:, slot, :], ALU.mult).then_inc(hid_done, 1)

            def hidden_lo(l, ffn, f, slot):
                dve.wait_ge(hid_hi_done, l * (2 * FT) + ffn * FT + f + 1)
                at = (slice(None), bass.ds(f, 1), slice(None))
                tt(hid_lo[at].rearrange("p a t -> p (a t)"), hidf[:, slot, :], hid_hi[at].rearrange("p a t -> p (a t)"),
                   ALU.subtract).then_inc(hid_lo_done, 1)

            def gate_up(l, ffn, i, last=False, ada=None):
                base = (P_GU1, P_GU2)[ffn]
                for q in range(4):
                    f, slot = 2 * i + q // 2, q // 2
                    if q % 2:
                        hidden(l, ffn, f, slot)
                    split_lo(l, base + 4 * i + q + 2, HALF if last and q >= 2 else KD, q)
                    if q % 2:
                        hidden_lo(l, ffn, f, slot)
                    if ada is not None:
                        for s in range(*ADA_SHARE[q]):
                            ada_piece(l, ada, s)
                if ada is not None:
                    ada_store(l, ada)

            def down(l, ffn, i, after):
                base = (P_DN1, P_DN2)[ffn]
                for q in range(4):
                    d = 2 * i + q // 2
                    hurry = q == 3 and after != HALF
                    if q % 2:
                        update_x(l, 2 * ffn, d, q // 2, l * PANELS + base + 4 * i + q + 1)
                    if hurry:
                        scale_x(l, 2 * ffn, d)
                        add_squares(l, 2 * ffn, d, q // 2)
                    if q < 2 or after:
                        split_lo(l, base + 4 * i + q + 2, HALF if q < 2 else after, q)
                    if q % 2 and not hurry:
                        scale_x(l, 2 * ffn, d)
                        add_squares(l, 2 * ffn, d, q // 2)
                    if ffn == 0:
                        for s in range(*ADA_SHARE[q]):
                            ada_piece(l, (1, i), s)
                if ffn == 0:
                    ada_store(l, (1, i))

            def ffn_phase(l, ffn):
                norm(l, 2 * ffn)
                phase = 2 * ffn
                n_ada = ADA_ITERATIONS[phase]
                with dve.Fori(0, n_ada) as i:
                    gate_up(l, ffn, i, ada=(phase, i))
                if n_ada < FT // 2 - 1:
                    with dve.Fori(n_ada, FT // 2 - 1) as i:
                        gate_up(l, ffn, i)
                gate_up(l, ffn, FT // 2 - 1, last=True)
                stage_columns(l, 2 * ffn)
                with dve.Fori(0, KD // 2 - 1) as i:
                    down(l, ffn, i, HALF)
                down(l, ffn, KD // 2 - 1, (KD, 0)[ffn])

            def mixers(l):
                count = [0]

                def own(ins):
                    count[0] += 1
                    ins.then_inc(step, 1)
                    dve.wait_ge(step, l * STEPS + count[0])

                def chunks(ap):
                    return ap.rearrange("p (c t) -> p c t", t=P)

                def split_(i):
                    split_lo(l, P_IN + i + 2, KD, i)

                def read(i):
                    kind, c = KINDS[IN_ORDER[i]], IN_ORDER[i] % 4
                    if kind == K_F:
                        dve.wait_ge(in_read, l * IN_TILES + i + 3)
                        ts(f_t[:, c, :], f_t[:, c, :], one_minus_lower[:, bass.ds(l, 1), c], lower[:, bass.ds(l, 1), c],
                           ALU.mult, ALU.add)
                        ins = ts(k_t[:, c, :], k_t[:, c, :], one_minus_lower[:, bass.ds(l, 1), c], None, ALU.mult)
                        if c == HH - 1:
                            ins.then_inc(gates_ready, 1)

                def ones(_):
                    own(nc.vector.memset(suf[:], 1.0))

                def diag(half):
                    for h in (2 * half, 2 * half + 1):
                        dve.wait_ge(att_done, l * UNITS + h + 1)
                        tt(chunks(att[:, h, :]), chunks(bank[6 + h % 2][:]), ident.unsqueeze(1).to_broadcast([P, NT, P]),
                           ALU.mult).then_inc(att_read, 1)

                def halves(ap, v):
                    return ap.rearrange("p h (b w s) -> p (h b) w s", w=2, s=1 << v)

                def operands(v):
                    return (halves(z, v) for z in (kq[:, v % 2], q_t[:], k_t[:], f_t[:], suf[:]))

                def build(v):
                    kq_v, q_v, k_v, p_v, s_v = operands(v)
                    if v == 0:
                        dve.wait_ge(gates_ready, l + 1)
                        dve.wait_ge(in_read, l * IN_TILES + 8 + 2)
                    tt(kq_v[:, :, 0], k_v[:, :, 0], s_v[:, :, 0], ALU.mult)
                    tt(kq_v[:, :, 1], q_v[:, :, 1], p_v[:, :, 1], ALU.mult).then_inc(kq_ready, 1)

                def extend(v):
                    _, _, _, p_v, s_v = operands(v)
                    b = 1 << v
                    shape = [P, HH * T // (2 * b), b]
                    own(tt(s_v[:, :, 0], s_v[:, :, 0], p_v[:, :, 1, b - 1:b].to_broadcast(shape), ALU.mult))
                    own(tt(p_v[:, :, 1], p_v[:, :, 1], p_v[:, :, 0, b - 1:b].to_broadcast(shape), ALU.mult))

                def level(at):
                    v, half = at
                    for h in (2 * half, 2 * half + 1):
                        u = HH * (v + 1) + h
                        dve.wait_ge(att_done, l * UNITS + u + 1)
                        dve.wait_ge(att_read, l * UNITS + u - HH + 3)
                        dve.sem_inc(passed, 1)
                        nc.vector.copy_predicated(chunks(att[:, h, :]), lmask[:, v].unsqueeze(1).to_broadcast([P, NT, P]),
                                                  chunks(bank[6 + u % 2][:])).then_inc(att_read, 1)

                def key_side(_):
                    tt(kq[:, 1], k_t[:], suf[:], ALU.mult).then_inc(kq_ready, 1)

                def query_side(_):
                    tt(kq[:, 0], q_t[:], f_t[:], ALU.mult).then_inc(kq_ready, 1)

                def update(h):
                    dve.wait_ge(kq_ready, (l + 1) * (LEVELS + 2))
                    dve.wait_ge(upd_done, l * HH + h + 1)
                    own(nc.vector.tensor_copy(state[:, h, 0, :], bank[6 + h % 2][:, 0:P]))
                    own(stt(state[:, h, 1, :], state[:, h, 0, :], f_t[:, h, 2 * P - 1:2 * P],
                            bank[6 + h % 2][:, P:2 * P], ALU.mult, ALU.add))
                    stt(state[:, h, 2, :], state[:, h, 1, :], f_t[:, h, 3 * P - 1:3 * P],
                        bank[6 + h % 2][:, 2 * P:3 * P], ALU.mult, ALU.add).then_inc(state_done, 1)

                def gates(_):
                    dve.wait_ge(oroot_done, l + 1)
                    nc.vector.reciprocal(o_inv[:], o_root[:]).then_inc(oinv_done, 1)

                def hlow(h):
                    dve.wait_ge(mix_hi, l * HH + h + 1)
                    tt(h_lo[:, h, :], o_mix[:, h % 2, :], h_hi[:, h, :], ALU.subtract).then_inc(mix_lo, 1)

                def hnorm(h):
                    dve.wait_ge(orstd_done, l * HH + h + 1)
                    own(tt(o_n[:, h, :], bank[h % 2][:], o_n[:, h, :], ALU.mult))
                    stt(o_mix[:, h % 2, :], o_n[:, h, :], cols[:, bass.ds(l, 1), C_HNORM],
                        g_t[:, h, :], ALU.mult, ALU.mult).then_inc(omix_done, 1)
                    if h:
                        hlow(h - 1)
                    if h == HH - 1:
                        hlow(h)

                def normalise(_):
                    dve.wait_ge(aroot_done, l + 1)
                    own(nc.vector.reciprocal(a_ss[:], a_ss[:]))
                    flat = aqk[:].rearrange("p n h d -> p (n h) d")
                    own(tt(flat, flat, a_ss[:].rearrange("p n h -> p (n h)").unsqueeze(2).to_broadcast([P, NT * QK, AD]),
                           ALU.mult))

                def weights(_):
                    dve.wait_ge(row_in, (l + 1) * 32)
                    flat = aqk[:].rearrange("p n h d -> p n (h d)")
                    own(tt(flat, flat, qkw[:].rearrange("p h d -> p (h d)").unsqueeze(1).to_broadcast([P, NT, QK * AD]),
                           ALU.mult))

                def rotate(_):
                    one_, two = aqk[:, :, :, 0:ROPE_HALF], aqk[:, :, :, ROPE_HALF:2 * ROPE_HALF]
                    shape = [P, NT, QK, ROPE_HALF]
                    cos_b, sin_b = (z[:].unsqueeze(2).to_broadcast(shape) for z in (cos_t, sin_t))
                    r = [a_rot[:, j].rearrange("p (n h d) -> p n h d", n=NT, h=QK) for j in range(4)]
                    tt(r[0], one_, cos_b, ALU.mult)
                    tt(r[1], two, sin_b, ALU.mult)
                    tt(r[2], two, cos_b, ALU.mult)
                    own(tt(r[3], one_, sin_b, ALU.mult))
                    tt(one_, r[0], r[1], ALU.subtract)
                    tt(two, r[2], r[3], ALU.add).then_inc(rot_done, 1)

                def score_(u):
                    n, head, _ = A_UNIT(u)
                    lo = 0 if n else P
                    dve.wait_ge(score_done, l * A_UNITS + u + 1)
                    own(nc.vector.tensor_reduce(a_max[:, u % 2, :], bank[2 + u % 2][:].rearrange("p (e k) -> p e k", e=2)[:, :, lo:],
                                                AX_X, ALU.max))
                    stt(a_negmax[:, n % 2, head:head + 2], a_max[:, u % 2, :], -1.0,
                        minus_sinks[:, bass.ds(l, 1), head:head + 2].rearrange("p a h -> p (a h)"), ALU.mult, ALU.min)\
                        .then_inc(max_done, 1)

                def sink(n):
                    dve.wait_ge(max_done, l * A_UNITS + 4 * n + 4)
                    tt(a_sink[:, n % 2, :], sinks[:, bass.ds(l, 1), :].rearrange("p a h -> p (a h)"), a_negmax[:, n % 2, :],
                       ALU.add).then_inc(sink_arg, 1)

                def anorm(n):
                    dve.wait_ge(sink_exp, l * NT + n + 1)
                    dve.wait_ge(exp_done, l * A_UNITS + 4 * n + 6)
                    own(tt(a_den[:, n % 2, :], a_den[:, n % 2, :], a_sink[:, n % 2, :], ALU.add))
                    own(nc.vector.reciprocal(a_den[:, n % 2, :], a_den[:, n % 2, :]))
                    dve.wait_ge(pv_done, l * A_UNITS + 4 * n + 6)
                    tt(a_out[:, n, :].rearrange("p (h d) -> p h d", d=AD), bank[O_BANK[n % 2]][:].rearrange("p (h d) -> p h d", d=AD),
                       a_den[:, n % 2, :].unsqueeze(2).to_broadcast([P, AH, AD]), ALU.mult).then_inc(anorm_done, 1)

                def back(j):
                    dve.wait_ge(amix_hi, l * 4 + j + 1)
                    tt(h_lo[:, HH + j, :], bank[2 + j % 2][:], h_hi[:, HH + j, :], ALU.subtract).then_inc(amix_lo, 1)

                do = dict(split=split_, read=read, ones=ones, diag=diag, build=build, extend=extend, level=level,
                          key_side=key_side, query_side=query_side, update=update, gates=gates,
                          hnorm=hnorm, normalise=normalise, weights=weights, rotate=rotate, score=score_,
                          sink=sink, anorm=anorm, back=back)
                for what, n in MIX_STEPS:
                    if what in do:
                        do[what](n)
                assert count[0] == STEPS, count[0]

            with dve.Fori(0, DEPTH) as l:
                for n in range(2):
                    split_lo(l, n, KD, n)
                ffn_phase(l, 0)
                norm(l, 1)
                mixers(l)
                stage_columns(l, 1)
                with dve.Fori(0, KD // 2 - 1) as i:
                    for q in range(2):
                        update_x(l, 1, 2 * i + q, q, l * PANELS + P_OUT + 2 * i + q + 1)
                        split_lo(l, P_OUT + 2 * i + q + 2, KD, q)
                        scale_x(l, 1, 2 * i + q)
                        add_squares(l, 1, 2 * i + q, q)
                update_x(l, 1, KD - 2, 0, l * PANELS + P_OUT + KD - 1)
                split_lo(l, P_OUT + KD, KD, 0)
                scale_x(l, 1, KD - 2)
                add_squares(l, 1, KD - 2, 0)
                update_x(l, 1, KD - 1, 1, l * PANELS + P_OUT + KD)
                scale_x(l, 1, KD - 1)
                add_squares(l, 1, KD - 1, 1)
                split_lo(l, P_OUT + KD + 1, KD, 1)
                ffn_phase(l, 1)


INPUTS = ["x", "c", "positions", "ada_w", "ada_b", "norm_ffn1", "ffn1_w_gate", "ffn1_w_up", "ffn1_w_down", "norm_mix",
          "w_in", "lb_logits", "hgrn_norm", "q_norm", "k_norm", "sinks", "w_out", "norm_ffn2", "ffn2_w_gate",
          "ffn2_w_up", "ffn2_w_down"]


def kernel(**inputs):
    import concourse.bacc as bacc
    from concourse.bass_utils import run_bass_kernel_spmd

    nc = bacc.Bacc("TRN2", target_bir_lowering=False, num_devices=1)
    arrays = {name: np.ascontiguousarray(inputs[name]) for name in INPUTS}
    arrays["const"], arrays["amask"], arrays["lmask"] = constants()
    aps = {name: nc.dram_tensor(name, v.shape, mybir.dt.from_np(v.dtype), kind="ExternalInput").ap()
           for name, v in arrays.items()}
    out = nc.dram_tensor("out", (1, T, D), F32, kind="ExternalOutput").ap()
    trunk_kernel(nc, aps, out)
    return run_bass_kernel_spmd(nc, [arrays], core_ids=[0]).results[0]["out"]
```

```python
from contextlib import ExitStack

import numpy as np

import concourse.bass as bass
from concourse import mybir

ALU = mybir.AluOpType
ACT = mybir.ActivationFunctionType
F32 = mybir.dt.float32
F32R = mybir.dt.float32r
I32 = mybir.dt.int32
AX_X = mybir.AxisListType.X

P = 128
DEPTH = 2
D = 1024
T = 512
KD = D // P
NT = T // P
F = 2816
FT = F // P
HH, HD = 4, 128
AH, KVH, AD = 8, 2, 64
QK = AH + KVH
ROPE_HALF = AD // 8
ROPE_THETA = 500000.0
N_MOD = 9
EPS = 1e-6
IN_TILES = 22
LEVELS = 7
NEG = -1e30
TWO_PI = float(2 * np.pi)
TWO_PI_PARTS = (6.28125, 4058 / 2.0 ** 21, 3.0199159795074593e-07)
PI_BELOW = 3.1415925
MAGIC = 1.5 * 2.0 ** 23

GU = 2 * FT
DN = 2 * KD
HALF = FT // 2
P_GU1, P_DN1 = 0, GU
P_IN = P_DN1 + DN
P_OUT = P_IN + IN_TILES
P_GU2 = P_OUT + KD
P_DN2 = P_GU2 + GU
PANELS = P_DN2 + DN
WIDE = HALF * P

C_ADAB, C_NORM = 0, N_MOD * KD
C_LB = C_NORM + 3 * KD
C_HNORM = C_LB + HH
C_C = C_HNORM + 1
N_COLS = C_C + KD

ADA_RING = 4
ADA_EARLY = 2
ADA_ITERATIONS = (10, 4, 4)
ADA_FIRST = (0, 10, 14)
ADA_UNITS = 18
assert ADA_UNITS == 2 * N_MOD and ADA_UNITS - ADA_FIRST[2] == 2 * ADA_EARLY
ADA_SHARE = ((0, 3), (3, 6), (6, 8), (8, 8))

IN_ORDER = [0, 1, 2, 3, 4, 5, 6, 7, 16, 17, 18, 19, 20, 21, 8, 9, 10, 11, 12, 13, 14, 15]
K_F, K_Q, K_V, K_G, K_AQ, K_AK, K_AV = "f", "q", "v", "g", "aq", "ak", "av"
KINDS = [K_Q] * 4 + [K_F] * 4 + [K_V] * 4 + [K_G] * 4 + [K_AQ] * 4 + [K_AK, K_AV]
TURNED = (K_V, K_AQ, K_AK, K_AV)
TURN_OF = {}
for _i, _c in enumerate(IN_ORDER):
    if KINDS[_c] in TURNED:
        TURN_OF[_i] = len(TURN_OF)
TURNS = len(TURN_OF)

A_UNITS = 4 * NT


def attention_at(u):
    steps = []
    if 0 <= u - 2 < A_UNITS:
        steps += [("weigh", u - 2)]
    if 0 <= u - 1 < A_UNITS:
        steps += [("prob", u - 1)]
    if u < A_UNITS:
        steps += [("score", u)]
        if u % 4 == 3:
            steps += [("sink", u // 4)]
    if u >= 2 and (u - 2) % 4 == 3:
        steps += [("anorm", (u - 2) // 4)]
    return steps


MIX_STEPS = []
for _i in range(8):
    MIX_STEPS += [("prod", (_i, 0, KD)), ("split", _i), ("read", _i)]
    if _i == 4:
        MIX_STEPS += [("ones", 0)]
MIX_STEPS += [("prod", (8, 0, 6)), ("diag", 0), ("build", 0), ("prod", (8, 6, KD)), ("diag", 1), ("extend", 0)]
for _v in range(LEVELS):
    _i = 9 + _v
    MIX_STEPS += [("read", _i - 1), ("level", (_v, 0)), ("split", _i - 1), ("prod", (_i, 0, 4))]
    MIX_STEPS += [("build", _v + 1)] if _v + 1 < LEVELS else [("key_side", 0)]
    MIX_STEPS += [("turn", _i - 1), ("level", (_v, 1))]
    if _v + 1 < LEVELS:
        MIX_STEPS += [("extend", _v + 1)]
    if _i == 13:
        MIX_STEPS += [("asq", 0)]
    if _i == 14:
        MIX_STEPS += [("asq", 1), ("asq", 2)]
    if _i == 15:
        MIX_STEPS += [("asq", 3), ("aroot", 0), ("normalise", 0)]
    MIX_STEPS += [("prod", (_i, 4, KD))]
MIX_STEPS += [("read", 15), ("split", 15), ("key", 0), ("key", 1), ("prod", (16, 0, 4)), ("turn", 15),
              ("weights", 0), ("rotate", 0), ("key", 2), ("key", 3), ("prod", (16, 4, KD))]
MIX_STEPS += [("read", 16), ("split", 16), ("prod", (17, 0, 4)), ("turn", 16), ("query_side", 0)]
MIX_STEPS += [("flip", _j) for _j in range(QK // 2)]
MIX_STEPS += [("prod", (17, 4, KD))] + attention_at(0) + [("update", 0), ("update", 1), ("update", 2)]
for _i in range(18, IN_TILES):
    _u = 4 * (_i - 18) + 1
    MIX_STEPS += [("read", _i - 1), ("split", _i - 1)]
    if _i == 18:
        MIX_STEPS += [("turn", 17), ("update", 3)]
    for _k in range(4):
        MIX_STEPS += [("prod", (_i, 2 * _k, KD - 1 if _i == IN_TILES - 1 and _k == 3 else 2 * _k + 2))]
        if _i < 20 and _k < 2:
            MIX_STEPS += [("hout", 2 * (_i - 18) + _k)]
        if _i == IN_TILES - 1 and _k == 0:
            MIX_STEPS += [("warm", ACT.Sqrt), ("hms", 0), ("gates", 0)]
        MIX_STEPS += attention_at(_u + _k)
        if _i == IN_TILES - 1 and _k:
            MIX_STEPS += [("hnorm", _k - 1)]
        if _i == IN_TILES - 1 and _k == 2:
            MIX_STEPS += [("warm", ACT.Silu)]
        if _i == IN_TILES - 1 and _k >= 2:
            MIX_STEPS += [("hmix", _k - 2)]
MIX_STEPS += [("prod", (IN_TILES - 1, KD - 1, KD)), ("hmix", 2), ("read", IN_TILES - 1), ("hnorm", HH - 1)]
MIX_STEPS += attention_at(A_UNITS + 1) + [("hmix", 3), ("out", 0)]
MIX_STEPS += [("back", 0), ("back", 1), ("split", IN_TILES - 1), ("back", 2), ("back", 3), ("out", 1)]

K_IDENT, K_INVF, K_ONE, K_PER_D, K_PER_H, K_EPS = 0, 128, 136, 137, 138, 139
K_COLS = 140


def constants():
    c = np.zeros((P, K_COLS), np.float32)
    c[:, K_IDENT:K_IDENT + P] = np.eye(P)
    q, k = np.arange(P)[:, None], np.arange(2 * P)[None, :] - P
    amask = np.where((q - k >= 0) & (q - k < P), 0.0, NEG).astype(np.float32)
    rope = np.arange(0, 2 * ROPE_HALF, 2, dtype=np.float32) / np.float32(2 * ROPE_HALF)
    c[:, K_INVF:K_INVF + ROPE_HALF] = np.float32(ROPE_THETA) ** (-rope)
    c[:, K_ONE], c[:, K_PER_D], c[:, K_PER_H], c[:, K_EPS] = 1.0, 1.0 / D, 1.0 / HD, EPS
    s, t = np.arange(P)[:, None], np.arange(P)[None, :]
    masks = [(((s ^ t) >> v) == 1) & (t > s) for v in range(LEVELS)]
    return c, amask, np.concatenate(masks, axis=1).astype(np.int32)


def trunk_kernel(nc, a, out):
    ctx = ExitStack()
    with ctx:
        place = [16512]

        def sb(name, shape, dt=F32, at=None):
            n = int(np.prod(shape[1:])) * 4
            off = place[0] if at is None else at
            if at is None:
                place[0] += (n + 31) // 32 * 32
            return nc.alloc_sbuf_tensor_at(name, shape, dt, offset=off)

        UNIT = T * 4
        x = sb("x", [P, KD, T])
        h_hi_at = place[0]
        h_hi = sb("h_hi", [P, KD, T], F32R)
        h_lo_at = place[0]
        h_lo = sb("h_lo", [P, KD, T], F32R)
        raw = sb("raw", [P, 2, WIDE])
        w_hi = sb("w_hi", [P, 2, WIDE], F32R)
        w_lo = sb("w_lo", [P, 2, WIDE], F32R)
        ada_at = place[0]
        ada_raw = sb("ada_raw", [P, ADA_RING, T])
        ada_acc = sb("ada_acc", [P, T])
        region = place[0]
        place[0] += 2 * FT * UNIT
        hid_hi = sb("hid_hi", [P, FT, T], F32R, at=region)
        hid_lo = sb("hid_lo", [P, FT, T], F32R, at=region + FT * UNIT)
        tmp_at = place[0]
        sil = sb("sil", [P, 2, T])
        hidf = sb("hidf", [P, 2, T])
        sq = sb("sq", [P, 2, T])
        root = sb("root", [P, NT])
        inv = sb("inv", [P, NT])
        o_root = sb("o_root", [P, HH * NT])
        o_inv = sb("o_inv", [P, HH * NT])
        ssum = sb("ssum", [P, T])
        const = sb("const", [P, K_COLS])
        lmask = sb("lmask", [P, LEVELS, P], I32)
        qkw = sb("qkw", [P, QK, AD])
        cols = sb("cols", [P, DEPTH, N_COLS])
        lower = sb("lower", [P, DEPTH, HH])
        one_minus_lower = sb("one_minus_lower", [P, DEPTH, HH])
        mod = sb("mod", [P, N_MOD * KD])
        scale_col = sb("scale_col", [P, KD])
        gate_col = sb("gate_col", [P, KD])
        cact = sb("cact", [P, KD])
        sin_t = sb("sin_t", [P, NT, ROPE_HALF])
        cos_t = sb("cos_t", [P, NT, ROPE_HALF])
        sinks = sb("sinks", [P, DEPTH, AH])
        minus_sinks = sb("minus_sinks", [P, DEPTH, AH])
        ident_r = sb("ident_r", [P, P], F32R)
        amask_r = sb("amask_r", [P, 2 * P], F32R)
        warm = sb("warm", [P, 1])
        a_ss = sb("a_ss", [P, NT, QK])
        a_max = sb("a_max", [P, 2, 2])
        a_negmax = sb("a_negmax", [P, 2, AH])
        a_sink = sb("a_sink", [P, 2, AH])
        a_den = sb("a_den", [P, 2, AH])
        assert place[0] <= 229344, place[0]
        y_h = sb("y_h", [P, KD, T], F32, at=h_lo_at)

        def unit(name, shape, first):
            return sb(name, shape, F32, at=region + first * UNIT)

        sq_first = sb("sq_first", [P, KD, T], F32, at=h_hi_at)
        x_rows = unit("x_rows", [P, NT, D], 0)
        col_rows = unit("col_rows", [P, DEPTH, P], 8)
        rope_tmp = unit("rope_tmp", [P, 4, NT, ROPE_HALF], 9)
        pos_i = sb("pos_i", [P, NT], I32, at=region + 10 * UNIT)
        pos_f = unit("pos_f", [P, NT], 11)
        lb_tmp = sb("lb_tmp", [P, 4 + DEPTH, HH], F32, at=region + 11 * UNIT + 64)
        amask = sb("amask", [P, 2 * P], F32, at=region + 11 * UNIT + 512)
        ada_first = unit("ada_first", [P, 2, KD, D], 12)
        ada_sum = sb("ada_sum", [P, 2, D], F32, at=ada_at)
        q_t = unit("q_t", [P, HH, T], 0)
        f_t = unit("f_t", [P, HH, T], 4)
        k_t = unit("k_t", [P, HH, T], 8)
        v_n = unit("v_n", [P, HH, NT, P], 12)
        g_t = unit("g_t", [P, HH, T], 16)
        aqk = unit("aqk", [P, NT, QK, AD], 20)
        a_v = unit("a_v", [P, NT, KVH, AD], 25)
        suf = unit("suf", [P, HH, T], 26)
        kq = unit("kq", [P, 2, HH, T], 30)
        att = unit("att", [P, HH, T], 38)
        evac = unit("evac", [P, 2, T], 42)
        state = unit("state", [P, HH, NT, P], 0)
        key_n = unit("key_n", [P, HH, NT, P], 26)
        o_n = unit("o_n", [P, HH, T], 4)
        o_sq = unit("o_sq", [P, HH, T], 8)
        o_mix = unit("o_mix", [P, HH, T], 8)
        aq_t = sb("aq_t", [P, 4, T], F32, at=ada_at)
        ak_t = sb("ak_t", [P, T], F32, at=ada_at + 4 * UNIT)
        xn = sb("xn", [P, 4, T], F32, at=tmp_at)
        probs = sb("probs", [P, 2, 2, 2 * P], F32, at=tmp_at)
        pt = sb("pt", [P, 2, 4, P], F32, at=tmp_at + 2 * UNIT)
        a_out = unit("a_out", [P, NT, AH * AD], 20)
        a_sq = sb("a_sq", [P, QK, AD], F32, at=tmp_at)
        a_rot = sb("a_rot", [P, 4, NT * QK * ROPE_HALF], F32, at=tmp_at + 2 * UNIT)
        y_r = unit("y_r", [P, KD, T], 0)

        bank = [ctx.enter_context(nc.psum_tensor(f"bank{i}", [P, T], F32)) for i in range(8)]

        ident = const[:, K_IDENT:K_IDENT + P]
        per_d, per_h = const[:, K_PER_D:K_PER_D + 1], const[:, K_PER_H:K_PER_H + 1]
        eps = const[:, K_EPS:K_EPS + 1]
        one = const[:, K_ONE:K_ONE + 1]

        def sem(name):
            return ctx.enter_context(nc.semaphore(name))

        setup_in = sem("setup_in")
        setup_pe = sem("setup_pe")
        setup_cols = sem("setup_cols")
        setup_step = sem("setup_step")
        setup_act = sem("setup_act")
        angles = sem("angles")
        raw_in = [sem("raw_in0"), sem("raw_in1")]
        hi_ready = sem("hi_ready")
        lo_ready = sem("lo_ready")
        panel_used = sem("panel_used")
        x_in = sem("x_in")
        lmask_in = sem("lmask_in")
        first_in = [[sem(f"first_in{v}_{k}") for k in range(KD)] for v in range(2)]
        first_step = sem("first_step")
        ada_in = [sem(f"ada_in{i}") for i in range(ADA_RING)]
        ada_step = sem("ada_step")
        ada_cols = sem("ada_cols")
        mod_ready = sem("mod_ready")
        silu_done = sem("silu_done")
        hid_done = sem("hid_done")
        hid_hi_done = sem("hid_hi_done")
        hid_lo_done = sem("hid_lo_done")
        setup_sum = sem("setup_sum")
        setup_x = sem("setup_x")
        x_done = sem("x_done")
        sq_done = sem("sq_done")
        sum_done = sem("sum_done")
        sum_zero = sem("sum_zero")
        ms_done = sem("ms_done")
        root_done = sem("root_done")
        inv_done = sem("inv_done")
        rstd_done = sem("rstd_done")
        xn_done = sem("xn_done")
        y_done = sem("y_done")
        h_hi_done = sem("h_hi_done")
        h_lo_done = sem("h_lo_done")
        gate_col_done = sem("gate_col_done")
        cols_done = sem("cols_done")
        in_read = sem("in_read")
        turn_done = sem("turn_done")
        turn_read = sem("turn_read")
        gates_ready = sem("gates_ready")
        att_done = sem("att_done")
        att_read = sem("att_read")
        kq_ready = sem("kq_ready")
        key_done = sem("key_done")
        key_read = sem("key_read")
        upd_done = sem("upd_done")
        state_done = sem("state_done")
        o_done = sem("o_done")
        osq_done = sem("osq_done")
        oms_done = sem("oms_done")
        oroot_done = sem("oroot_done")
        gates_done = sem("gates_done")
        oinv_done = sem("oinv_done")
        orstd_done = sem("orstd_done")
        aroot_done = sem("aroot_done")
        h_free = sem("h_free")
        omix_done = sem("omix_done")
        mix_hi = sem("mix_hi")
        mix_lo = sem("mix_lo")
        asq_done = sem("asq_done")
        rot_done = sem("rot_done")
        at_done = sem("at_done")
        at_read = sem("at_read")
        score_done = sem("score_done")
        max_done = sem("max_done")
        exp_done = sem("exp_done")
        sink_arg = sem("sink_arg")
        sink_exp = sem("sink_exp")
        pt_done = sem("pt_done")
        pt_read = sem("pt_read")
        pv_done = sem("pv_done")
        anorm_done = sem("anorm_done")
        back_done = sem("back_done")
        amix_hi = sem("amix_hi")
        amix_lo = sem("amix_lo")
        passed = sem("passed")
        step = sem("step")
        row_in = sem("row_in")
        out_pe = sem("out_pe")
        out_act = sem("out_act")
        out_dve = sem("out_dve")
        stored = sem("stored")

        STARTS = [(lo_ready, 2), (panel_used, 2), (ada_step, ADA_RING), (silu_done, 2), (hid_done, 2), (x_done, 2),
                  (sum_done, 2), (h_lo_done, 2), (in_read, 2), (turn_done, 2), (turn_read, 1), (att_read, 2),
                  (rot_done, 1), (exp_done, 2), (pt_done, 2), (pt_read, 1), (pv_done, 2),
                  (anorm_done, 1)]

        def X(l, stage, d):
            return KD + l * 3 * KD + stage * KD + d

        def A(l, u):
            return l * ADA_UNITS + ADA_FIRST[u[0]] + u[1]

        def A_COL(u):
            return (ADA_EARLY * KD, ADA_EARLY * KD + ADA_ITERATIONS[0] * KD // 2, 0)[u[0]] + u[1] * (KD // 2)

        def A_LAYER(l, u):
            return DEPTH - 1 if u[0] == 2 else l

        def M(l, v):
            return l * ADA_UNITS + 2 + (0 if v < ADA_EARLY else 2 * (v + 1 - ADA_EARLY))

        def N_COLS_DONE(l, n):
            return l * 3 + n + 1

        def A_UNIT(u):
            n, pair, g = u // 4, u % 4 // 2, u % 2
            return n, 4 * g + 2 * pair, g

        N_SETUP = 1 + 2 + 6 + 3
        UNITS = HH * (LEVELS + 1)
        STEPS = 55

        def T_BANK(i):
            return i % 4 if i < 8 else i % 2

        O_BANK = (4, 6)
        BUSY = (2, 1, 2, 3, 4)
        FIRST_BANK = (3, 7)
        R_BANK = (7, 0)

        w_gu = {P_GU1: (a["ffn1_w_gate"], a["ffn1_w_up"]), P_GU2: (a["ffn2_w_gate"], a["ffn2_w_up"])}
        w_dn = {P_DN1: a["ffn1_w_down"], P_DN2: a["ffn2_w_down"]}

        block = ctx.enter_context(nc.Block())

        @block.sync
        def _(sp):
            def load_in(dst, src):
                sp.dma_start(dst, src).then_inc(setup_in, 16)

            load_in(const[:], a["const"])
            sp.dma_start(x_rows[:], a["x"][0].rearrange("(n p) d -> p n d", p=P)).then_inc(x_in, 16)
            load_in(col_rows[C_C:C_C + KD, 0, :], a["c"][0].rearrange("(r p) -> r p", p=P))
            load_in(col_rows[C_C:C_C + KD, 1, :], a["c"][0].rearrange("(r p) -> r p", p=P))
            for at, src, n in ((C_ADAB, a["ada_b"], N_MOD * KD), (C_NORM, a["norm_ffn1"], KD),
                               (C_NORM + KD, a["norm_mix"], KD), (C_NORM + 2 * KD, a["norm_ffn2"], KD),
                               (C_LB, a["lb_logits"], HH), (C_HNORM, a["hgrn_norm"], 1)):
                load_in(col_rows[at:at + n, :, :], src.rearrange("l (r p) -> r l p", p=P))
            sp.dma_start(pos_i[:], a["positions"][0].rearrange("(n p) -> p n", p=P), allow_slow_non_contiguous=True)\
              .then_inc(setup_in, 16)
            load_in(sinks[:].rearrange("p l h -> p (l h)"),
                    a["sinks"].rearrange("(o l) h -> o (l h)", o=1).to_broadcast([P, DEPTH * AH]))
            load_in(amask[:], a["amask"])
            for v in (1, 0):
                for k in range(KD):
                    sp.dma_start(ada_first[:, v, k, :], a["ada_w"][0, k * P:(k + 1) * P, v * D:(v + 1) * D])\
                      .then_inc(first_in[v][k], 16)
            def load_panel(l, n, kind, i, slot, layer=None):
                sp.wait_ge(lo_ready, l * PANELS + n + 1)
                sp.sem_inc(passed, 1)
                if kind in w_gu:
                    src = w_gu[kind][slot % 2][bass.ds(l if layer is None else layer, 1), :, bass.ds(i * P, P)]
                    k = KD
                elif kind in w_dn:
                    d, half = i
                    src = w_dn[kind][bass.ds(l, 1), half * HALF * P:(half + 1) * HALF * P, bass.ds(d * P, P)]
                    k = HALF
                else:
                    src = (a["w_in"] if kind == P_IN else a["w_out"])[bass.ds(l, 1), :, bass.ds(i * P, P)]
                    k = KD
                dst = raw[:, slot % 2, 0:k * P].rearrange("p (k c) -> p k c", c=P)
                sp.dma_start(dst, src.rearrange("a (k p) c -> p (a k) c", p=P)).then_inc(raw_in[slot % 2], 16)

            def load_ada(l, u, s):
                sp.wait_ge(ada_step, A(l, u) * KD + s + 1)
                src = a["ada_w"][bass.ds(A_LAYER(l, u), 1), s * P:(s + 1) * P, bass.ds(A_COL(u) * P, T)]
                sp.dma_start(ada_raw[:, s % ADA_RING, :], src.rearrange("a p c -> p (a c)"))\
                  .then_inc(ada_in[s % ADA_RING], 16)

            def gate_up_loads(l, ffn, i, ada=None, last=False):
                base = (P_GU1, P_GU2)[ffn]
                for q in range(4):
                    if last and q >= 2:
                        load_panel(l, base + GU + q - 2, base + GU, (0, q % 2), q)
                    else:
                        load_panel(l, base + 4 * i + q + 2, base, 2 * i + (q + 2) // 2, q)
                    if ada is not None:
                        for s in range(*ADA_SHARE[q]):
                            load_ada(l, ada, s)

            def down_loads(l, ffn, i, last=False):
                base = (P_DN1, P_DN2)[ffn]
                for q in range(4):
                    if last and q >= 2:
                        if ffn == 0:
                            load_panel(l, P_IN + q - 2, P_IN, IN_ORDER[q - 2], q)
                        else:
                            load_panel(l, PANELS + q - 2, P_GU1, 0, q, layer=DEPTH - 1)
                    else:
                        load_panel(l, base + 4 * i + q + 2, base, (2 * i + (q + 2) // 2, q % 2), q)
                    if ffn == 0:
                        for s in range(*ADA_SHARE[q]):
                            load_ada(l, (1, i), s)

            def ffn_loads(l, ffn):
                phase = 2 * ffn
                n_ada = ADA_ITERATIONS[phase]
                with sp.Fori(0, n_ada) as i:
                    gate_up_loads(l, ffn, i, (phase, i))
                if n_ada < FT // 2 - 1:
                    with sp.Fori(n_ada, FT // 2 - 1) as i:
                        gate_up_loads(l, ffn, i)
                gate_up_loads(l, ffn, FT // 2 - 1, last=True)
                with sp.Fori(0, KD // 2 - 1) as i:
                    down_loads(l, ffn, i)
                down_loads(l, ffn, KD // 2 - 1, last=True)

            for q in range(2):
                load_panel(0, P_GU1 + q, P_GU1, 0, q)
            sp.dma_start(lmask[:], a["lmask"].rearrange("p (v t) -> p v t", v=LEVELS)).then_inc(lmask_in, 16)
            sp.wait_ge(mod_ready, 2)
            sp.sem_inc(passed, 1)
            with sp.Fori(0, DEPTH) as l:
                sp.wait_ge(rot_done, l + 1)
                sp.dma_start(qkw[:, 0:AH, :], a["q_norm"][bass.ds(l, 1)].unsqueeze(1).to_broadcast([P, AH, AD]))\
                  .then_inc(row_in, 16)
                sp.dma_start(qkw[:, AH:QK, :], a["k_norm"][bass.ds(l, 1)].unsqueeze(1).to_broadcast([P, KVH, AD]))\
                  .then_inc(row_in, 16)
                ffn_loads(l, 0)
                for i in range(2, IN_TILES):
                    load_panel(l, P_IN + i, P_IN, IN_ORDER[i], i)
                with sp.Fori(0, KD // 2) as i:
                    for q in range(2):
                        load_panel(l, P_OUT + 2 * i + q, P_OUT, 2 * i + q, q)
                for q in range(2):
                    load_panel(l, P_GU2 + q, P_GU2, 0, q)
                sp.wait_ge(score_done, (l + 1) * A_UNITS)
                sp.sem_inc(passed, 1)
                ffn_loads(l, 1)

            for j in range(KD // 2):
                sp.wait_ge(out_act, j + 1)
                sp.wait_ge(out_dve, j + 1)
                cut = slice(2 * j * P, (2 * j + 2) * P)
                sp.dma_start(out[0, :, cut].rearrange("(n p) d -> p n d", p=P), x_rows[:, :, cut]).then_inc(stored, 16)
            sp.wait_ge(stored, KD // 2 * 16)

        @block.scalar
        def _(act):
            def split_hi(l, n, k, slot):
                act.wait_ge(raw_in[slot % 2], l * (PANELS // 2 * 16) + (n // 2 + 1) * 16 if isinstance(n, int)
                            else l * (PANELS // 2 * 16) + n * 8 + (16 - 8 * (slot % 2)))
                act.wait_ge(panel_used, l * PANELS + n + 1)
                nc.scalar.activation(w_hi[:, slot % 2, 0:k * P], raw[:, slot % 2, 0:k * P], ACT.Copy)\
                    .then_inc(hi_ready, 1)

            def square_tile(l, stage, d, slot):
                act.wait_ge(x_done, X(l, stage, d) + 3)
                act.wait_ge(sum_done, X(l, stage, d) + 1)
                nc.scalar.activation(sq[:, slot % 2, :], x[:, bass.ds(d, 1), :].rearrange("p a t -> p (a t)"), ACT.Square)\
                    .then_inc(sq_done, 1)

            def warm_up(function):
                nc.scalar.activation(warm[:], eps, function)

            act.wait_ge(setup_cols, DEPTH)
            nc.scalar.activation(cact[:], cols[:, 0, C_C:C_C + KD], ACT.Silu).then_inc(setup_act, 1)
            for d in range(KD):
                act.wait_ge(setup_x, d + 1)
                nc.scalar.activation(x[:, d, :], bank[4 + d % 2][:], ACT.Copy).then_inc(x_done, 1)
                nc.scalar.activation(sq_first[:, d, :], bank[4 + d % 2][:], ACT.Square).then_inc(sq_done, 1)
            act.wait_ge(setup_sum, 1)
            nc.scalar.activation(ssum[:], bank[6][:], ACT.Copy).then_inc(sum_done, KD)
            nc.scalar.activation(ident_r[:], ident, ACT.Copy)
            nc.scalar.activation(amask_r[:], amask[:], ACT.Copy).then_inc(setup_act, 1)
            act.wait_ge(angles, 1)
            nc.scalar.activation(lb_tmp[:, 4:4 + DEPTH], lb_tmp[:, 4:4 + DEPTH], ACT.Exp).then_inc(setup_act, 1)
            act.wait_ge(angles, 2)
            nc.scalar.activation(sin_t[:], rope_tmp[:, 0], ACT.Sin).then_inc(setup_act, 1)
            nc.scalar.activation(cos_t[:], rope_tmp[:, 0], ACT.Sin, scale=0.5).then_inc(setup_act, 1)
            for n in range(2):
                split_hi(0, n, KD, n)

            def norm(l, n):
                vec = (0, 3, 6)[n]
                act.wait_ge(ms_done, l * 3 + n + 1)
                nc.scalar.activation(root[:], bank[6][:, 0:NT], ACT.Sqrt, bias=eps).then_inc(root_done, 1)
                for k in range(KD):
                    act.wait_ge(xn_done, l * (3 * KD) + n * KD + k + 1)
                    nc.scalar.activation(h_hi[:, k, :], xn[:, k % 4, :], ACT.Identity,
                                         bias=mod[:, vec * KD + k:vec * KD + k + 1]).then_inc(h_hi_done, 1)

            def silu_tile(l, ffn, f, slot):
                at = l * (2 * FT) + ffn * FT + f
                act.wait_ge(panel_used, l * PANELS + (P_GU1, P_GU2)[ffn] + 2 * f + 3)
                act.wait_ge(hid_done, at + 1)
                nc.scalar.activation(sil[:, slot, :], bank[2 * slot][:], ACT.Silu).then_inc(silu_done, 1)

            def hidden_hi(l, ffn, f, slot):
                act.wait_ge(hid_done, l * (2 * FT) + ffn * FT + f + 3)
                nc.scalar.activation(hid_hi[:, bass.ds(f, 1), :].rearrange("p a t -> p (a t)"), hidf[:, slot, :], ACT.Copy)\
                    .then_inc(hid_hi_done, 1)

            def gate_up(l, ffn, i, last=False):
                base = (P_GU1, P_GU2)[ffn]
                for q in range(4):
                    split_hi(l, base + 4 * i + q + 2, HALF if last and q >= 2 else KD, q)
                    if q % 2 == 0:
                        silu_tile(l, ffn, 2 * i + q // 2, q // 2)
                    else:
                        hidden_hi(l, ffn, 2 * i + q // 2, q // 2)

            def down(l, ffn, i, after):
                base = (P_DN1, P_DN2)[ffn]
                for q in range(4):
                    if q == 3 and after != HALF:
                        warm_up(ACT.Sqrt)
                        square_tile(l, 2 * ffn, 2 * i + 1, 1)
                    split_hi(l, base + 4 * i + q + 2, HALF if q < 2 else after, q)
                    if q == 1 or q == 3 and after == HALF:
                        square_tile(l, 2 * ffn, 2 * i + q // 2, q // 2)

            def ffn_phase(l, ffn):
                norm(l, 2 * ffn)
                with act.Fori(0, FT // 2 - 1) as i:
                    gate_up(l, ffn, i)
                gate_up(l, ffn, FT // 2 - 1, last=True)
                with act.Fori(0, KD // 2 - 1) as i:
                    down(l, ffn, i, HALF)
                down(l, ffn, KD // 2 - 1, KD)

            def mixers(l):
                def split_(i):
                    split_hi(l, P_IN + i + 2, KD, i)

                def read(i):
                    kind, c = KINDS[IN_ORDER[i]], IN_ORDER[i] % 4
                    act.wait_ge(panel_used, l * PANELS + P_IN + i + 3)
                    src = bank[T_BANK(i)][:]
                    if kind == K_F:
                        nc.scalar.activation(f_t[:, c, :], src, ACT.Sigmoid)
                        nc.scalar.activation(k_t[:, c, :], src, ACT.Sigmoid, scale=-1.0).then_inc(in_read, 1)
                    elif kind == K_Q:
                        nc.scalar.activation(q_t[:, c, :], src, ACT.Copy, scale=HD ** -0.5).then_inc(in_read, 1)
                    elif kind == K_G:
                        nc.scalar.activation(g_t[:, c, :], src, ACT.Silu if c == HH - 1 else ACT.Copy).then_inc(in_read, 1)
                    else:
                        act.wait_ge(turn_done, l * TURNS + TURN_OF[i] + 1)
                        nc.scalar.activation(evac[:, TURN_OF[i] % 2, :], src, ACT.Copy).then_inc(in_read, 1)

                def turn(i):
                    kind, c, e = KINDS[IN_ORDER[i]], IN_ORDER[i] % 4, TURN_OF[i]
                    act.wait_ge(turn_done, l * TURNS + e + 3)
                    src = bank[5][:].rearrange("p (c t) -> p c t", t=P)
                    if kind == K_V:
                        dst = v_n[:, c]
                    elif kind == K_AV:
                        dst = a_v[:].rearrange("p n g d -> p n (g d)")
                    elif kind == K_AK:
                        dst = aqk[:, :, AH:QK, :].rearrange("p n g d -> p n (g d)")
                    else:
                        at = 2 * (2 * c % 4) + 2 * c // 4
                        dst, src = aqk[:, :, at:at + 3:2, :], src.rearrange("p n (e d) -> p n e d", d=AD)
                    nc.scalar.activation(dst, src, ACT.Copy).then_inc(turn_read, 1)

                def key(h):
                    act.wait_ge(key_done, l * HH + h + 1)
                    nc.scalar.activation(key_n[:, h, 0:NT - 1, :],
                                         bank[6 + h % 2][:, 0:(NT - 1) * P].rearrange("p (c d) -> p c d", d=P),
                                         ACT.Copy).then_inc(key_read, 1)

                def hout(h):
                    act.wait_ge(o_done, l * HH + h + 1)
                    nc.scalar.activation(o_n[:, h, :], bank[6 + h % 2][:], ACT.Copy)
                    nc.scalar.activation(o_sq[:, h, :], bank[6 + h % 2][:], ACT.Square).then_inc(osq_done, 1)

                def gates(_):
                    act.wait_ge(oms_done, l + 1)
                    nc.scalar.activation(o_root[:], bank[0][:, 0:HH * NT], ACT.Sqrt, bias=eps).then_inc(oroot_done, 1)
                    act.wait_ge(in_read, (l + 1) * IN_TILES + 1)
                    nc.scalar.activation(g_t[:, 0:HH - 1, :], g_t[:, 0:HH - 1, :], ACT.Silu).then_inc(gates_done, 1)

                def hmix(h):
                    act.wait_ge(omix_done, l * HH + h + 1)
                    act.wait_ge(h_free, l * 2 + h // 2 + 1)
                    nc.scalar.activation(h_hi[:, h, :], o_mix[:, h, :], ACT.Copy).then_inc(mix_hi, 1)

                def asq(n):
                    act.wait_ge(turn_read, l * TURNS + 6)
                    act.wait_ge(rot_done, l + 1)
                    if n:
                        act.wait_ge(asq_done, l * NT + n)
                    for j in range(QK):
                        ins = nc.scalar.activation(a_sq[:, j, :], aqk[:, n, j, :], ACT.Square, accum_out=a_ss[:, n, j:j + 1])
                    ins.then_inc(asq_done, 1)

                def aroot(_):
                    act.wait_ge(asq_done, (l + 1) * NT)
                    nc.scalar.activation(a_ss[:], a_ss[:], ACT.Sqrt, bias=eps, scale=1.0 / AD).then_inc(aroot_done, 1)

                def flip(j):
                    act.wait_ge(at_done, l * 5 + j + 1)
                    dst, mul = (aq_t[:, j, :], AD ** -0.5) if j < 4 else (ak_t[:], 1.0)
                    nc.scalar.activation(dst, bank[2 + j % 2][:], ACT.Copy, scale=mul).then_inc(at_read, 1)

                def score_(u):
                    n, head, _ = A_UNIT(u)
                    lo = 0 if n else P
                    act.wait_ge(max_done, l * A_UNITS + u + 1)
                    act.wait_ge(pt_done, l * A_UNITS + u + 1)
                    for e in range(2):
                        ins = nc.scalar.activation(probs[:, u % 2, e, lo:], bank[2 + u % 2][:, e * 2 * P + lo:(e + 1) * 2 * P],
                                                   ACT.Exp, bias=a_negmax[:, n % 2, head + e:head + e + 1],
                                                   accum_out=a_den[:, n % 2, head + e:head + e + 1])
                    ins.then_inc(exp_done, 1)

                def sink(n):
                    act.wait_ge(sink_arg, l * NT + n + 1)
                    nc.scalar.activation(a_sink[:, n % 2, :], a_sink[:, n % 2, :], ACT.Exp).then_inc(sink_exp, 1)

                def prob(u):
                    n, _, _ = A_UNIT(u)
                    act.wait_ge(pt_done, l * A_UNITS + u + 3)
                    act.wait_ge(pv_done, l * A_UNITS + u + 1)
                    src, dst = bank[5][:].rearrange("p (a q) -> p a q", q=P), pt[:, u % 2]
                    if n == 0:
                        src, dst = src[:, 1::2], dst[:, 1::2]
                    nc.scalar.activation(dst, src, ACT.Copy).then_inc(pt_read, 1)

                def back(j):
                    act.wait_ge(back_done, l * 4 + j + 1)
                    act.wait_ge(panel_used, l * PANELS + P_OUT + 2)
                    nc.scalar.activation(h_hi[:, HH + j, :], bank[2 + j % 2][:], ACT.Copy).then_inc(amix_hi, 1)

                do = dict(warm=warm_up, split=split_, read=read, turn=turn, key=key, hout=hout, gates=gates, hmix=hmix,
                          asq=asq, aroot=aroot, flip=flip, score=score_, sink=sink, prob=prob, back=back)
                for what, n in MIX_STEPS:
                    if what in do:
                        do[what](n)

            with act.Fori(0, DEPTH) as l:
                ffn_phase(l, 0)
                norm(l, 1)
                mixers(l)
                with act.Fori(0, KD // 2 - 1) as i:
                    for q in range(2):
                        split_hi(l, P_OUT + 2 * i + q + 2, KD, q)
                        square_tile(l, 1, 2 * i + q, q)
                split_hi(l, P_OUT + KD, KD, 0)
                square_tile(l, 1, KD - 2, 0)
                warm_up(ACT.Sqrt)
                square_tile(l, 1, KD - 1, 1)
                split_hi(l, P_OUT + KD + 1, KD, 1)
                ffn_phase(l, 1)

            for d in range(0, KD, 2):
                act.wait_ge(out_pe, d + 1)
                nc.scalar.activation(x_rows[:, :, d * P:(d + 1) * P], bank[d][:].rearrange("p (n c) -> p n c", c=P),
                                     ACT.Copy).then_inc(out_act, 1)

        @block.tensor
        def _(pe):
            def product(dst, wslot, k, act_hi, act_lo, k0=0, first=True, last=True, ready=None, part=None):
                lo_k, hi_k = part or (0, k)
                for kt in range(lo_k, hi_k):
                    hi = w_hi[:, wslot, kt * P:(kt + 1) * P]
                    lo = w_lo[:, wslot, kt * P:(kt + 1) * P]
                    if ready is not None:
                        ready(kt)
                    nc.tensor.matmul(dst, hi, act_hi[:, k0 + kt, :], start=first and kt == 0, stop=False)
                    nc.tensor.matmul(dst, hi, act_lo[:, k0 + kt, :], start=False, stop=False)
                    mm = nc.tensor.matmul(dst, lo, act_hi[:, k0 + kt, :], start=False, stop=last and kt == k - 1)
                if hi_k == k:
                    mm.then_inc(panel_used, 1)
                return mm

            def keep_busy(n):
                for _ in range(n):
                    nc.tensor.matmul(bank[2][:], ident, x[:, 0, :], start=True, stop=True)

            def product_pair(dsts, at):
                def run(n, kt, passes):
                    hi = w_hi[:, n, kt * P:(kt + 1) * P]
                    lo = w_lo[:, n, kt * P:(kt + 1) * P]
                    for which in passes:
                        w, act_part = ((hi, h_hi), (lo, h_hi), (hi, h_lo))[which]
                        mm = nc.tensor.matmul(dsts[n], w, act_part[:, kt, :], start=kt == 0 and which == 0,
                                              stop=kt == KD - 1 and which == 2)
                    if kt == KD - 1 and passes[-1] == 2:
                        mm.then_inc(panel_used, 1)

                for k in range(KD + 1):
                    if k < KD:
                        pe.wait_ge(h_hi_done, at * KD + k + 1)
                        run(0, k, (0, 1))
                    if k:
                        run(1, k - 1, (0, 1, 2))
                    if k < KD:
                        pe.wait_ge(h_lo_done, at * KD + k + 3)
                        run(0, k, (2,))

            def product_hi_first(dst, slot, l, n):
                pe.wait_ge(hi_ready, l * PANELS + n + 1)
                for kt in range(KD):
                    hi = w_hi[:, slot, kt * P:(kt + 1) * P]
                    nc.tensor.matmul(dst, hi, h_hi[:, kt, :], start=kt == 0, stop=False)
                    nc.tensor.matmul(dst, hi, h_lo[:, kt, :], start=False, stop=False)
                pe.wait_ge(lo_ready, l * PANELS + n + 3)
                for kt in range(KD):
                    mm = nc.tensor.matmul(dst, w_lo[:, slot, kt * P:(kt + 1) * P], h_hi[:, kt, :], start=False,
                                          stop=kt == KD - 1)
                mm.then_inc(panel_used, 1)

            pe.wait_ge(setup_in, N_SETUP * 16)
            for l in range(DEPTH):
                nc.tensor.transpose(bank[l][:, 0:N_COLS], col_rows[0:N_COLS, l, :], ident[0:N_COLS, 0:N_COLS])\
                    .then_inc(setup_pe, 1)
            pe.wait_ge(x_in, 16)
            for d in range(KD):
                if d >= 2:
                    pe.wait_ge(sq_done, d - 1)
                for n in range(NT):
                    mm = nc.tensor.transpose(bank[4 + d % 2][:, n * P:(n + 1) * P], x_rows[:, n, d * P:(d + 1) * P], ident)
                mm.then_inc(setup_x, 1)
            for d in range(KD):
                pe.wait_ge(sq_done, d + 1)
                mm = nc.tensor.matmul(bank[6][:], ident, sq_first[:, d, :], start=d == 0, stop=d == KD - 1)
            mm.then_inc(setup_sum, 1)

            for v in (1, 0):
                if v == 0:
                    pe.wait_ge(first_step, KD + BUSY[3])
                    keep_busy(BUSY[4])
                pe.wait_ge(first_step, (2 - v) * KD)
                for m in range(KD):
                    mm = nc.tensor.matmul(bank[FIRST_BANK[v]][:, m:m + 1], ada_sum[:, v, m * P:(m + 1) * P], one,
                                          start=True, stop=True)
                mm.then_inc(ada_cols, 1)

            def ada_columns(l, u):
                pe.wait_ge(ada_step, A(l, u) * KD + KD + ADA_RING)
                for m in range(KD // 2):
                    mm = nc.tensor.matmul(bank[7][:, m:m + 1], ada_acc[:, m * P:(m + 1) * P], one, start=True, stop=True)
                mm.then_inc(ada_cols, 1)

            def norm(l, n):
                keep_busy(BUSY[0])
                pe.wait_ge(sum_done, X(l, n - 1, 0) + KD + 2)
                for c in range(NT):
                    mm = nc.tensor.matmul(bank[6][:, c:c + 1], ssum[:, c * P:(c + 1) * P], per_d, start=True, stop=True)
                mm.then_inc(ms_done, 1)
                keep_busy(BUSY[1])
                pe.wait_ge(inv_done, l * 3 + n + 1)
                for c in range(NT):
                    mm = nc.tensor.matmul(bank[6][:, c * P:(c + 1) * P], inv[:, c:c + 1].to_broadcast([P, P]), ident,
                                          start=True, stop=True)
                mm.then_inc(rstd_done, 1)
                keep_busy(BUSY[2])

            def gate_up(l, ffn, i, ada=None, first=False):
                base = (P_GU1, P_GU2)[ffn]
                for q in range(4):
                    f = 2 * i + q // 2
                    if not first or q != 2:
                        pe.wait_ge(lo_ready, l * PANELS + base + 4 * i + q + 3)
                    pe.wait_ge(hid_done if q % 2 else silu_done, l * (2 * FT) + ffn * FT + f + 1)
                    if first and q == 2:
                        product_hi_first(bank[q][:], 0, l, base + 2)
                    elif not first or q == 3:
                        product(bank[q][:], q % 2, KD, h_hi, h_lo)
                    elif q == 1:
                        product_pair([bank[0][:], bank[1][:]], l * 3 + 2 * ffn)
                if ada is not None:
                    ada_columns(l, ada)

            def down(l, ffn, i, first):
                base = (P_DN1, P_DN2)[ffn]
                for q in range(4):
                    d = 2 * i + q // 2
                    pe.wait_ge(lo_ready, l * PANELS + base + 4 * i + q + 3)
                    if q % 2 == 0:
                        pe.wait_ge(x_done, X(l, 2 * ffn, d) + 1)
                    ready = None
                    if first and q < 2:
                        def ready(kt, q=q):
                            pe.wait_ge(hid_lo_done, l * (2 * FT) + ffn * FT + q * HALF + kt + 1)
                    product(bank[4 + q // 2][:], q % 2, HALF, hid_hi, hid_lo, k0=(q % 2) * HALF, first=q % 2 == 0,
                            last=q % 2 == 1, ready=ready)
                if ffn == 0:
                    ada_columns(l, (1, i))

            def ffn_phase(l, ffn):
                norm(l, 2 * ffn)
                phase = 2 * ffn
                n_ada = ADA_ITERATIONS[phase]
                gate_up(l, ffn, 0, (phase, 0), first=True)
                with pe.Fori(1, n_ada) as i:
                    gate_up(l, ffn, i, (phase, i))
                with pe.Fori(n_ada, FT // 2) as i:
                    gate_up(l, ffn, i)
                down(l, ffn, 0, True)
                with pe.Fori(1, KD // 2) as i:
                    down(l, ffn, i, False)

            def out_product(l, i, q, ready=None, part=None):
                pe.wait_ge(lo_ready, l * PANELS + P_OUT + 2 * i + q + 3)
                pe.wait_ge(x_done, X(l, 1, 2 * i + q) + 1)
                product(bank[4 + q][:], q, KD, h_hi, h_lo, ready=ready, part=part)

            def mixers(l):
                def prod(at):
                    i, k0, k1 = at
                    if i == 0:
                        return
                    if i == 1:
                        pe.wait_ge(lo_ready, l * PANELS + P_IN + 4)
                        pe.wait_ge(in_read, l * IN_TILES + 2)
                        product_pair([bank[0][:], bank[1][:]], l * 3 + 1)
                        return
                    if i == 2:
                        product_hi_first(bank[T_BANK(i)][:], 0, l, P_IN + i)
                        return
                    if k0 == 0:
                        pe.wait_ge(lo_ready, l * PANELS + P_IN + i + 3)
                        pe.wait_ge(in_read, l * IN_TILES + (i - 1 if i < 8 else i + 1))
                    mm = product(bank[T_BANK(i)][:], i % 2, KD, h_hi, h_lo, part=(k0, k1))
                    if i == IN_TILES - 1 and k1 <= HH:
                        mm.then_inc(h_free, 1)

                def turn(i):
                    e = TURN_OF[i]
                    pe.wait_ge(in_read, l * IN_TILES + i + 3)
                    pe.wait_ge(turn_read, l * TURNS + e + 1)
                    for n in range(NT):
                        mm = nc.tensor.transpose(bank[5][:, n * P:(n + 1) * P], evac[:, e % 2, n * P:(n + 1) * P], ident)
                    mm.then_inc(turn_done, 1)

                def units(first, half, left, right):
                    for h in (2 * half, 2 * half + 1):
                        u = first + h
                        pe.wait_ge(att_read, l * UNITS + u + 1)
                        for c in range(NT):
                            cut = slice(c * P, (c + 1) * P)
                            mm = nc.tensor.matmul(bank[6 + u % 2][:, cut], left(h)[:, cut], right(h)[:, cut],
                                                  start=True, stop=True)
                        mm.then_inc(att_done, 1)

                def diag(half):
                    pe.wait_ge(gates_ready, l + 1)
                    pe.wait_ge(in_read, l * IN_TILES + 8 + 2)
                    units(0, half, lambda h: k_t[:, h, :], lambda h: q_t[:, h, :])

                def level(at):
                    v, half = at
                    pe.wait_ge(kq_ready, l * (LEVELS + 2) + v + 1)
                    units(HH * (v + 1), half, lambda h: kq[:, v % 2, h, :], lambda h: kq[:, v % 2, h, :])

                def key(h):
                    pe.wait_ge(kq_ready, l * (LEVELS + 2) + LEVELS + 1)
                    if h < 2:
                        pe.wait_ge(att_read, (l + 1) * UNITS + 2)
                    else:
                        pe.wait_ge(key_read, l * HH + h - 1)
                    for c in range(NT - 1):
                        mm = nc.tensor.transpose(bank[6 + h % 2][:, c * P:(c + 1) * P], kq[:, 1, h, c * P:(c + 1) * P], ident)
                    mm.then_inc(key_done, 1)

                def update(h):
                    pe.wait_ge(turn_read, l * TURNS + TURN_OF[IN_ORDER.index(8 + h)] + 2)
                    pe.wait_ge(key_read, l * HH + max(h, 2 + h % 2) + 1)
                    if h >= 2:
                        pe.wait_ge(state_done, l * HH + h - 1)
                    for c in range(NT - 1):
                        mm = nc.tensor.matmul(bank[6 + h % 2][:, c * P:(c + 1) * P], key_n[:, h, c, :],
                                              v_n[:, h, c, :], start=True, stop=True)
                    mm.then_inc(upd_done, 1)

                def hout(h):
                    pe.wait_ge(kq_ready, (l + 1) * (LEVELS + 2))
                    pe.wait_ge(state_done, l * HH + max(h, 2 + h % 2) + 1)
                    if h >= 2:
                        pe.wait_ge(osq_done, l * HH + h - 1)
                    for c in range(NT):
                        cut = slice(c * P, (c + 1) * P)
                        mm = nc.tensor.matmul(bank[6 + h % 2][:, cut], v_n[:, h, c, :], att[:, h, cut], start=True, stop=c == 0)
                        if c:
                            mm = nc.tensor.matmul(bank[6 + h % 2][:, cut], state[:, h, c - 1, :], kq[:, 0, h, cut],
                                                  start=False, stop=True)
                    mm.then_inc(o_done, 1)

                def hms(_):
                    pe.wait_ge(osq_done, (l + 1) * HH)
                    pe.wait_ge(in_read, (l + 1) * IN_TILES - 1 + 2)
                    for h in range(HH):
                        for c in range(NT):
                            mm = nc.tensor.matmul(bank[0][:, h * NT + c:h * NT + c + 1], o_sq[:, h, c * P:(c + 1) * P], per_h,
                                                  start=True, stop=True)
                    mm.then_inc(oms_done, 1)

                def hnorm(h):
                    pe.wait_ge(oinv_done, l + 1)
                    if h >= 2:
                        pe.wait_ge(omix_done, l * HH + h - 1)
                    for c in range(NT):
                        mm = nc.tensor.matmul(bank[R_BANK[h % 2]][:, c * P:(c + 1) * P],
                                              o_inv[:, h * NT + c:h * NT + c + 1].to_broadcast([P, P]), ident,
                                              start=True, stop=True)
                    mm.then_inc(orstd_done, 1)

                def flip(j):
                    pe.wait_ge(rot_done, l + 2)
                    if j >= 2:
                        pe.wait_ge(at_read, l * 5 + j - 1)
                    for n in range(NT):
                        mm = nc.tensor.transpose(bank[2 + j % 2][:, n * P:(n + 1) * P],
                                                 aqk[:, n, 2 * j:2 * j + 2, :].rearrange("p a d -> p (a d)"), ident)
                    mm.then_inc(at_done, 1)

                def score_(u):
                    n, head, g = A_UNIT(u)
                    lo = 0 if n else P
                    if u == 0:
                        pe.wait_ge(at_read, l * 5 + 5)
                    pe.wait_ge(exp_done, l * A_UNITS + u + 1)
                    dst = bank[2 + u % 2][:].rearrange("p (e k) -> p e k", e=2)
                    for e in range(2):
                        nc.tensor.matmul(dst[:, e, lo:], aq_t[AD * g:AD * (g + 1), (head + e) % 4, n * P:(n + 1) * P],
                                         ak_t[AD * g:AD * (g + 1), (n - 1) * P + lo:(n + 1) * P],
                                         start=True, stop=False, skip_group_check=True)
                        mm = nc.tensor.matmul(dst[:, e, lo:], ident_r[:], amask_r[:, lo:], start=False, stop=True,
                                              skip_group_check=True)
                    mm.then_inc(score_done, 1)

                def prob(u):
                    n, _, _ = A_UNIT(u)
                    pe.wait_ge(exp_done, l * A_UNITS + u + 3)
                    pe.wait_ge(pt_read, l * A_UNITS + u + 1)
                    if u == 0:
                        pe.wait_ge(turn_read, (l + 1) * TURNS + 1)
                    for e in range(2):
                        for b in range(0 if n else 1, 2):
                            mm = nc.tensor.transpose(bank[5][:, (2 * e + b) * P:(2 * e + b + 1) * P],
                                                     probs[:, u % 2, e, b * P:(b + 1) * P], ident)
                    mm.then_inc(pt_done, 1)

                def weigh(u):
                    n, head, g = A_UNIT(u)
                    pe.wait_ge(pt_read, l * A_UNITS + u + 2)
                    if u == 4:
                        pe.wait_ge(osq_done, l * HH + 3)
                    elif u > 4 and u % 4 == 0:
                        pe.wait_ge(anorm_done, l * NT + n)
                    for e in range(2):
                        for b in range(0 if n else 1, 2):
                            mm = nc.tensor.matmul(bank[O_BANK[n % 2]][:, (head + e) * AD:(head + e + 1) * AD],
                                                  pt[:, u % 2, 2 * e + b, :], a_v[:, n - 1 + b, g, :],
                                                  start=b == 0 or n == 0, stop=b == 1, skip_group_check=True)
                    mm.then_inc(pv_done, 1)

                def back(j):
                    pe.wait_ge(anorm_done, (l + 1) * NT + 1)
                    if j >= 2:
                        pe.wait_ge(amix_lo, l * 4 + j - 1)
                    else:
                        pe.wait_ge(exp_done, (l + 1) * A_UNITS + 2)
                    for n in range(NT):
                        mm = nc.tensor.transpose(bank[2 + j % 2][:, n * P:(n + 1) * P], a_out[:, n, j * P:(j + 1) * P], ident)
                    mm.then_inc(back_done, 1)

                def out(part):
                    if part == 0:
                        pe.wait_ge(anorm_done, l * NT + 4)
                    out_product(l, 0, 0, lambda kt: pe.wait_ge(mix_lo, l * HH + kt + 1) if kt < HH
                                else pe.wait_ge(amix_lo, l * 4 + kt - HH + 1), (part * KD // 2, (part + 1) * KD // 2))

                do = dict(out=out, prod=prod, turn=turn, diag=diag, level=level, key=key, update=update, hout=hout, hms=hms,
                          hnorm=hnorm, flip=flip, score=score_, prob=prob, weigh=weigh, back=back)
                for what, n in MIX_STEPS:
                    if what in do:
                        do[what](n)

            with pe.Fori(0, DEPTH) as l:
                ffn_phase(l, 0)
                norm(l, 1)
                mixers(l)
                out_product(l, 0, 1)
                with pe.Fori(1, KD // 2) as i:
                    for q in range(2):
                        out_product(l, i, q)
                ffn_phase(l, 1)

            for d in range(KD):
                pe.wait_ge(x_done, X(DEPTH - 1, 2, d if d < 4 else KD - 1) + 3)
                for n in range(NT):
                    mm = nc.tensor.transpose(bank[d][:, n * P:(n + 1) * P], x[:, d, n * P:(n + 1) * P], ident)
                mm.then_inc(out_pe, 1)

        @block.vector
        def _(dve):
            tt, ts, stt = nc.vector.tensor_tensor, nc.vector.tensor_scalar, nc.vector.scalar_tensor_tensor
            for signal, start in STARTS:
                dve.sem_inc(signal, start)

            def add_squares(l, stage, d, slot):
                at = X(l, stage, d)
                dve.wait_ge(sq_done, at + 1)
                dve.wait_ge(sum_done, at + 2)
                tt(ssum[:], ssum[:], sq[:, slot, :], ALU.add).then_inc(sum_done, 1)

            def split_lo(l, n, k, slot):
                dve.wait_ge(hi_ready, l * PANELS + n + 1)
                tt(w_lo[:, slot % 2, 0:k * P], raw[:, slot % 2, 0:k * P], w_hi[:, slot % 2, 0:k * P], ALU.subtract)\
                    .then_inc(lo_ready, 1)

            def scale_column(l, n, ready=None):
                dve.wait_ge(mod_ready, ready or M(l, 3 * n + 1))
                stt(scale_col[:], mod[:, (3 * n + 1) * KD:(3 * n + 2) * KD], 1.0,
                    cols[:, bass.ds(l, 1), C_NORM + n * KD:C_NORM + (n + 1) * KD].rearrange("p a k -> p (a k)"),
                    ALU.add, ALU.mult).then_inc(cols_done, 1)
                dve.wait_ge(cols_done, N_COLS_DONE(l, n))
                dve.sem_inc(passed, 1)

            def scale_x(l, stage, d):
                dve.wait_ge(x_done, X(l, stage, d) + 3)
                y = y_r if stage == 1 else y_h
                ts(y[:, bass.ds(d, 1), :].rearrange("p a t -> p (a t)"), x[:, bass.ds(d, 1), :].rearrange("p a t -> p (a t)"),
                   scale_col[:, bass.ds(d, 1)], None, ALU.mult).then_inc(y_done, 1)

            done = [0]

            def link(ins):
                done[0] += 1
                ins.then_inc(setup_step, 1)
                dve.wait_ge(setup_step, done[0])

            dve.wait_ge(setup_in, N_SETUP * 16)
            for l in range(DEPTH):
                dve.wait_ge(setup_pe, l + 1)
                nc.vector.tensor_copy(cols[:, l, :], bank[l][:, 0:N_COLS]).then_inc(setup_cols, 1)
            dve.wait_ge(setup_act, 1)
            def first_products(v, k):
                dve.wait_ge(first_in[v][k], 16)
                rows, acc = ada_first[:, v, k, :], ada_sum[:, v, :]
                if k == 0:
                    ins = ts(acc, rows, cact[:, k:k + 1], None, ALU.mult)
                else:
                    dve.wait_ge(first_step, (1 - v) * KD + k)
                    ins = stt(acc, rows, cact[:, k:k + 1], acc, ALU.mult, ALU.add)
                ins.then_inc(first_step, 1)

            def first_store(v):
                dve.wait_ge(ada_cols, 2 - v)
                tt(mod[:, v * KD:(v + 1) * KD], bank[FIRST_BANK[v]][:, 0:KD], cols[:, 0, v * KD:(v + 1) * KD], ALU.add)\
                    .then_inc(mod_ready, 1)

            for k in range(KD):
                first_products(1, k)
            dve.wait_ge(setup_cols, DEPTH)
            logit = lambda l: cols[:, l, C_LB:C_LB + HH]
            top, total, run = lb_tmp[:, 0], lb_tmp[:, 1], lb_tmp[:, 2]
            prob_l = lambda l: lb_tmp[:, 4 + l]
            link(nc.vector.tensor_copy(top, logit(0)))
            for l in range(1, DEPTH):
                link(tt(top, top, logit(l), ALU.max))
            for l in range(DEPTH):
                link(tt(prob_l(l), logit(l), top, ALU.subtract))
            dve.sem_inc(angles, 1)
            ang, turns_, part = rope_tmp[:, 0], rope_tmp[:, 1], rope_tmp[:, 2]
            link(nc.vector.tensor_copy(pos_f[:], pos_i[:]))
            link(tt(ang, pos_f[:].unsqueeze(2).to_broadcast([P, NT, ROPE_HALF]),
                    const[:, K_INVF:K_INVF + ROPE_HALF].unsqueeze(1).to_broadcast([P, NT, ROPE_HALF]), ALU.mult))
            link(ts(turns_, ang, 1.0 / TWO_PI, MAGIC, ALU.mult, ALU.add))
            link(ts(turns_, turns_, MAGIC, None, ALU.subtract))
            for c in TWO_PI_PARTS:
                link(stt(ang, turns_, -c, ang, ALU.mult, ALU.add))
            ts(ang, ang, PI_BELOW, -PI_BELOW, ALU.min, ALU.max).then_inc(angles, 1)
            for k in range(2):
                first_products(0, k)
            first_store(1)
            scale_column(0, 0, ready=1)
            for k in range(2, KD):
                first_products(0, k)
                scale_x(0, -1, k - 2)
            scale_x(0, -1, KD - 2)
            scale_x(0, -1, KD - 1)
            dve.wait_ge(setup_act, 3)
            for l in range(DEPTH):
                link(nc.vector.tensor_copy(total, prob_l(0)) if l == 0 else tt(total, total, prob_l(l), ALU.add))
            link(nc.vector.reciprocal(total, total))
            for l in range(DEPTH):
                link(tt(prob_l(l), prob_l(l), total, ALU.mult))
                link(nc.vector.tensor_copy(run, prob_l(0)) if l == 0 else tt(run, run, prob_l(l), ALU.add))
                link(tt(lower[:, l, :], run, prob_l(0), ALU.subtract))
                link(ts(one_minus_lower[:, l, :], lower[:, l, :], -1.0, 1.0, ALU.mult, ALU.add))
            dve.wait_ge(setup_act, 5)
            link(tt(part, cos_t[:], cos_t[:], ALU.mult))
            link(ts(cos_t[:], part, -2.0, 1.0, ALU.mult, ALU.add))

            nc.vector.tensor_scalar(minus_sinks[:], sinks[:], -1.0, None, ALU.mult)
            for n in range(2):
                split_lo(0, n, KD, n)
            dve.wait_ge(lmask_in, 16)
            first_store(0)

            def ada_piece(l, u, k):
                dve.wait_ge(ada_in[k % ADA_RING], A(l, u) * (KD // ADA_RING * 16) + (k // ADA_RING + 1) * 16)
                if k == 0:
                    ins = ts(ada_acc[:], ada_raw[:, k % ADA_RING, :], cact[:, k:k + 1], None, ALU.mult)
                else:
                    dve.wait_ge(ada_step, A(l, u) * KD + k + ADA_RING)
                    ins = stt(ada_acc[:], ada_raw[:, k % ADA_RING, :], cact[:, k:k + 1], ada_acc[:], ALU.mult, ALU.add)
                ins.then_inc(ada_step, 1)

            def ada_store(l, u):
                dve.wait_ge(ada_cols, A(l, u) + 3)
                tt(mod[:, bass.ds(A_COL(u), KD // 2)], bank[7][:, 0:KD // 2],
                   cols[:, bass.ds(A_LAYER(l, u), 1), bass.ds(A_COL(u), KD // 2)].rearrange("p a k -> p (a k)"), ALU.add)\
                    .then_inc(mod_ready, 1)

            def norm(l, n):
                dve.wait_ge(root_done, l * 3 + n + 1)
                nc.vector.reciprocal(inv[:], root[:]).then_inc(inv_done, 1)
                dve.wait_ge(rstd_done, l * 3 + n + 1)
                dve.wait_ge(y_done, l * (3 * KD) + (n + 1) * KD)
                y = y_r if n == 2 else y_h

                def low(k):
                    vec = 3 * n * KD + k
                    dve.wait_ge(h_hi_done, l * (3 * KD) + n * KD + k + 1)
                    stt(h_lo[:, k, :], xn[:, k % 4, :], mod[:, vec:vec + 1], h_hi[:, k, :], ALU.add, ALU.subtract)\
                        .then_inc(h_lo_done, 1)

                for k in range(KD):
                    if k >= 2:
                        low(k - 2)
                    if k >= 4:
                        dve.wait_ge(h_lo_done, l * (3 * KD) + n * KD + k - 1)
                    tt(xn[:, k % 4, :], bank[6][:], y[:, k, :], ALU.mult).then_inc(xn_done, 1)
                low(KD - 2)
                low(KD - 1)

            def stage_columns(l, stage):
                nc.vector.memset(ssum[:], 0.0).then_inc(sum_zero, 1)
                dve.wait_ge(mod_ready, M(l, 3 * stage + 2))
                ts(gate_col[:], mod[:, (3 * stage + 2) * KD:(3 * stage + 3) * KD], 1.0 if stage == 1 else 0.5, None, ALU.mult)\
                    .then_inc(gate_col_done, 1)
                dve.wait_ge(gate_col_done, l * 3 + stage + 1)
                dve.sem_inc(passed, 1)
                if stage < 2:
                    scale_column(l, stage + 1)
                else:
                    stt(scale_col[:], mod[:, KD:2 * KD], 1.0, cols[:, DEPTH - 1, C_NORM:C_NORM + KD], ALU.add, ALU.mult)\
                        .then_inc(cols_done, 1)
                    dve.wait_ge(cols_done, N_COLS_DONE(l, 3))
                    dve.sem_inc(passed, 1)

            def update_x(l, stage, d, slot, panels):
                dve.wait_ge(panel_used, panels + 2)
                xd = x[:, bass.ds(d, 1), :].rearrange("p a t -> p (a t)")
                stt(xd, bank[4 + slot][:], gate_col[:, bass.ds(d, 1)], xd, ALU.mult, ALU.add).then_inc(x_done, 1)

            def hidden(l, ffn, f, slot):
                dve.wait_ge(panel_used, l * PANELS + (P_GU1, P_GU2)[ffn] + 2 * f + 4)
                dve.wait_ge(silu_done, l * (2 * FT) + ffn * FT + f + 3)
                tt(hidf[:, slot, :], bank[2 * slot + 1][:], sil[:, slot, :], ALU.mult).then_inc(hid_done, 1)

            def hidden_lo(l, ffn, f, slot):
                dve.wait_ge(hid_hi_done, l * (2 * FT) + ffn * FT + f + 1)
                at = (slice(None), bass.ds(f, 1), slice(None))
                tt(hid_lo[at].rearrange("p a t -> p (a t)"), hidf[:, slot, :], hid_hi[at].rearrange("p a t -> p (a t)"),
                   ALU.subtract).then_inc(hid_lo_done, 1)

            def gate_up(l, ffn, i, last=False, ada=None):
                base = (P_GU1, P_GU2)[ffn]
                for q in range(4):
                    f, slot = 2 * i + q // 2, q // 2
                    if q % 2:
                        hidden(l, ffn, f, slot)
                    split_lo(l, base + 4 * i + q + 2, HALF if last and q >= 2 else KD, q)
                    if q % 2:
                        hidden_lo(l, ffn, f, slot)
                    if ada is not None:
                        for s in range(*ADA_SHARE[q]):
                            ada_piece(l, ada, s)
                if ada is not None:
                    ada_store(l, ada)

            def down(l, ffn, i, after):
                base = (P_DN1, P_DN2)[ffn]
                for q in range(4):
                    d = 2 * i + q // 2
                    hurry = q == 3 and after != HALF
                    if q % 2:
                        update_x(l, 2 * ffn, d, q // 2, l * PANELS + base + 4 * i + q + 1)
                    if hurry:
                        scale_x(l, 2 * ffn, d)
                        add_squares(l, 2 * ffn, d, q // 2)
                    split_lo(l, base + 4 * i + q + 2, HALF if q < 2 else after, q)
                    if q % 2 and not hurry:
                        scale_x(l, 2 * ffn, d)
                        add_squares(l, 2 * ffn, d, q // 2)
                    if ffn == 0:
                        for s in range(*ADA_SHARE[q]):
                            ada_piece(l, (1, i), s)
                if ffn == 0:
                    ada_store(l, (1, i))

            def ffn_phase(l, ffn):
                norm(l, 2 * ffn)
                phase = 2 * ffn
                n_ada = ADA_ITERATIONS[phase]
                with dve.Fori(0, n_ada) as i:
                    gate_up(l, ffn, i, ada=(phase, i))
                if n_ada < FT // 2 - 1:
                    with dve.Fori(n_ada, FT // 2 - 1) as i:
                        gate_up(l, ffn, i)
                gate_up(l, ffn, FT // 2 - 1, last=True)
                stage_columns(l, 2 * ffn)
                with dve.Fori(0, KD // 2 - 1) as i:
                    down(l, ffn, i, HALF)
                down(l, ffn, KD // 2 - 1, KD)

            def mixers(l):
                count = [0]

                def own(ins):
                    count[0] += 1
                    ins.then_inc(step, 1)
                    dve.wait_ge(step, l * STEPS + count[0])

                def chunks(ap):
                    return ap.rearrange("p (c t) -> p c t", t=P)

                def split_(i):
                    split_lo(l, P_IN + i + 2, KD, i)

                def read(i):
                    kind, c = KINDS[IN_ORDER[i]], IN_ORDER[i] % 4
                    if kind == K_F:
                        dve.wait_ge(in_read, l * IN_TILES + i + 3)
                        ts(f_t[:, c, :], f_t[:, c, :], one_minus_lower[:, bass.ds(l, 1), c], lower[:, bass.ds(l, 1), c],
                           ALU.mult, ALU.add)
                        ins = ts(k_t[:, c, :], k_t[:, c, :], one_minus_lower[:, bass.ds(l, 1), c], None, ALU.mult)
                        if c == HH - 1:
                            ins.then_inc(gates_ready, 1)

                def ones(_):
                    own(nc.vector.memset(suf[:], 1.0))

                def diag(half):
                    for h in (2 * half, 2 * half + 1):
                        dve.wait_ge(att_done, l * UNITS + h + 1)
                        tt(chunks(att[:, h, :]), chunks(bank[6 + h % 2][:]), ident.unsqueeze(1).to_broadcast([P, NT, P]),
                           ALU.mult).then_inc(att_read, 1)

                def halves(ap, v):
                    return ap.rearrange("p h (b w s) -> p (h b) w s", w=2, s=1 << v)

                def operands(v):
                    return (halves(z, v) for z in (kq[:, v % 2], q_t[:], k_t[:], f_t[:], suf[:]))

                def build(v):
                    kq_v, q_v, k_v, p_v, s_v = operands(v)
                    if v == 0:
                        dve.wait_ge(gates_ready, l + 1)
                        dve.wait_ge(in_read, l * IN_TILES + 8 + 2)
                    tt(kq_v[:, :, 0], k_v[:, :, 0], s_v[:, :, 0], ALU.mult)
                    tt(kq_v[:, :, 1], q_v[:, :, 1], p_v[:, :, 1], ALU.mult).then_inc(kq_ready, 1)

                def extend(v):
                    _, _, _, p_v, s_v = operands(v)
                    b = 1 << v
                    shape = [P, HH * T // (2 * b), b]
                    own(tt(s_v[:, :, 0], s_v[:, :, 0], p_v[:, :, 1, b - 1:b].to_broadcast(shape), ALU.mult))
                    own(tt(p_v[:, :, 1], p_v[:, :, 1], p_v[:, :, 0, b - 1:b].to_broadcast(shape), ALU.mult))

                def level(at):
                    v, half = at
                    for h in (2 * half, 2 * half + 1):
                        u = HH * (v + 1) + h
                        dve.wait_ge(att_done, l * UNITS + u + 1)
                        dve.wait_ge(att_read, l * UNITS + u - HH + 3)
                        dve.sem_inc(passed, 1)
                        nc.vector.copy_predicated(chunks(att[:, h, :]), lmask[:, v].unsqueeze(1).to_broadcast([P, NT, P]),
                                                  chunks(bank[6 + u % 2][:])).then_inc(att_read, 1)

                def key_side(_):
                    tt(kq[:, 1], k_t[:], suf[:], ALU.mult).then_inc(kq_ready, 1)

                def query_side(_):
                    tt(kq[:, 0], q_t[:], f_t[:], ALU.mult).then_inc(kq_ready, 1)

                def update(h):
                    dve.wait_ge(kq_ready, (l + 1) * (LEVELS + 2))
                    dve.wait_ge(upd_done, l * HH + h + 1)
                    own(nc.vector.tensor_copy(state[:, h, 0, :], bank[6 + h % 2][:, 0:P]))
                    own(stt(state[:, h, 1, :], state[:, h, 0, :], f_t[:, h, 2 * P - 1:2 * P],
                            bank[6 + h % 2][:, P:2 * P], ALU.mult, ALU.add))
                    stt(state[:, h, 2, :], state[:, h, 1, :], f_t[:, h, 3 * P - 1:3 * P],
                        bank[6 + h % 2][:, 2 * P:3 * P], ALU.mult, ALU.add).then_inc(state_done, 1)

                def gates(_):
                    dve.wait_ge(oroot_done, l + 1)
                    nc.vector.reciprocal(o_inv[:], o_root[:]).then_inc(oinv_done, 1)

                def hmix(h):
                    dve.wait_ge(mix_hi, l * HH + h + 1)
                    tt(h_lo[:, h, :], o_mix[:, h, :], h_hi[:, h, :], ALU.subtract).then_inc(mix_lo, 1)

                def hnorm(h):
                    dve.wait_ge(orstd_done, l * HH + h + 1)
                    if h < HH - 1:
                        dve.wait_ge(gates_done, l + 1)
                    else:
                        dve.wait_ge(in_read, (l + 1) * IN_TILES + 2)
                    own(tt(o_n[:, h, :], bank[R_BANK[h % 2]][:], o_n[:, h, :], ALU.mult))
                    stt(o_mix[:, h, :], o_n[:, h, :], cols[:, bass.ds(l, 1), C_HNORM],
                        g_t[:, h, :], ALU.mult, ALU.mult).then_inc(omix_done, 1)

                def normalise(_):
                    dve.wait_ge(aroot_done, l + 1)
                    own(nc.vector.reciprocal(a_ss[:], a_ss[:]))
                    flat = aqk[:].rearrange("p n h d -> p (n h) d")
                    own(tt(flat, flat, a_ss[:].rearrange("p n h -> p (n h)").unsqueeze(2).to_broadcast([P, NT * QK, AD]),
                           ALU.mult))

                def weights(_):
                    dve.wait_ge(row_in, (l + 1) * 32)
                    flat = aqk[:].rearrange("p n h d -> p n (h d)")
                    own(tt(flat, flat, qkw[:].rearrange("p h d -> p (h d)").unsqueeze(1).to_broadcast([P, NT, QK * AD]),
                           ALU.mult))

                def rotate(_):
                    one_, two = aqk[:, :, :, 0:ROPE_HALF], aqk[:, :, :, ROPE_HALF:2 * ROPE_HALF]
                    shape = [P, NT, QK, ROPE_HALF]
                    cos_b, sin_b = (z[:].unsqueeze(2).to_broadcast(shape) for z in (cos_t, sin_t))
                    r = [a_rot[:, j].rearrange("p (n h d) -> p n h d", n=NT, h=QK) for j in range(4)]
                    tt(r[0], one_, cos_b, ALU.mult)
                    tt(r[1], two, sin_b, ALU.mult)
                    tt(r[2], two, cos_b, ALU.mult)
                    own(tt(r[3], one_, sin_b, ALU.mult))
                    tt(one_, r[0], r[1], ALU.subtract)
                    tt(two, r[2], r[3], ALU.add).then_inc(rot_done, 1)

                def score_(u):
                    n, head, _ = A_UNIT(u)
                    lo = 0 if n else P
                    dve.wait_ge(score_done, l * A_UNITS + u + 1)
                    own(nc.vector.tensor_reduce(a_max[:, u % 2, :], bank[2 + u % 2][:].rearrange("p (e k) -> p e k", e=2)[:, :, lo:],
                                                AX_X, ALU.max))
                    stt(a_negmax[:, n % 2, head:head + 2], a_max[:, u % 2, :], -1.0,
                        minus_sinks[:, bass.ds(l, 1), head:head + 2].rearrange("p a h -> p (a h)"), ALU.mult, ALU.min)\
                        .then_inc(max_done, 1)

                def sink(n):
                    dve.wait_ge(max_done, l * A_UNITS + 4 * n + 4)
                    tt(a_sink[:, n % 2, :], sinks[:, bass.ds(l, 1), :].rearrange("p a h -> p (a h)"), a_negmax[:, n % 2, :],
                       ALU.add).then_inc(sink_arg, 1)

                def anorm(n):
                    dve.wait_ge(sink_exp, l * NT + n + 1)
                    dve.wait_ge(exp_done, l * A_UNITS + 4 * n + 6)
                    own(tt(a_den[:, n % 2, :], a_den[:, n % 2, :], a_sink[:, n % 2, :], ALU.add))
                    own(nc.vector.reciprocal(a_den[:, n % 2, :], a_den[:, n % 2, :]))
                    dve.wait_ge(pv_done, l * A_UNITS + 4 * n + 6)
                    tt(a_out[:, n, :].rearrange("p (h d) -> p h d", d=AD), bank[O_BANK[n % 2]][:].rearrange("p (h d) -> p h d", d=AD),
                       a_den[:, n % 2, :].unsqueeze(2).to_broadcast([P, AH, AD]), ALU.mult).then_inc(anorm_done, 1)

                def back(j):
                    dve.wait_ge(amix_hi, l * 4 + j + 1)
                    tt(h_lo[:, HH + j, :], bank[2 + j % 2][:], h_hi[:, HH + j, :], ALU.subtract).then_inc(amix_lo, 1)

                do = dict(split=split_, read=read, ones=ones, diag=diag, build=build, extend=extend, level=level,
                          key_side=key_side, query_side=query_side, update=update, gates=gates,
                          hnorm=hnorm, hmix=hmix, normalise=normalise, weights=weights, rotate=rotate, score=score_,
                          sink=sink, anorm=anorm, back=back)
                for what, n in MIX_STEPS:
                    if what in do:
                        do[what](n)
                assert count[0] == STEPS, count[0]

            with dve.Fori(0, DEPTH) as l:
                ffn_phase(l, 0)
                norm(l, 1)
                mixers(l)
                stage_columns(l, 1)
                with dve.Fori(0, KD // 2 - 1) as i:
                    for q in range(2):
                        update_x(l, 1, 2 * i + q, q, l * PANELS + P_OUT + 2 * i + q + 1)
                        split_lo(l, P_OUT + 2 * i + q + 2, KD, q)
                        scale_x(l, 1, 2 * i + q)
                        add_squares(l, 1, 2 * i + q, q)
                update_x(l, 1, KD - 2, 0, l * PANELS + P_OUT + KD - 1)
                split_lo(l, P_OUT + KD, KD, 0)
                scale_x(l, 1, KD - 2)
                add_squares(l, 1, KD - 2, 0)
                update_x(l, 1, KD - 1, 1, l * PANELS + P_OUT + KD)
                scale_x(l, 1, KD - 1)
                add_squares(l, 1, KD - 1, 1)
                split_lo(l, P_OUT + KD + 1, KD, 1)
                ffn_phase(l, 1)

            for d in range(1, KD, 2):
                dve.wait_ge(out_pe, d + 1)
                nc.vector.tensor_copy(x_rows[:, :, d * P:(d + 1) * P], bank[d][:].rearrange("p (n c) -> p n c", c=P))\
                    .then_inc(out_dve, 1)


INPUTS = ["x", "c", "positions", "ada_w", "ada_b", "norm_ffn1", "ffn1_w_gate", "ffn1_w_up", "ffn1_w_down", "norm_mix",
          "w_in", "lb_logits", "hgrn_norm", "q_norm", "k_norm", "sinks", "w_out", "norm_ffn2", "ffn2_w_gate",
          "ffn2_w_up", "ffn2_w_down"]


def kernel(**inputs):
    import concourse.bacc as bacc
    from concourse.bass_utils import run_bass_kernel_spmd

    nc = bacc.Bacc("TRN2", target_bir_lowering=False, num_devices=1)
    arrays = {name: np.ascontiguousarray(inputs[name]) for name in INPUTS}
    arrays["const"], arrays["amask"], arrays["lmask"] = constants()
    aps = {name: nc.dram_tensor(name, v.shape, mybir.dt.from_np(v.dtype), kind="ExternalInput").ap()
           for name, v in arrays.items()}
    out = nc.dram_tensor("out", (1, T, D), F32, kind="ExternalOutput").ap()
    trunk_kernel(nc, aps, out)
    return run_bass_kernel_spmd(nc, [arrays], core_ids=[0]).results[0]["out"]
```
